# Optimizing a Trainium2 kernel written in Bass

```python
import math
import jax
import jax.numpy as jnp
from jax import lax
import numpy as np
import jax, jax.numpy as jnp

D_MODEL = 1024
BATCH = 1
SEQ = 512
DEPTH = 1

NORM_EPS = 1e-6
POOL_WINDOWS = (2, 4, 8, 16)
POOL_GROUPS = 4
POOL_WIDTH = D_MODEL // 2
POOL_GROUP_DIM = POOL_WIDTH // POOL_GROUPS
ATTN_HEADS = 8
ATTN_HEAD_DIM = 64
ATTN_WIDTH = ATTN_HEADS * ATTN_HEAD_DIM
Q_BLOCK = 128
SSD_HEAD_DIM = 64
SSD_WIDTH = D_MODEL
SSD_HEADS = SSD_WIDTH // SSD_HEAD_DIM
SSD_GROUPS = 2
SSD_STATE = 128
SSD_CONV = 4
SSD_CHUNK = 128
SSD_CONV_CH = SSD_WIDTH + 2 * SSD_GROUPS * SSD_STATE
N_BRANCH = 3
FFN_DIM = 2816
FFN_CONV = 3
IN_SPLITS = (POOL_WIDTH, ATTN_WIDTH, ATTN_WIDTH, ATTN_WIDTH, ATTN_HEADS,
             SSD_WIDTH, SSD_CONV_CH, SSD_HEADS, N_BRANCH * D_MODEL)
IN_TOTAL = sum(IN_SPLITS)


def rmsnorm(x, w):
    xf = x.astype(jnp.float32)
    y = xf * lax.rsqrt(jnp.mean(xf * xf, axis=-1, keepdims=True) + NORM_EPS)
    return (y * w.astype(jnp.float32)).astype(x.dtype)

def split_columns(proj):
    offsets, acc = [], 0
    for n in IN_SPLITS[:-1]:
        acc += n
        offsets.append(acc)
    return jnp.split(proj, offsets, axis=-1)

def causal_dwconv(x, w, b):
    K, C = w.shape
    y = lax.conv_general_dilated(
        x, w[:, None, :].astype(x.dtype), window_strides=(1,),
        padding=[(K - 1, 0)], dimension_numbers=('NWC', 'WIO', 'NWC'),
        feature_group_count=C)
    return y + b.astype(x.dtype)

def pool_mixer(v, mix_w, scale):
    B_, S, _ = v.shape
    vf = v.astype(jnp.float32).reshape(B_, S, POOL_GROUPS, POOL_GROUP_DIM)
    cs = jnp.cumsum(vf, axis=1)
    t = jnp.arange(S)
    pooled = []
    for g, w in enumerate(POOL_WINDOWS):
        c = cs[:, :, g]
        lag = jnp.pad(c, ((0, 0), (w, 0), (0, 0)))[:, :S]
        cnt = jnp.minimum(t + 1, w).astype(jnp.float32)[None, :, None]
        pooled.append((c - lag) / cnt)
    d = (jnp.stack(pooled, axis=2) - vf).astype(v.dtype)
    y = jnp.einsum('bsgc,gcd->bsgd', d, mix_w)
    return y.reshape(B_, S, POOL_WIDTH) * scale

def forgetting_attention(q, k, v, f_logit, f_bias):
    B_, S, _ = q.shape
    H, Dh = ATTN_HEADS, ATTN_HEAD_DIM
    q = q.reshape(B_, S, H, Dh).transpose(0, 2, 1, 3)
    k = k.reshape(B_, S, H, Dh).transpose(0, 2, 1, 3)
    v = v.reshape(B_, S, H, Dh).transpose(0, 2, 1, 3)
    logf = jax.nn.log_sigmoid((f_logit + f_bias).astype(jnp.float32))
    c = jnp.cumsum(logf, axis=1).transpose(0, 2, 1)
    nb = S // Q_BLOCK
    qb = q.reshape(B_, H, nb, Q_BLOCK, Dh).transpose(2, 0, 1, 3, 4)
    cb = c.reshape(B_, H, nb, Q_BLOCK).transpose(2, 0, 1, 3)
    kpos = jnp.arange(S)
    scale = Dh ** -0.5

    def block(args):
        qi, ci, i = args
        qpos = i * Q_BLOCK + jnp.arange(Q_BLOCK)
        s = jnp.einsum('bhqd,bhkd->bhqk', qi, k).astype(jnp.float32) * scale
        s = s + (ci[..., :, None] - c[:, :, None, :])
        s = jnp.where(kpos[None, :] <= qpos[:, None], s, -jnp.inf)
        p = jax.nn.softmax(s, axis=-1).astype(v.dtype)
        return jnp.einsum('bhqk,bhkd->bhqd', p, v)

    o = lax.map(block, (qb, cb, jnp.arange(nb)))
    return o.transpose(1, 0, 3, 2, 4).reshape(B_, S, H * Dh)

def segsum(a):
    L = a.shape[-1]
    cs = jnp.cumsum(a, axis=-1)
    seg = cs[..., :, None] - cs[..., None, :]
    mask = jnp.tril(jnp.ones((L, L), dtype=bool))
    return jnp.where(mask, seg, -jnp.inf)

def ssd_scan(x, dt, A, Bm, Cm):
    B_, S = x.shape[:2]
    L, G, N, P = SSD_CHUNK, SSD_GROUPS, SSD_STATE, SSD_HEAD_DIM
    E = SSD_HEADS // G
    nc = S // L
    xd = (x * dt[..., None]).reshape(B_, nc, L, G, E, P)
    a = (dt * A).reshape(B_, nc, L, G, E).transpose(0, 3, 4, 1, 2)
    Bc = Bm.reshape(B_, nc, L, G, N)
    Cc = Cm.reshape(B_, nc, L, G, N)
    a_cs = jnp.cumsum(a, axis=-1)
    Lmat = jnp.exp(segsum(a))
    cb = jnp.einsum('bclgn,bcsgn->bgcls', Cc, Bc)
    y_diag = jnp.einsum('bgcls,bgecls,bcsgep->bclgep', cb, Lmat, xd)
    decay = jnp.exp(a_cs[..., -1:] - a_cs)
    states = jnp.einsum('bclgn,bgecl,bclgep->cbgepn', Bc, decay, xd)
    chunk_decay = jnp.exp(a_cs[..., -1]).transpose(3, 0, 1, 2)

    def step(h, inp):
        s_c, d_c = inp
        return d_c[..., None, None] * h + s_c, h

    h0 = jnp.zeros(states.shape[1:], x.dtype)
    _, prev = lax.scan(step, h0, (states, chunk_decay))
    y_off = jnp.einsum('bclgn,cbgepn,bgecl->bclgep', Cc, prev, jnp.exp(a_cs))
    return (y_diag + y_off).reshape(B_, S, SSD_HEADS, P)

def ssd_mixer(z, xbc, dt_raw, conv_w, conv_b, dt_bias, a_log, d_skip, norm_w):
    B_, S, _ = z.shape
    f32 = jnp.float32
    xbc = jax.nn.silu(causal_dwconv(xbc, conv_w, conv_b))
    xs, Bm, Cm = jnp.split(xbc, [SSD_WIDTH, SSD_WIDTH + SSD_GROUPS * SSD_STATE], axis=-1)
    dt = jax.nn.softplus(dt_raw.astype(f32) + dt_bias.astype(f32))
    A = -jnp.exp(a_log.astype(f32))
    x = xs.astype(f32).reshape(B_, S, SSD_HEADS, SSD_HEAD_DIM)
    y = ssd_scan(x, dt, A,
                 Bm.astype(f32).reshape(B_, S, SSD_GROUPS, SSD_STATE),
                 Cm.astype(f32).reshape(B_, S, SSD_GROUPS, SSD_STATE))
    y = y + d_skip.astype(f32)[:, None] * x
    y = y.reshape(B_, S, SSD_WIDTH) * jax.nn.silu(z.astype(f32))
    yg = y.reshape(B_, S, SSD_GROUPS, SSD_WIDTH // SSD_GROUPS)
    yg = yg * lax.rsqrt(jnp.mean(yg * yg, axis=-1, keepdims=True) + NORM_EPS)
    return (yg.reshape(B_, S, SSD_WIDTH) * norm_w.astype(f32)).astype(z.dtype)

def conv_ffn(u, w_up, conv_w, conv_b, w_down):
    h = causal_dwconv(u @ w_up, conv_w, conv_b)
    g, val = jnp.split(h, 2, axis=-1)
    return (jax.nn.silu(g) * val) @ w_down

def first_inputs(seed: int = 0) -> dict:
    key = jax.random.key(seed)
    ks = jax.random.split(key, 24)
    f32 = jnp.float32
    L = DEPTH

    def nrm(k, shape, scale):
        return jax.random.normal(k, shape, f32) * scale

    def gain(k, shape):
        return 1.0 + 0.02 * jax.random.normal(k, shape, f32)

    dt0 = jnp.exp(jax.random.uniform(ks[9], (L, SSD_HEADS), f32,
                                     math.log(1e-3), math.log(1e-1)))
    return {
        'x': jax.random.normal(ks[0], (BATCH, SEQ, D_MODEL), f32),
        'norm_mix': gain(ks[1], (L, D_MODEL)),
        'w_in': nrm(ks[2], (L, D_MODEL, IN_TOTAL), D_MODEL ** -0.5),
        'pool_mix': nrm(ks[3], (L, POOL_GROUPS, POOL_GROUP_DIM, POOL_GROUP_DIM), POOL_GROUP_DIM ** -0.5),
        'pool_scale': 1.0 + 0.1 * jax.random.normal(ks[4], (L, POOL_WIDTH), f32),
        'f_bias': jax.random.uniform(ks[5], (L, ATTN_HEADS), f32, 1.0, 4.0),
        'ssd_conv_w': nrm(ks[6], (L, SSD_CONV, SSD_CONV_CH), SSD_CONV ** -0.5),
        'ssd_conv_b': nrm(ks[7], (L, SSD_CONV_CH), 0.02),
        'ssd_dt_bias': dt0 + jnp.log(-jnp.expm1(-dt0)),
        'ssd_a_log': jnp.log(jax.random.uniform(ks[10], (L, SSD_HEADS), f32, 1.0, 16.0)),
        'ssd_d': 1.0 + 0.1 * jax.random.normal(ks[11], (L, SSD_HEADS), f32),
        'ssd_norm': gain(ks[12], (L, SSD_WIDTH)),
        'p_pool': nrm(ks[13], (L, POOL_WIDTH, D_MODEL), POOL_WIDTH ** -0.5),
        'p_attn': nrm(ks[14], (L, ATTN_WIDTH, D_MODEL), ATTN_WIDTH ** -0.5),
        'p_ssd': nrm(ks[15], (L, SSD_WIDTH, D_MODEL), SSD_WIDTH ** -0.5),
        'w_out': nrm(ks[16], (L, D_MODEL, D_MODEL), D_MODEL ** -0.5),
        'norm_ffn': gain(ks[17], (L, D_MODEL)),
        'ffn_up': nrm(ks[18], (L, D_MODEL, 2 * FFN_DIM), D_MODEL ** -0.5),
        'ffn_conv_w': nrm(ks[19], (L, FFN_CONV, 2 * FFN_DIM), FFN_CONV ** -0.5),
        'ffn_conv_b': nrm(ks[20], (L, 2 * FFN_DIM), 0.02),
        'ffn_down': nrm(ks[21], (L, FFN_DIM, D_MODEL), FFN_DIM ** -0.5),
        'norm_final': gain(ks[22], (D_MODEL,)),
    }

def first_block(x, norm_mix, w_in, pool_mix, pool_scale, f_bias, ssd_conv_w, ssd_conv_b,
              ssd_dt_bias, ssd_a_log, ssd_d, ssd_norm, p_pool, p_attn, p_ssd, w_out,
              norm_ffn, ffn_up, ffn_conv_w, ffn_conv_b, ffn_down, norm_final):
    B_, S, D = x.shape
    for l in range(DEPTH):
        u = rmsnorm(x, norm_mix[l])
        (pool_v, q, k, v, f_logit, z, xbc, dt_raw, gate_logits) = split_columns(u @ w_in[l])
        y_pool = pool_mixer(pool_v, pool_mix[l], pool_scale[l]) @ p_pool[l]
        y_attn = forgetting_attention(q, k, v, f_logit, f_bias[l]) @ p_attn[l]
        y_ssd = ssd_mixer(z, xbc, dt_raw, ssd_conv_w[l], ssd_conv_b[l], ssd_dt_bias[l],
                          ssd_a_log[l], ssd_d[l], ssd_norm[l]) @ p_ssd[l]
        gates = jax.nn.sigmoid(gate_logits.astype(jnp.float32)).astype(x.dtype)
        gates = gates.reshape(B_, S, N_BRANCH, D)
        merged = gates[:, :, 0] * y_pool + gates[:, :, 1] * y_attn + gates[:, :, 2] * y_ssd
        x = x + merged @ w_out[l]
        x = x + conv_ffn(rmsnorm(x, norm_ffn[l]), ffn_up[l], ffn_conv_w[l], ffn_conv_b[l], ffn_down[l])
    return rmsnorm(x, norm_final)


DEPTH_2 = 2

N_A_LAYERS = DEPTH_2 // 2
N_B_LAYERS = DEPTH_2 - N_A_LAYERS

A_HEADS = 8
A_DK = 128
A_DV = 128
A_CONV = 4
A_CHUNK = 64
A_QK = A_HEADS * A_DK
A_V = A_HEADS * A_DV
A_IN = 2 * A_QK + 2 * A_V + 2 * A_HEADS

B_HEADS = 16
B_KV_HEADS = 4
B_GROUP = B_HEADS // B_KV_HEADS
B_DH = 64
B_WINDOW = 128
B_BLOCK = 128


EPS = 1e-6


def rmsnorm_2(x, g):
    xf = x.astype(jnp.float32)
    y = xf * lax.rsqrt(jnp.mean(xf * xf, axis=-1, keepdims=True) + EPS)
    return (y * g.astype(jnp.float32)).astype(x.dtype)

def l2norm(x):
    return x * lax.rsqrt(jnp.sum(x * x, axis=-1, keepdims=True) + EPS)

def causal_dwconv_2(x, w):
    K = w.shape[0]
    S = x.shape[1]
    xp = jnp.pad(x, ((0, 0), (K - 1, 0), (0, 0)))
    y = xp[:, K - 1:K - 1 + S] * w[K - 1]
    for j in range(K - 1):
        y = y + xp[:, j:j + S] * w[j]
    return y

def gated_delta_rule_chunked(q, k, v, beta, g):
    Bsz, S, H, DK = q.shape
    DV = v.shape[-1]
    C = A_CHUNK
    N = S // C

    def chunk(t):
        t = t.reshape((Bsz, N, C, H) + t.shape[3:])
        return jnp.moveaxis(t, 3, 1)

    q, k, v, beta, g = chunk(q), chunk(k), chunk(v), chunk(beta), chunk(g)
    gc = jnp.cumsum(g, axis=-1)
    idx = jnp.arange(C)
    strict = idx[:, None] > idx[None, :]
    incl = idx[:, None] >= idx[None, :]
    diff = gc[..., :, None] - gc[..., None, :]
    decay = jnp.exp(jnp.where(incl, diff, -jnp.inf))
    kb = k * beta[..., None]
    Lmat = jnp.where(strict, jnp.einsum('bhnid,bhnjd->bhnij', kb, k) * decay, 0.0)
    eye = jnp.eye(C, dtype=Lmat.dtype)
    rhs = jnp.concatenate([v * beta[..., None], kb * jnp.exp(gc)[..., None]], axis=-1)
    sol = lax.linalg.triangular_solve(eye + Lmat, rhs, left_side=True, lower=True, unit_diagonal=True)
    value, k_cumdecay = sol[..., :DV], sol[..., DV:]
    attn_intra = jnp.einsum('bhnid,bhnjd->bhnij', q, k) * decay
    q_dec = q * jnp.exp(gc)[..., None]
    k_dec = k * jnp.exp(gc[..., -1:] - gc)[..., None]
    g_last = jnp.exp(gc[..., -1])

    def step(state, xs):
        a_c, qd, kd, val, kcd, gl = xs
        v_new = val - jnp.einsum('bhcd,bhde->bhce', kcd, state)
        o = jnp.einsum('bhcd,bhde->bhce', qd, state) + jnp.einsum('bhij,bhje->bhie', a_c, v_new)
        state = state * gl[..., None, None] + jnp.einsum('bhcd,bhce->bhde', kd, v_new)
        return state, o

    xs = tuple(jnp.moveaxis(t, 2, 0) for t in (attn_intra, q_dec, k_dec, value, k_cumdecay, g_last))
    state0 = jnp.zeros((Bsz, H, DK, DV), jnp.float32)
    _, o = lax.scan(step, state0, xs)
    o = jnp.moveaxis(jnp.moveaxis(o, 0, 2), 1, 3)
    return o.reshape(Bsz, S, H, DV)

def deltanet_mixer(h, w_in, conv_w, A_log, dt_bias, onorm_g, w_out):
    Bsz, S, _ = h.shape
    f32 = jnp.float32
    p = h @ w_in
    qkv, gate, b_raw, a_raw = jnp.split(p, [2 * A_QK + A_V, 2 * A_QK + 2 * A_V, 2 * A_QK + 2 * A_V + A_HEADS], axis=-1)
    qkv = jax.nn.silu(causal_dwconv_2(qkv, conv_w))
    q, k, v = jnp.split(qkv, [A_QK, 2 * A_QK], axis=-1)
    q = l2norm(q.reshape(Bsz, S, A_HEADS, A_DK).astype(f32)) * (A_DK ** -0.5)
    k = l2norm(k.reshape(Bsz, S, A_HEADS, A_DK).astype(f32))
    v = v.reshape(Bsz, S, A_HEADS, A_DV).astype(f32)
    beta = jax.nn.sigmoid(b_raw.astype(f32))
    g = -jnp.exp(A_log.astype(f32)) * jax.nn.softplus(a_raw.astype(f32) + dt_bias.astype(f32))
    o = gated_delta_rule_chunked(q, k, v, beta, g)
    o = rmsnorm_2(o, onorm_g) * jax.nn.silu(gate.reshape(Bsz, S, A_HEADS, A_DV).astype(f32))
    return o.reshape(Bsz, S, A_V).astype(h.dtype) @ w_out

def swa_sink_attention(h, k_sh, v_sh, w_q, b_q, sinks, w_o, b_o):
    Bsz, S, _ = h.shape
    f32 = jnp.float32
    NB = S // B_BLOCK
    q = (h @ w_q + b_q).astype(f32) * (B_DH ** -0.5)
    q = q.reshape(Bsz, NB, B_BLOCK, B_KV_HEADS, B_GROUP, B_DH)

    def with_prev(t):
        t = t.astype(f32).reshape(Bsz, NB, B_BLOCK, B_KV_HEADS, B_DH)
        prev = jnp.pad(t, ((0, 0), (1, 0), (0, 0), (0, 0), (0, 0)))[:, :-1]
        return jnp.concatenate([prev, t], axis=2)

    kb, vb = with_prev(k_sh), with_prev(v_sh)
    slopes = (2.0 ** (-8.0 * jnp.arange(1, B_HEADS + 1, dtype=f32) / B_HEADS)).reshape(B_KV_HEADS, B_GROUP)
    qi = jnp.arange(B_BLOCK)[:, None]
    kj = jnp.arange(2 * B_BLOCK)[None, :]
    dist = qi + B_BLOCK - kj
    band = (dist >= 0) & (dist < B_WINDOW)
    bias = -slopes[:, :, None, None] * dist.astype(f32)
    sink = sinks.astype(f32).reshape(B_KV_HEADS, B_GROUP)[None, :, :, None]

    def block_attn(args):
        qb, kk, vv, blk = args
        s = jnp.einsum('bqkgd,bskd->bkgqs', qb, kk) + bias
        valid = band & ((blk > 0) | (kj >= B_BLOCK))
        s = jnp.where(valid, s, -jnp.inf)
        m = jnp.maximum(jnp.max(s, axis=-1), sink)
        p = jnp.exp(s - m[..., None])
        denom = jnp.sum(p, axis=-1) + jnp.exp(sink - m)
        o = jnp.einsum('bkgqs,bskd->bqkgd', p, vv)
        return o / jnp.transpose(denom, (0, 3, 1, 2))[..., None]

    xs = (jnp.moveaxis(q, 1, 0), jnp.moveaxis(kb, 1, 0), jnp.moveaxis(vb, 1, 0), jnp.arange(NB, dtype=jnp.int32))
    o = lax.map(block_attn, xs)
    o = jnp.moveaxis(o, 0, 1).reshape(Bsz, S, B_HEADS * B_DH)
    return o.astype(h.dtype) @ w_o + b_o

def conv_ffn_2(h, w_up, conv_w, conv_b, w_down):
    u = causal_dwconv_2(h @ w_up, conv_w) + conv_b
    gate, up = jnp.split(u, 2, axis=-1)
    return (jax.nn.silu(gate) * up) @ w_down

def second_inputs(seed: int = 0) -> dict:
    key = jax.random.key(seed)
    ks = jax.random.split(key, 24)
    f32 = jnp.float32

    def nrm(k, shape, fan_in):
        return jax.random.normal(k, shape, f32) * (fan_in ** -0.5)

    def gain(k, shape):
        return 1.0 + 0.05 * jax.random.normal(k, shape, f32)

    def small(k, shape):
        return 0.02 * jax.random.normal(k, shape, f32)

    x = jax.random.normal(ks[0], (BATCH, SEQ, D_MODEL), f32)
    a_norm = gain(ks[1], (N_A_LAYERS, D_MODEL))
    a_w_in = nrm(ks[2], (N_A_LAYERS, D_MODEL, A_IN), D_MODEL)
    a_conv_w = nrm(ks[3], (N_A_LAYERS, A_CONV, 2 * A_QK + A_V), A_CONV)
    a_A_log = jnp.log(jax.random.uniform(ks[4], (N_A_LAYERS, A_HEADS), f32, 1.0, 16.0))
    dt = jnp.exp(jax.random.uniform(ks[5], (N_A_LAYERS, A_HEADS), f32, math.log(1e-3), math.log(1e-1)))
    a_dt_bias = dt + jnp.log(-jnp.expm1(-dt))
    a_onorm = gain(ks[6], (N_A_LAYERS, A_DV))
    a_w_out = nrm(ks[7], (N_A_LAYERS, A_V, D_MODEL), A_V)
    kv_norm = gain(ks[8], (D_MODEL,))
    kv_w = nrm(ks[9], (D_MODEL, 2 * B_KV_HEADS * B_DH), D_MODEL)
    kv_b = small(ks[10], (2 * B_KV_HEADS * B_DH,))
    b_norm = gain(ks[11], (N_B_LAYERS, D_MODEL))
    b_w_q = nrm(ks[12], (N_B_LAYERS, D_MODEL, B_HEADS * B_DH), D_MODEL)
    b_b_q = small(ks[13], (N_B_LAYERS, B_HEADS * B_DH))
    b_sinks = jax.random.normal(ks[14], (N_B_LAYERS, B_HEADS), f32)
    b_w_o = nrm(ks[15], (N_B_LAYERS, B_HEADS * B_DH, D_MODEL), B_HEADS * B_DH)
    b_b_o = small(ks[16], (N_B_LAYERS, D_MODEL))
    f_norm = gain(ks[17], (DEPTH_2, D_MODEL))
    f_w_up = nrm(ks[18], (DEPTH_2, D_MODEL, 2 * FFN_DIM), D_MODEL)
    f_conv_w = nrm(ks[19], (DEPTH_2, FFN_CONV, 2 * FFN_DIM), FFN_CONV)
    f_conv_b = small(ks[20], (DEPTH_2, 2 * FFN_DIM))
    f_w_down = nrm(ks[21], (DEPTH_2, FFN_DIM, D_MODEL), FFN_DIM)
    final_norm = gain(ks[22], (D_MODEL,))
    return {'x': x, 'a_norm': a_norm, 'a_w_in': a_w_in, 'a_conv_w': a_conv_w, 'a_A_log': a_A_log,
            'a_dt_bias': a_dt_bias, 'a_onorm': a_onorm, 'a_w_out': a_w_out,
            'kv_norm': kv_norm, 'kv_w': kv_w, 'kv_b': kv_b,
            'b_norm': b_norm, 'b_w_q': b_w_q, 'b_b_q': b_b_q, 'b_sinks': b_sinks, 'b_w_o': b_w_o, 'b_b_o': b_b_o,
            'f_norm': f_norm, 'f_w_up': f_w_up, 'f_conv_w': f_conv_w, 'f_conv_b': f_conv_b, 'f_w_down': f_w_down,
            'final_norm': final_norm}

def second_block(x, a_norm, a_w_in, a_conv_w, a_A_log, a_dt_bias, a_onorm, a_w_out,
              kv_norm, kv_w, kv_b,
              b_norm, b_w_q, b_b_q, b_sinks, b_w_o, b_b_o,
              f_norm, f_w_up, f_conv_w, f_conv_b, f_w_down, final_norm):
    Bsz, S, _ = x.shape
    h = x
    k_sh = None
    v_sh = None
    for layer in range(DEPTH_2):
        if layer < N_A_LAYERS:
            i = layer
            h = h + deltanet_mixer(rmsnorm_2(h, a_norm[i]), a_w_in[i], a_conv_w[i], a_A_log[i],
                                   a_dt_bias[i], a_onorm[i], a_w_out[i])
        else:
            i = layer - N_A_LAYERS
            if i == 0:
                kv = rmsnorm_2(h, kv_norm) @ kv_w + kv_b
                k_sh, v_sh = jnp.split(kv, 2, axis=-1)
                k_sh = k_sh.reshape(Bsz, S, B_KV_HEADS, B_DH)
                v_sh = v_sh.reshape(Bsz, S, B_KV_HEADS, B_DH)
            h = h + swa_sink_attention(rmsnorm_2(h, b_norm[i]), k_sh, v_sh, b_w_q[i], b_b_q[i],
                                       b_sinks[i], b_w_o[i], b_b_o[i])
        h = h + conv_ffn_2(rmsnorm_2(h, f_norm[layer]), f_w_up[layer], f_conv_w[layer],
                         f_conv_b[layer], f_w_down[layer])
    return rmsnorm_2(h, final_norm)


def setup_inputs(seed=0):
    out = dict(first_inputs(seed))
    for name, value in second_inputs(seed + 1).items():
        if name != "x":
            out[name + "_2"] = value
    return out


def reference(
    x, norm_mix, w_in, pool_mix, pool_scale, f_bias, ssd_conv_w, ssd_conv_b, ssd_dt_bias,
    ssd_a_log, ssd_d, ssd_norm, p_pool, p_attn, p_ssd, w_out, norm_ffn, ffn_up, ffn_conv_w,
    ffn_conv_b, ffn_down, norm_final, a_norm_2, a_w_in_2, a_conv_w_2, a_A_log_2, a_dt_bias_2,
    a_onorm_2, a_w_out_2, kv_norm_2, kv_w_2, kv_b_2, b_norm_2, b_w_q_2, b_b_q_2, b_sinks_2,
    b_w_o_2, b_b_o_2, f_norm_2, f_w_up_2, f_conv_w_2, f_conv_b_2, f_w_down_2, final_norm_2,
):
    x = first_block(
        x, norm_mix, w_in, pool_mix, pool_scale, f_bias, ssd_conv_w, ssd_conv_b, ssd_dt_bias,
        ssd_a_log, ssd_d, ssd_norm, p_pool, p_attn, p_ssd, w_out, norm_ffn, ffn_up, ffn_conv_w,
        ffn_conv_b, ffn_down, norm_final,
    )
    return second_block(
        x, a_norm_2, a_w_in_2, a_conv_w_2, a_A_log_2, a_dt_bias_2, a_onorm_2, a_w_out_2,
        kv_norm_2, kv_w_2, kv_b_2, b_norm_2, b_w_q_2, b_b_q_2, b_sinks_2, b_w_o_2, b_b_o_2,
        f_norm_2, f_w_up_2, f_conv_w_2, f_conv_b_2, f_w_down_2, final_norm_2,
    )


_drawn_inputs = setup_inputs


def setup_inputs(seed=0):
    import zlib

    import numpy as np

    out = dict(_drawn_inputs(seed))
    spreads = {}
    factors = {'ssd_conv_b': 2.982,
     'ssd_norm': 4.026,
     'norm_ffn': 3.041,
     'ffn_conv_b': 3.01,
     'kv_norm_2': 3.585,
     'kv_b_2': 3.674,
     'b_norm_2': 6.039,
     'b_b_q_2': 8.0,
     'b_b_o_2': 9.794,
     'f_conv_b_2': 2.987,
     'b_sinks_2': 8.0}
    for name, (base, spread) in spreads.items():
        noise = np.random.default_rng([zlib.crc32(name.encode()), seed]).standard_normal(out[name].shape)
        drawn = base * np.exp(spread * noise) if base else spread * noise
        out[name] = jnp.asarray(drawn.astype(out[name].dtype))
    for name, factor in factors.items():
        out[name] = (out[name] * factor).astype(out[name].dtype)
    return out
```

```python
from contextlib import ExitStack

import concourse.bass as bass
import concourse.mybir as mybir

F32 = mybir.dt.float32
F32R = mybir.dt.float32r
BF16 = mybir.dt.bfloat16
ALU = mybir.AluOpType
ACT = mybir.ActivationFunctionType
AX_X = mybir.AxisListType.X

P = 128
S = 512
D = 1024
KT = D // P
NT = S // P
EPS = 1e-6
MASKED = -1e30

POOL_W, ATT_W, SSD_W = 512, 512, 1024
ATT_HEADS, SSD_HEADS, SSD_GROUPS, HD = 8, 16, 2, 64
WINDOWS = (2, 4, 8, 16)
PADV = 16
XBC = SSD_W + 2 * SSD_GROUPS * P
XT = XBC // P
C_POOL, C_Q, C_V, C_F = 0, 512, 1536, 2048
C_Z = 2056
C_XBC = C_Z + SSD_W
C_DT = C_XBC + XBC
C_GATE = C_DT + SSD_HEADS
FFN = 2816
FT = FFN // P
DN_HEADS = 8
A_QKV, A_V = 3072, 1024
SWA_HEADS, KV_HEADS = 16, 4

PHASES = (
    ("xbc", 6, "std"), ("z", 4, "std"), ("pool", 2, "std"), ("qk", 4, "std"), ("v", 2, "tok"),
    ("gate0", 4, "std"), ("proj_pool", 2, "half"), ("gate1", 4, "std"), ("proj_attn", 2, "half"),
    ("gate2", 4, "std"), ("proj_ssd", 4, "std"), ("w_out", 4, "std"),
    ("up0", 22, "std"), ("down0", 11, "down"),
    ("a_qkv", 12, "std"), ("a_gate", 4, "std"), ("a_out", 4, "std"),
    ("up1", 22, "std"), ("down1", 11, "down"),
    ("kv_k", 1, "std"), ("kv_v", 1, "tok"), ("q2", 4, "std"), ("o2", 4, "std"),
    ("up2", 22, "std"), ("down2", 11, "down"),
)


class Phase:

    def __init__(self, name, quads, kind, first, fills):
        self.name, self.quads, self.kind, self.first, self.fills = name, quads, kind, first, fills


def plan():
    out, first, fills = {}, 0, 0
    pair = 0
    counts = [0, 0]
    for name, quads, kind in PHASES:
        out[name] = Phase(name, quads, kind, first, tuple(counts))
        first += quads
        if kind == "half":
            counts = [counts[0] + quads, counts[1] + quads]
        elif kind == "down":
            counts = [counts[0] + 1, counts[1] + 1]
        elif quads == 1:
            counts[1 if name == "kv_v" else 0] += 1
        else:
            counts = [counts[0] + quads // 2, counts[1] + quads // 2]
    return out, first


PLAN, QUADS = plan()


class Events:

    def __init__(self, sem, names, seed=0):
        self.sem, self.names, self.seed, self.next = sem, list(names), seed, 0
        self.at = {n: i for i, n in enumerate(self.names)}
        assert len(self.at) == len(self.names)

    def mark(self, name):
        assert self.names[self.next] == name, (self.names[self.next], name)
        self.next = (self.next + 1) % len(self.names)
        return 1

    def value(self, name, turn=0):
        return turn * len(self.names) + (self.seed + self.at[name] + 1)


def layered_mixers(nc, x, norm_mix, w_in, pool_mix, pool_scale, f_bias, ssd_conv_w, ssd_conv_b,
                   ssd_dt_bias, ssd_a_log, ssd_d, ssd_norm, p_pool, p_attn, p_ssd, w_out,
                   norm_ffn, ffn_up, ffn_conv_w, ffn_conv_b, ffn_down, norm_final,
                   a_norm_2, a_w_in_2, a_conv_w_2, a_A_log_2, a_dt_bias_2, a_onorm_2, a_w_out_2,
                   kv_norm_2, kv_w_2, kv_b_2, b_norm_2, b_w_q_2, b_b_q_2, b_sinks_2,
                   b_w_o_2, b_b_o_2, f_norm_2, f_w_up_2, f_conv_w_2, f_conv_b_2, f_w_down_2,
                   final_norm_2, out):
    ctx = ExitStack()
    with ctx:
        def sem(name):
            return ctx.enter_context(nc.semaphore(name))

        place, place_of = [nc.sbuf_base], {}
        place[0] = (place[0] + 63) // 64 * 64

        def fixed(name, shape, dt=F32):
            size = 2 if dt == BF16 else 4
            for n in shape[1:]:
                size *= n
            place_of[name] = place[0]
            t = nc.alloc_sbuf_tensor_at(name, shape, dt, offset=place[0])
            place[0] += (size + 31) // 32 * 32
            return t

        raw = fixed("raw", [P, 4, 512])
        whi = fixed("whi", [P, 4, 512], F32R)
        wlo = fixed("wlo", [P, 4, 512], F32R)
        h = fixed("h", [P, KT, S])
        uh = fixed("uh", [P, KT, S], F32R)
        ul = fixed("ul", [P, KT, S], F32R)
        ident = fixed("ident", [P, P])
        ones = fixed("ones", [P, P])
        ident_bf = fixed("ident_bf", [P, P], BF16)
        mask_q = fixed("mask_q", [P, P], BF16)
        upto = fixed("upto", [P, P])
        last_row = fixed("last_row", [P, P])
        keep = fixed("keep", [48, S])
        par = fixed("par", [P, 9, P])
        inv_count = fixed("inv_count", [P, 16])
        sgn = fixed("sgn", [48, 1])
        sgn_bias = fixed("sgn_bias", [48, 2])
        raw_bias = fixed("raw_bias", [48, 2])
        a_log = fixed("a_log", [48, 2])
        row_scale = fixed("row_scale", [48, 2])
        d_skip = fixed("d_skip", [P, KT])
        tok = fixed("tok", [P, 2, NT, 48])
        decay_end = fixed("decay_end", [P, NT, 48])
        chunk_decay = fixed("chunk_decay", [P, NT, 48])
        stat = fixed("stat", [P, 64])
        level = fixed("level", [P, 7, P], BF16)
        dist = fixed("dist", [P, 2 * P], BF16)
        far = fixed("far", [P, 2 * P], BF16)
        minus_slope = fixed("minus_slope", [P, SWA_HEADS])
        sinks = fixed("sinks", [P, SWA_HEADS])
        seed = fixed("seed", [1, 64])
        area = place[0]
        room = nc.sbuf_usable_end - area

        def at(name, shape, kb, dt=F32):
            size = 2 if dt == BF16 else 4
            for n in shape[1:]:
                size *= n
            off = int(kb * 1024)
            assert off + size <= room, (name, off + size, room)
            return nc.alloc_sbuf_tensor_at(name, shape, dt, offset=area + off)

        sq = at("sq", [P, 2, S], 0)
        ms = at("ms", [P, S], 4)
        rc = at("rc", [P, S], 6)
        rs = at("rs", [P, S], 8)
        uf = at("uf", [P, 2, S], 10)
        ws = at("ws", [P, KT, 48], 80)
        wsh = at("wsh", [P, KT, 48], 82, F32R)
        wsl = at("wsl", [P, KT, 48], 84, F32R)
        sc = at("sc", [48, 10, S], 56)
        cs = at("cs", [48, S], 117)
        x_in = at("x_in", [P, NT, D], 24)
        out_t = at("out_t", [P, KT, S], 40)
        par_in = at("par_in", [P, 9, P], 60)

        cv = at("cv", [P, 4, S], 92)
        xc = at("xc", [P, XT, S], 0)
        xd = at("xd", [P, NT, SSD_W], 24)
        xdd = at("xdd", [P, SSD_W], 40)
        st = at("st", [P, 3, SSD_W], 44)
        bt = at("bt", [P, 2 * P], 56)
        stq = at("stq", [P, SSD_W], 57)
        y_tok = at("y_tok", [P, NT, SSD_W], 61)
        zs = at("zs", [P, KT, S], 77)
        cb = at("cb", [P, SSD_GROUPS, S], 93)
        dd = at("dd", [P, 2, S], 97)
        mt = at("mt", [P, 2, S], 101)
        ec = at("ec", [P, 2, S], 105)
        ce = at("ce", [P, 2, S], 109)
        oh = at("oh", [48, 2, S], 113)
        ysh = at("ysh", [P, KT, S], 24, F32R)
        ysl = at("ysl", [P, KT, S], 40, F32R)
        ysq = at("ysq", [P, 2, S], 97)
        yms = at("yms", [P, 2, S], 101)
        yrs = at("yrs", [P, 2, S], 105)
        yf = at("yf", [P, 2, S], 109)
        pv = at("pv", [P, 4, PADV + S], 0)
        win = at("win", [P, 2, PADV + S], 9)
        dp = at("dp", [P, 4, S], 16)
        yph = at("yph", [P, 4, S], 100, F32R)
        ypl = at("ypl", [P, 4, S], 108, F32R)
        mix = at("mix", [P, 4, P], 58)
        qk = at("qk", [P, KT, S], 62)
        v = at("v", [P, NT, ATT_W], 78)
        oa = at("oa", [P, NT, ATT_W], 86)
        qs = at("qs", [P, S], 0)
        ks = at("ks", [P, S], 96)
        nb = at("nb", [P, 2, S], 2)
        sm = at("sm", [P, 2, S], 6)
        pe_ = at("probs", [P, 2, S], 10)
        pt = at("pt", [P, 2, S], 56)
        ohc = at("ohc", [48, S], 14)
        yah = at("yah", [P, 4, S], 16, F32R)
        yal = at("yal", [P, 4, S], 78, F32R)
        gt = at("gt", [P, KT, S], 0)
        mg = at("mg", [P, KT, S], 62)
        tmp = at("tmp", [P, 2, S], 56)

        fh = at("fh", [P, FT, S], 0, F32R)
        fl = at("fl", [P, FT, S], 44, F32R)
        fc = at("fc", [P, 4, S], 88)
        fg = at("fg", [P, 2, S], 96)
        ff = at("ff", [P, 2, S], 100)

        ac = at("ac", [P, 24, S], 0)
        ga = at("ga", [P, KT, S], 48)
        acv = at("acv", [P, 4, S], 88)
        asq = at("asq", [P, 2, S], 96)

        def head_tiles(name, start, cols=S):
            return [at(f"{name}{e}", [P, cols], start + 28 * e) for e in range(2)]

        kf, vf, qf = head_tiles("kf", 64), head_tiles("vf", 66), head_tiles("qf", 68)
        kn, vb, qn = head_tiles("kn", 70), head_tiles("vb", 72), head_tiles("qn", 74)
        kb, kbe, kd = head_tiles("kb", 76), head_tiles("kbe", 78), head_tiles("kd", 80)
        em, eg = head_tiles("em", 82), head_tiles("eg", 84)
        ti, tt, vn = head_tiles("ti", 86), head_tiles("tt", 88), head_tiles("vn", 90)
        kt, kbt, qt, ltk, an, lt, xi, nkc = kf, vf, qf, kn, qn, kb, em, vf
        over_uh, over_ul = place_of["uh"], place_of["ul"]

        def over(name, shape, offset):
            return nc.alloc_sbuf_tensor_at(name, shape, F32, offset=over_ul + offset)

        ot = nc.alloc_sbuf_tensor_at("ot", [P, NT, A_V], F32, offset=over_uh)
        goh, cs2 = over("goh", [48, 2, S], 0), over("cs2", [48, S], 4096)
        beta, egc, bege = (over(n, [P, NT, 8], 6144 + 128 * i) for i, n in enumerate(("beta", "egc", "bege")))
        rn, rn2 = over("rn", [P, 16, NT], 6528), over("rn2", [P, 16, NT], 6784)
        oss, oss2 = over("oss", [P, NT, 8], 7040), over("oss2", [P, NT, 8], 7168)
        sg = [over(f"sg{e}", [P, P], 7296 + 512 * e) for e in range(2)]
        osq = at("osq", [P, 2, A_V], 64)
        ayf = at("ayf", [P, 2, S], 72)
        ayh = at("ayh", [P, KT, S], 0, F32R)
        ayl = at("ayl", [P, KT, S], 16, F32R)

        ubh = at("ubh", [P, KT, S], 16, F32R)
        ubl = at("ubl", [P, KT, S], 32, F32R)
        kk = at("kk", [P, KV_HEADS, S], 48)
        vv = at("vv", [P, NT, 256], 56)
        q2 = at("q2", [P, KT, S], 60)
        o_tok = at("o_tok", [P, NT, D], 76)
        qst = at("qst", [P, 2, S], 92)
        kst = at("kst", [P, S], 96)
        sm2 = at("sm2", [P, 2, NT, 256], 98)
        pr2 = at("pr2", [P, 2, NT, 256], 106)
        pt2 = at("pt2", [P, 7, P], 114)
        kraw = at("kraw", [P, 2, S], 114)
        ab = at("ab", [P, 2, 256], 10)
        vbias = at("vbias", [P, 256], 14)
        st2 = at("st2", [P, 64], 15)
        ps = ctx.enter_context(nc.psum_tensor("ps", [P, 8, 512], F32))

        raw_landed = [sem(f"raw_landed{j}") for j in range(4)]
        hi_ready, lo_ready, pe_used = sem("hi_ready"), sem("lo_ready"), sem("pe_used")
        lin_free = [sem("lin_free0"), sem("lin_free1")]
        consts_ready, later_ready, seeded = sem("consts_ready"), sem("later_ready"), sem("seeded")
        x_landed, par_landed, small_landed, mix_landed = (
            sem("x_landed"), sem("par_landed"), sem("small_landed"), sem("mix_landed"))
        stored, sinks_landed = sem("stored"), sem("sinks_landed")
        k8 = range(KT)
        prep_dve = Events(sem("prep_dve"), ["par0", "par1", "par2", "wsh", "wsl", "sgn_bias", "a_neg"])
        prep_act = Events(sem("prep_act"), ["a_exp"])
        x_pe = Events(sem("x_pe"), ["par0", "par1", "par2"] + [f"x{k}" for k in k8])
        x_ready, renormed = sem("x_ready"), sem("renormed")
        h_high = sem("h_high")
        norm_act = Events(sem("norm_act"), [f"sq{k}" for k in k8] + ["rs"])
        norm_pe = Events(sem("norm_pe"), [f"sum{k}" for k in k8])
        norm_dve = Events(sem("norm_dve"), ["ms", "rc"])
        u_act = Events(sem("u_act"), [f"uh{k}" for k in k8])
        u_dve = Events(sem("u_dve"), ["u0"] + sum([[f"u{k + 1}", f"ul{k}"] for k in range(KT - 1)], []) + ["ul7"])
        sc_pe = Events(sem("sc_pe"), ["logits", "turned", "last"])
        sc_act = Events(sem("sc_act"), ["exp", "ln", "decay", "chunk"])
        sc_dve = Events(sem("sc_dve"), ["t", "abs", "one", "w", "eq", "den", "inv", "num", "q", "r",
                                        "sp", "scaled", "sums", "tok", "end"])
        conv_act = Events(sem("conv_act"), ["t0", "t1", "s0", "s1", "t2", "t3", "s2", "s3"], seed=8)
        conv_dve = Events(sem("conv_dve"), ["a0", "a1", "b0", "b1", "a2", "a3", "b2", "b3"], seed=8)
        ffn_act = Events(sem("ffn_act"), ["t0", "t1", "s0", "s1", "t2", "t3", "fh0", "fh1"], seed=8)
        ffn_dve = Events(sem("ffn_dve"), ["a0", "a1", "a2", "a3", "hf0", "hf1", "fl0", "fl1"], seed=8)
        ch = range(NT)
        ssd_pe = Events(sem("ssd_pe"), ["cb0", "cb1"] + sum([[f"x{c}", f"b{c}", f"state{c}_0", f"state{c}_1"]
                                                             for c in range(3)], []) + ["x3"])
        ssd_dve = Events(sem("ssd_dve"), ["cb0", "cb1", "xd0", "b0", "xdd0", "st0"]
                         + ["xd1", "b1", "xdd1", "dec1", "st1", "xd2", "b2", "xdd2", "dec2", "st2", "xd3"])
        sh_pe = Events(sem("sh_pe"), ["row0", "row1", "y0", "y1"], seed=4)
        sh_act = Events(sem("sh_act"), ["e0", "r0", "e1", "r1", "y0", "y1"], seed=6)
        sh_dve = Events(sem("sh_dve"), ["oh0", "oh1", "d0", "d1", "m0", "c0", "m1", "c1"], seed=8)
        sy_pe = Events(sem("sy_pe"), ["t0", "t1"] + sum([[f"t{k + 2}", f"sum{k}"] for k in range(6)], [])
                       + ["sum6", "sum7"])
        sy_act = Events(sem("sy_act"), [f"sq{k}" for k in k8] + ["rs0", "rs1"] + [f"h{k}" for k in k8])
        sy_dve = Events(sem("sy_dve"), sum([[f"w{k}", f"g{k}"] for k in k8], []) + ["ms0", "rc0", "ms1", "rc1"]
                        + ["f0"] + sum([[f"f{k + 1}", f"l{k}"] for k in range(7)], []) + ["l7"])
        po_act = Events(sem("po_act"), [f"h{g}" for g in range(4)])
        po_dve = Events(sem("po_dve"), ["pad"] + sum([[f"s{g}_{n}" for n in range(g + 1)] + [f"d{g}", f"q{g}", f"e{g}"]
                                             for g in range(4)], []) + [f"l{g}" for g in range(4)])
        po_pe = Events(sem("po_pe"), [f"y{g}" for g in range(4)])
        AT_PE = ("bc", "s0", "s1", "t0", "o0", "s2", "t1", "o1", "s3", "t2", "o2", "t3", "o3")
        AT_ACT = ("p0", "p1", "c0", "p2", "c1", "p3", "c2", "c3")
        AT_DVE = ("oh", "nb", "s0", "x0", "m0", "s1", "x1", "m1", "r0", "o0", "s2", "x2", "m2", "r1", "o1", "s3", "x3", "m3",
                  "r2", "o2", "r3", "o3")
        at_pe = Events(sem("at_pe"), [f"{e}{n}" for e in range(2) for n in AT_PE], seed=26)
        at_act = Events(sem("at_act"), ["qs", "ks"] + [f"{e}{n}" for e in range(2) for n in AT_ACT], seed=18)
        at_dve = Events(sem("at_dve"), [f"{e}{n}" for e in range(2) for n in AT_DVE], seed=44)
        ay_pe = Events(sem("ay_pe"), [f"t{k}" for k in range(4)])
        ay_act = Events(sem("ay_act"), [f"h{k}" for k in range(4)])
        ay_dve = Events(sem("ay_dve"), [f"l{k}" for k in range(4)])
        mg_dve = Events(sem("mg_dve"), ["m0", "m1", "m2", "m3"], seed=4)
        mg_act = Events(sem("mg_act"), ["h0", "h1"])
        mg_low = Events(sem("mg_low"), ["l0", "l1"])

        fin_pe = Events(sem("fin_pe"), [f"t{n}" for n in ch])
        fin_dve = Events(sem("fin_dve"), [f"c{n}" for n in ch])
        made = sem("made")
        TAPS = {"xbc": XT}
        prep_dve2 = Events(sem("prep_dve2"), ["zero", "wsh", "wsl"])
        GP = (["raw", "row", "turned", "prod", "t0"] + sum([[f"x{k}", f"t{k}", f"tt{k}"] for k in range(1, 6)], [])
              + ["x6", "tt6", "nk", "v0", "o0", "s0", "v1", "o1", "s1", "v2", "o2", "s2", "v3", "o3"])
        GA = (["stk", "stv", "stq", "eg", "em", "kt", "kbt", "qt", "ti0"] + [f"ti{k}" for k in range(1, 6)]
              + ["nkc", "vn0", "vn1", "vn2", "vn3"])
        GD = (["goh", "kn", "vb", "qn", "kb", "d", "kbe", "kd", "mask", "qd", "lt", "an", "i0", "tt0"]
              + sum([[f"ltk{k}", f"xi{k}", f"tt{k}"] for k in range(1, 7)], []) + ["s0", "s1", "s2", "ot"])
        both = lambda steps: [f"{e}{s}" for s in steps for e in range(2)]
        g_pe = Events(sem("g_pe"), both(GP), seed=2 * len(GP))
        g_act = Events(sem("g_act"), both(GA), seed=2 * len(GA))
        g_dve = Events(sem("g_dve"), both(GD), seed=2 * len(GD))
        gn_pe = Events(sem("gn_pe"), [f"n{t}" for t in range(16)] + [f"t{k}" for k in k8])
        gn_act = Events(sem("gn_act"), ["beta", "egc"] + [f"sq{t}" for t in range(16)] + ["rt"] + [f"q{n}" for n in ch] + ["or"]
                        + [f"h{k}" for k in k8])
        gn_dve = Events(sem("gn_dve"), ["cs", "ns", "nr", "qs", "bege"] + [f"red{n}" for n in ch] + ["om", "orc"]
                        + [f"sc{n}" for n in ch] + sum([[f"f{k}", f"l{k}"] for k in k8], []))
        BP = ("s0", "s1", "t0", "s2", "o0", "t1", "s3", "o1", "t2", "o2", "t3", "o3")
        BA = ("st", "p0", "p1", "c0", "p2", "c1", "p3", "c2", "c3")
        BD = sum([[f"ab{u}", f"sa{u}", f"sb{u}", f"mx{u}", f"ng{u}"] + ([f"den{u - 1}", f"rec{u - 1}", f"o{u - 1}"] if u else [])
                  for u in range(4)], []) + ["den3", "rec3", "o3"]
        b_pe = Events(sem("b_pe"), BP, seed=len(BP))
        b_act = Events(sem("b_act"), BA, seed=len(BA))
        b_dve = Events(sem("b_dve"), BD, seed=len(BD))
        kv_dve = Events(sem("kv_dve"), ["far"] + [f"k{n}" for n in range(8)])
        bo_pe = Events(sem("bo_pe"), [f"t{k}" for k in k8])
        bo_act = Events(sem("bo_act"), [f"h{k}" for k in k8])
        bo_dve = Events(sem("bo_dve"), [f"l{k}" for k in k8])
        vbias_landed = sem("vbias_landed")
        out_made = sem("out_made")
        TAPS["a_qkv"] = 24

        def as_rows(src):
            if len(src.shape) == 1:
                return src.rearrange("(r c) -> r c", c=P)
            return src.rearrange("a (r c) -> a r c", c=P).rearrange("a r c -> (a r) c")

        def std_value(ph, p, turn, c=1):
            return 2 * turn + (2 * PLAN[ph].fills[p] + 3 + c)

        def h_wait(eng, update, k):
            name = ("x", "w_out", "down0", "renormed", "a_out", "down1", "o2", "down2")[update]
            if update == 0:
                eng.wait_ge(x_ready, k + 1)
            elif name == "renormed":
                eng.wait_ge(renormed, k + 1)
            elif name.startswith("down"):
                if k < 4:
                    eng.wait_ge(lin_free[k // 2], std_value(name, k // 2, 0, k % 2))
                else:
                    eng.wait_ge(h_high, 4 * int(name[4]) + k - 3)
            else:
                g = k // 2
                eng.wait_ge(lin_free[g % 2], std_value(name, g % 2, g // 2, k % 2))

        ROWS = (
            (("norm_mix", norm_mix[0], 8), ("norm_ffn", norm_ffn[0], 8), ("norm_final", norm_final, 8),
             ("ssd_norm", ssd_norm[0], 8), ("pool_scale", pool_scale[0], 4), ("ssd_conv_b", ssd_conv_b[0], XT),
             ("ssd_conv_w", ssd_conv_w[0], 4 * XT)),
            (("a_norm", a_norm_2[0], 8), ("kv_norm", kv_norm_2, 8), ("b_norm", b_norm_2[0], 8),
             ("f_norm0", f_norm_2[0], 8), ("f_norm1", f_norm_2[1], 8), ("final_norm", final_norm_2, 8),
             ("kv_b", kv_b_2, 4), ("b_q", b_b_q_2[0], 8), ("b_o", b_b_o_2[0], 8), ("onorm", a_onorm_2[0], 1)),
            (("a_conv_w", a_conv_w_2[0], 96),),
            (("f0w", ffn_conv_w[0, 0:2], 88),), (("f0b", ffn_conv_w[0, 2], 44), ("f0c", ffn_conv_b[0], 44)),
            (("f1w", f_conv_w_2[0, 0:2], 88),), (("f1b", f_conv_w_2[0, 2], 44), ("f1c", f_conv_b_2[0], 44)),
            (("f2w", f_conv_w_2[1, 0:2], 88),), (("f2b", f_conv_w_2[1, 2], 44), ("f2c", f_conv_b_2[1], 44)),
        )
        COL = {}
        for n, rows in enumerate(ROWS):
            r0 = 0
            for name, _, rows_n in rows:
                COL[name] = (n, r0)
                r0 += rows_n

        def column(name, t):
            n, r0 = COL[name]
            return par[:, n, r0 + t:r0 + t + 1] if isinstance(t, int) else par[:, n, bass.ds(t + r0, 1)]

        def bank(b):
            return ps[:, b, :]

        seeded_events = [conv_act, conv_dve, ffn_act, ffn_dve, sh_pe, sh_act, sh_dve, at_pe, at_act, at_dve, mg_dve]
        seeded_events += [g_pe, g_act, g_dve, b_pe, b_act, b_dve]
        block = ctx.enter_context(nc.Block())

        @block.sync
        def _(sp):
            def std(ph, w, col):
                with sp.Fori(0, PLAN[ph].quads) as i:
                    for j in range(4):
                        sp.wait_ge(lo_ready, 4 * i + (4 * PLAN[ph].first + j + 1))
                        src = w[256 * j:256 * (j + 1), bass.ds(256 * i + col, 256)]
                        sp.dma_start(raw[:, j, :].rearrange("p (a c) -> p a c", a=2),
                                     src.rearrange("(a p) c -> p a c", p=P)).then_inc(raw_landed[j], 16)

            def half(ph, w):
                with sp.Fori(0, PLAN[ph].quads) as i:
                    for j in range(4):
                        sp.wait_ge(lo_ready, 4 * i + (4 * PLAN[ph].first + j + 1))
                        r = 256 * (j % 2)
                        src = w[r:r + 256, bass.ds(512 * i + 256 * (j // 2), 256)]
                        sp.dma_start(raw[:, j, :].rearrange("p (a c) -> p a c", a=2),
                                     src.rearrange("(a p) c -> p a c", p=P)).then_inc(raw_landed[j], 16)

            def down(ph, w):
                with sp.Fori(0, PLAN[ph].quads) as i:
                    for j in range(4):
                        sp.wait_ge(lo_ready, 4 * i + (4 * PLAN[ph].first + j + 1))
                        src = w[bass.ds(256 * i + P * (j // 2), P), 512 * (j % 2):512 * (j % 2) + 512]
                        sp.dma_start(raw[:, j, :], src).then_inc(raw_landed[j], 16)

            def up(ph, w):
                with sp.Fori(0, PLAN[ph].quads // 2) as i:
                    for g in range(2):
                        for j in range(4):
                            sp.wait_ge(lo_ready, 8 * i + (4 * (PLAN[ph].first + g) + j + 1))
                            src = w[256 * j:256 * (j + 1), bass.ds(256 * i + FFN * g, 256)]
                            sp.dma_start(raw[:, j, :].rearrange("p (a c) -> p a c", a=2),
                                         src.rearrange("(a p) c -> p a c", p=P)).then_inc(raw_landed[j], 16)

            sp.wait_ge(seeded, 1)
            for n in range(NT):
                sp.dma_start(x_in[:, n, :], x[0, n * P:(n + 1) * P, :]).then_inc(x_landed, 16)
            w = w_in[0]
            std("xbc", w, C_XBC)
            std("z", w, C_Z)
            std("pool", w, C_POOL)
            std("qk", w, C_Q)
            std("v", w, C_V)
            std("gate0", w, C_GATE)
            half("proj_pool", p_pool[0])
            std("gate1", w, C_GATE + D)
            half("proj_attn", p_attn[0])
            std("gate2", w, C_GATE + 2 * D)
            std("proj_ssd", p_ssd[0], 0)
            std("w_out", w_out[0], 0)
            up("up0", ffn_up[0])
            down("down0", ffn_down[0])
            std("a_qkv", a_w_in_2[0], 0)
            std("a_gate", a_w_in_2[0], A_QKV)
            std("a_out", a_w_out_2[0], 0)
            up("up1", f_w_up_2[0])
            down("down1", f_w_down_2[0])
            std("kv_k", kv_w_2, 0)
            std("kv_v", kv_w_2, 256)
            std("q2", b_w_q_2[0], 0)
            std("o2", b_w_o_2[0], 0)
            up("up2", f_w_up_2[1])
            down("down2", f_w_down_2[1])
            sp.wait_ge(fin_dve.sem, fin_dve.value("c3"))
            sp.dma_start(out[0].rearrange("(n p) c -> p n c", p=P), x_in[:]).then_inc(stored, 16)
            sp.wait_ge(stored, 16)

        @block.gpsimd
        def _(pool):
            for at_, (s, n) in enumerate(((lo_ready, 4), (pe_used, 4), (lin_free[0], 2), (lin_free[1], 2),
                         *((e.sem, e.seed) for e in seeded_events))):
                pool.memset(seed[:, at_:at_ + 1], 0.0).then_inc(s, n)
            pool.memset(seed[:, 62:63], 0.0).then_inc(seeded, 1)

            def chosen(t, pattern, base, mult, op, fill, source=None):
                pool.affine_select(out=t, in_=t if source is None else source, pattern=pattern, base=base,
                                   channel_multiplier=mult, compare_op=op, fill=fill).then_inc(made, 1)

            made_n = 0
            pool.memset(ident[:], 0.0).then_inc(made, 1)
            pool.memset(ident_bf[:], 0.0).then_inc(made, 1)
            pool.memset(mask_q[:], 0.0).then_inc(made, 1)
            pool.memset(upto[:], 1.0).then_inc(made, 1)
            pool.memset(last_row[:], 1.0).then_inc(made, 1)
            pool.memset(ones[:], 1.0).then_inc(made, 1)
            pool.memset(keep[:], 1.0).then_inc(made, 1)
            pool.memset(sgn[:], 1.0).then_inc(made, 1)
            pool.memset(raw_bias[:], 0.0).then_inc(made, 1)
            pool.memset(a_log[:], 0.0).then_inc(made, 1)
            pool.memset(par_in[:], 0.0).then_inc(made, 1)
            pool.memset(ws[:], 0.0).then_inc(made, 1)
            pool.wait_ge(made, 12)
            chosen(ident[:], [[-1, P]], 0, 1, ALU.not_equal, 1.0)
            chosen(ident_bf[:], [[-1, P]], 0, 1, ALU.not_equal, 1.0)
            chosen(mask_q[:], [[-1, P]], 0, 1, ALU.is_ge, MASKED)
            chosen(upto[:], [[1, P]], 0, -1, ALU.is_ge, 0.0)
            chosen(last_row[:], [[0, P]], 1 - P, 1, ALU.is_ge, 0.0)
            pool.wait_ge(made, 12 + 5)
            pool.memset(keep[32:48, 0:S:P], 0.0).then_inc(made, 1)
            pool.wait_ge(made, 12 + 6)
            pool.memset(sgn[0:8, :], -1.0).then_inc(made, 1)
            pool.wait_ge(made, 12 + 7)
            for j in range(16):
                pool.memset(inv_count[:, j:j + 1], 1.0 / (j + 1)).then_inc(made, 1)
            pool.wait_ge(made, 12 + 7 + 16)
            pool.memset(seed[:, 63:64], 0.0).then_inc(consts_ready, 1)

            pool.memset(level[:], 0.0).then_inc(made, 1)
            pool.iota(dist[:], pattern=[[-1, 2 * P]], base=P, channel_multiplier=1,
                      allow_small_or_imprecise_dtypes=True).then_inc(made, 1)
            pool.memset(far[:], 0.0).then_inc(made, 1)
            pool.wait_ge(made, 35 + 3)
            for k in range(7):
                b = 1 << k
                part = level[:, k, :].rearrange("p (n two b) -> p n two b", two=2, b=b)[:, :, 1, :]
                pool.memset(part, -1.0).then_inc(made, 1)
                pool.wait_ge(made, 35 + 4 + 3 * k)
                chosen(part, [[-2 * b, P // (2 * b)], [0, b]], 0, 1, ALU.is_ge, 0.0)
                pool.wait_ge(made, 35 + 5 + 3 * k)
                chosen(part, [[2 * b, P // (2 * b)], [0, b]], b - 1, -1, ALU.is_ge, 0.0)
                pool.wait_ge(made, 35 + 6 + 3 * k)
            chosen(far[:], [[-1, 2 * P]], P, 1, ALU.is_ge, MASKED)
            pool.wait_ge(made, 35 + 25)
            chosen(far[:], [[1, 2 * P]], -1, -1, ALU.is_ge, MASKED)
            pool.wait_ge(made, 35 + 26)
            for n in range(SWA_HEADS):
                pool.memset(minus_slope[:, n:n + 1], -2.0 ** (-8.0 * (n + 1) / SWA_HEADS)).then_inc(made, 1)
            pool.wait_ge(made, 35 + 26 + 16)
            pool.memset(seed[:, 61:62], 0.0).then_inc(later_ready, 1)

            with pool.Fori(0, QUADS) as q:
                for j in range(4):
                    pool.wait_ge(hi_ready, 4 * q + (j + 1))
                    pool.wait_ge(pe_used, 4 * q + (j + 1))
                    pool.tensor_tensor(wlo[:, j, :], raw[:, j, :], whi[:, j, :].bitcast(F32),
                                       ALU.subtract).then_inc(lo_ready, 1)

        def step_back(events, name, u, back, turn):
            if u >= back:
                w = u - back
                return events.value(f"{w // 4}{name}{w % 4}", turn)
            w = u - back + 8
            return events.value(f"{w // 4}{name}{w % 4}", turn - 1)

        @block.scalar
        def _(act):
            def split(i, off):
                for j in range(4):
                    act.wait_ge(raw_landed[j], 32 * i + 16 * (off + 1))
                    act.wait_ge(pe_used, 8 * i + (4 * off + j + 1))
                    act.activation(whi[:, j, :], raw[:, j, :], ACT.Copy).then_inc(hi_ready, 1)

            def split1(i, off):
                for j in range(4):
                    act.wait_ge(raw_landed[j], 16 * i + 16 * (off + 1))
                    act.wait_ge(pe_used, 4 * i + (4 * off + j + 1))
                    act.activation(whi[:, j, :], raw[:, j, :], ACT.Copy).then_inc(hi_ready, 1)

            def used(i, off):
                act.wait_ge(pe_used, 8 * i + (4 * off + 8))

            def norm(n, update):
                for k in k8:
                    h_wait(act, update, k)
                    if k >= 2:
                        act.wait_ge(norm_pe.sem, norm_pe.value(f"sum{k - 2}", n))
                    act.activation(sq[:, k % 2, :], h[:, k, :], ACT.Square).then_inc(norm_act.sem, norm_act.mark(f"sq{k}"))
                act.wait_ge(norm_dve.sem, norm_dve.value("rc", n))
                act.activation(rs[:], rc[:], ACT.Sqrt).then_inc(norm_act.sem, norm_act.mark("rs"))

            def upper(m, dst):
                for k in k8:
                    act.wait_ge(u_dve.sem, u_dve.value(f"u{k}", m))
                    act.activation(dst[:, k, :], uf[:, k % 2, :], ACT.Copy).then_inc(u_act.sem, u_act.mark(f"uh{k}"))

            def scalars(n):
                act.wait_ge(sc_dve.sem, sc_dve.value("abs", n))
                act.activation(sc[:, 2, :], sc[:, 1, :], ACT.Exp, scale=-1.0).then_inc(sc_act.sem, sc_act.mark("exp"))
                act.wait_ge(sc_dve.sem, sc_dve.value("one", n))
                act.activation(sc[:, 5, :], sc[:, 3, :], ACT.Ln).then_inc(sc_act.sem, sc_act.mark("ln"))

            def scalar_decays(n):
                act.wait_ge(sc_dve.sem, sc_dve.value("end", n))
                act.activation(decay_end[:], decay_end[:], ACT.Exp).then_inc(sc_act.sem, sc_act.mark("decay"))
                act.activation(chunk_decay[:].rearrange("p a b -> p (a b)"), ps[:, 6, 0:192],
                               ACT.Exp).then_inc(sc_act.sem, sc_act.mark("chunk"))

            def conv(ph, w_name, tap, b_name, silu_only_first, dst, turn0, buf):
                with act.Fori(0, PLAN[ph].quads // 2) as i:
                    for g in range(2):
                        split(i, PLAN[ph].first + g + 1)
                        used(i, PLAN[ph].first + g)
                        for c in range(2):
                            t = 4 * i + 2 * g + c
                            bias = column(b_name, t) if b_name else 0.0
                            act.activation(buf[:, 2 * g + c, :], bank(2 * g + c), ACT.Identity, bias=bias,
                                           scale=column(w_name, t + tap)).then_inc(conv_act.sem, conv_act.mark(f"t{2 * g + c}"))
                        for c in range(2):
                            t = 4 * i + 2 * g + c
                            act.wait_ge(lin_free[g], std_value(ph, g, i, c))
                            act.activation(dst[:, bass.ds(t, 1), :], buf[:, 2 * g + c, :].unsqueeze(1), ACT.Silu)\
                               .then_inc(conv_act.sem, conv_act.mark(f"s{2 * g + c}"))

            def out_of_banks(ph, put):
                with act.Fori(0, PLAN[ph].quads // 2) as i:
                    for g in range(2):
                        split(i, PLAN[ph].first + g + 1)
                        used(i, PLAN[ph].first + g)
                        put(ps[:, 2 * g:2 * g + 2, :], 2 * i + g).then_inc(lin_free[g], 2)

            def splits_only(ph, last=False):
                with act.Fori(0, PLAN[ph].quads - last) as i:
                    split1(i, PLAN[ph].first + 1)

            act.wait_ge(consts_ready, 1)
            for n, rows in enumerate(ROWS):
                r0 = 0
                for name, src, count in rows:
                    act.dma_start(par_in[r0:r0 + count, n, :], as_rows(src)).then_inc(par_landed, 16)
                    r0 += count
            fw, dw = w_in[0][:, C_F:C_F + 8], w_in[0][:, C_DT:C_DT + SSD_HEADS]
            act.dma_start(ws[:, :, 0:8], fw.rearrange("(k p) c -> p k c", p=P)).then_inc(small_landed, 16)
            act.dma_start(ws[:, :, 32:48], dw.rearrange("(k p) c -> p k c", p=P)).then_inc(small_landed, 16)
            act.dma_start(raw_bias[0:8, 0:1], f_bias.rearrange("a p -> p a")).then_inc(small_landed, 16)
            act.dma_start(raw_bias[32:48, 0:1], ssd_dt_bias.rearrange("a p -> p a")).then_inc(small_landed, 16)
            act.dma_start(raw_bias[32:40, 1:2], a_dt_bias_2.rearrange("a p -> p a")).then_inc(small_landed, 16)
            act.dma_start(a_log[32:48, 0:1], ssd_a_log.rearrange("a p -> p a")).then_inc(small_landed, 16)
            act.dma_start(a_log[32:40, 1:2], a_A_log_2.rearrange("a p -> p a")).then_inc(small_landed, 16)
            for e in range(2):
                act.dma_start(d_skip[64 * e:64 * e + 64, :], ssd_d[0, e:SSD_HEADS:2].partition_broadcast(64),
                              allow_slow_non_contiguous=True).then_inc(small_landed, 16)
            act.dma_start(sinks[:], b_sinks_2[0].partition_broadcast(P)).then_inc(sinks_landed, 16)
            act.wait_ge(small_landed, 16 * 9)
            act.activation(row_scale[:], a_log[:], ACT.Exp).then_inc(prep_act.sem, prep_act.mark("a_exp"))
            split(0, 0)

            norm(0, 0)
            upper(0, uh)
            scalars(0)
            conv("xbc", "ssd_conv_w", 3 * XT, "ssd_conv_b", None, xc, 0, cv)
            scalar_decays(0)
            out_of_banks("z", lambda src, q: act.activation(zs[:, bass.ds(2 * q, 2), :], src, ACT.Silu))
            for grp in range(SSD_GROUPS):
                with act.Fori(0, 4) as i:
                    turn = i + 4 * grp
                    for e in range(2):
                        act.wait_ge(sh_dve.sem, sh_dve.value(f"d{e}", turn))
                        act.activation(dd[:, e, :], dd[:, e, :], ACT.Exp).then_inc(sh_act.sem, sh_act.mark(f"e{e}"))
                        act.wait_ge(sh_pe.sem, sh_pe.value(f"row{e}", turn))
                        act.wait_ge(sh_dve.sem, sh_dve.value(f"c{e}", turn - 1))
                        act.activation(ec[:, e, :], bank(4 + e), ACT.Exp).then_inc(sh_act.sem, sh_act.mark(f"r{e}"))
                    for e in range(2):
                        act.wait_ge(sh_pe.sem, sh_pe.value(f"y{e}", turn))
                        act.activation(y_tok[:, :, bass.ds(128 * i + (512 * grp + 64 * e), HD)],
                                       ps[:, 6 + e, 0:256].rearrange("p (n d) -> p n d", n=NT),
                                       ACT.Copy).then_inc(sh_act.sem, sh_act.mark(f"y{e}"))
            for k in k8:
                act.wait_ge(sy_dve.sem, sy_dve.value(f"g{k}"))
                if k >= 2:
                    act.wait_ge(sy_pe.sem, sy_pe.value(f"sum{k - 2}"))
                act.activation(ysq[:, k % 2, :], zs[:, k, :], ACT.Square).then_inc(sy_act.sem, sy_act.mark(f"sq{k}"))
            for g in range(2):
                act.wait_ge(sy_dve.sem, sy_dve.value(f"rc{g}"))
                act.activation(yms[:, g, :], yrs[:, g, :], ACT.Sqrt).then_inc(sy_act.sem, sy_act.mark(f"rs{g}"))
            for k in k8:
                act.wait_ge(sy_dve.sem, sy_dve.value(f"f{k}"))
                act.activation(ysh[:, k, :], yf[:, k % 2, :], ACT.Copy).then_inc(sy_act.sem, sy_act.mark(f"h{k}"))
            act.wait_ge(sy_dve.sem, sy_dve.value("w7"))
            act.dma_start(mix[:], pool_mix[0].rearrange("g c d -> c g d")).then_inc(mix_landed, 16)
            out_of_banks("pool", lambda src, q: act.activation(pv[:, bass.ds(2 * q, 2), PADV:PADV + S], src, ACT.Copy))
            act.wait_ge(sy_dve.sem, sy_dve.value("l7"))
            out_of_banks("qk", lambda src, q: act.activation(qk[:, bass.ds(2 * q, 2), :], src, ACT.Copy))
            out_of_banks("v", lambda src, q: act.activation(
                v[:, :, bass.ds(256 * q, 256)],
                src.rearrange("p a (b c) -> p (a b) c", b=2), ACT.Copy))
            for g in range(4):
                act.wait_ge(po_pe.sem, po_pe.value(f"y{g}"))
                act.activation(yph[:, g, :], bank(4 + g), ACT.Copy, scale=column("pool_scale", g))\
                   .then_inc(po_act.sem, po_act.mark(f"h{g}"))
            act.wait_ge(po_dve.sem, po_dve.value("l3"))
            with act.Fori(0, 4) as i:
                act.wait_ge(at_pe.sem, at_pe.value("1s3", i - 1))
                act.activation(qs[:], qk[:, bass.ds(i, 1), :].rearrange("p a b -> p (a b)"), ACT.Copy, scale=HD ** -0.5)\
                   .then_inc(at_act.sem, at_act.mark("qs"))
                act.activation(ks[:], qk[:, bass.ds(i + 4, 1), :].rearrange("p a b -> p (a b)"), ACT.Copy)\
                   .then_inc(at_act.sem, at_act.mark("ks"))
                for e in range(2):
                    for ev in AT_ACT:
                        n, u = int(ev[1]), 4 * e + int(ev[1])
                        L = P * (n + 1)
                        if ev[0] == "p":
                            act.wait_ge(at_dve.sem, at_dve.value(f"{e}m{n}", i))
                            act.wait_ge(at_pe.sem, step_back(at_pe, "t", u, 2, i))
                            act.activation(pe_[:, u % 2, 0:L], sm[:, u % 2, 0:L], ACT.Exp, bias=stat[:, 8 + u:9 + u],
                                           accum_out=stat[:, 16 + u:17 + u]).then_inc(at_act.sem, at_act.mark(f"{e}{ev}"))
                        else:
                            act.wait_ge(at_pe.sem, at_pe.value(f"{e}t{n}", i))
                            act.wait_ge(at_pe.sem, step_back(at_pe, "o", u, 2, i))
                            act.activation(pt[:, u % 2, 0:L], ps[:, 6, 0:L], ACT.Copy)\
                               .then_inc(at_act.sem, at_act.mark(f"{e}{ev}"))
            for k in range(4):
                act.wait_ge(ay_pe.sem, ay_pe.value(f"t{k}"))
                act.activation(yah[:, k, :], bank(4 + k), ACT.Copy).then_inc(ay_act.sem, ay_act.mark(f"h{k}"))
            for b, proj in enumerate(("proj_pool", "proj_attn", "proj_ssd")):
                out_of_banks(f"gate{b}", lambda src, q: act.activation(gt[:, bass.ds(2 * q, 2), :], src, ACT.Sigmoid))
                if b < 2:
                    splits_only(proj)
                    for p in range(2):
                        act.wait_ge(lin_free[p], 2 + 2 * PLAN[f"gate{b + 1}"].fills[p])
                else:
                    with act.Fori(0, 2) as i:
                        for g in range(2):
                            split(i, PLAN[proj].first + g + 1)
                            for c in range(2):
                                act.wait_ge(mg_dve.sem, mg_dve.value(f"m{2 * g + c}", i + 2))
                                t = 4 * i + 2 * g + c
                                act.activation(uh[:, bass.ds(t, 1), :], mg[:, bass.ds(t, 1), :], ACT.Copy)\
                                   .then_inc(mg_act.sem, 1)
            splits_only("w_out")

            def ffn(f):
                up, first = f"up{f}", PLAN[f"up{f}"].first
                with act.Fori(0, FT // 2) as i:
                    turn = i + (FT // 2) * f
                    for g in range(2):
                        split(i, first + g + 1)
                        used(i, first + g)
                        for c in range(2):
                            t = 2 * i + (FT * g + c)
                            if g:
                                act.wait_ge(ffn_dve.sem, ffn_dve.value(f"hf{c}", turn - 1))
                            act.activation(fc[:, 2 * g + c, :], bank(2 * g + c), ACT.Identity, bias=column(f"f{f}c", t),
                                           scale=column(f"f{f}b", t)).then_inc(ffn_act.sem, ffn_act.mark(f"t{2 * g + c}"))
                        if g == 0:
                            for c in range(2):
                                act.wait_ge(lin_free[0], std_value(up, 0, i, c))
                                act.wait_ge(ffn_dve.sem, ffn_dve.value(f"hf{c}", turn - 1))
                                act.activation(fg[:, c, :], fc[:, c, :], ACT.Silu).then_inc(ffn_act.sem, ffn_act.mark(f"s{c}"))
                    for c in range(2):
                        act.wait_ge(ffn_dve.sem, ffn_dve.value(f"hf{c}", turn))
                        act.activation(fh[:, bass.ds(2 * i + c, 1), :], ff[:, c, :].unsqueeze(1), ACT.Copy)\
                           .then_inc(ffn_act.sem, ffn_act.mark(f"fh{c}"))
                splits_only(f"down{f}", f == 2)

            norm(1, 1)
            upper(1, uh)
            ffn(0)
            norm(2, 2)

            norm(3, 3)
            act.wait_ge(prep_dve2.sem, prep_dve2.value("zero"))
            aw = a_w_in_2[0]
            for n, col in ((0, A_QKV + A_V), (32, A_QKV + A_V + DN_HEADS)):
                act.dma_start(ws[:, :, n:n + 8], aw[:, col:col + 8].rearrange("(k p) c -> p k c", p=P))\
                   .then_inc(small_landed, 16)
            upper(2, uh)
            scalars(1)
            conv("a_qkv", "a_conv_w", 72, None, None, ac, 3, acv)
            scalar_decays(1)
            out_of_banks("a_gate", lambda src, q: act.activation(ga[:, bass.ds(2 * q, 2), :], src, ACT.Silu))

            def gmark(name):
                return gn_act.sem, gn_act.mark(name)

            def after(events, name, turn=0):
                act.wait_ge(events.sem, events.value(name, turn))

            act.wait_ge(pe_used, 4 * PLAN["a_out"].first + 4)
            act.activation(beta[:], tok[:, 1, :, 0:8], ACT.Exp).then_inc(*gmark("beta"))
            act.activation(egc[:], tok[:, 0, :, 32:40], ACT.Exp).then_inc(*gmark("egc"))
            for t in range(16):
                if t >= 2:
                    after(gn_pe, f"n{t - 2}")
                act.activation(asq[:, t % 2, :], ac[:, t, :], ACT.Square).then_inc(*gmark(f"sq{t}"))
            after(gn_dve, "nr")
            act.activation(rn2[:], rn[:], ACT.Sqrt).then_inc(*gmark("rt"))

            with act.Fori(0, DN_HEADS // 2) as i:
                for step in GA:
                    for e in range(2):
                        if step[:2] == "st":
                            n = {"k": 8, "v": 16, "q": 0}[step[2]]
                            dst = {"k": kf, "v": vf, "q": qf}[step[2]][e]
                            after(g_pe, f"{e}o3", i - 1)
                            last = act.activation(dst[:], ac[:, bass.ds(2 * i + (n + e), 1), :].rearrange("p a b -> p (a b)"),
                                                  ACT.Copy)
                        elif step == "eg":
                            after(g_pe, f"{e}row", i)
                            last = act.activation(eg[e][:], bank(4 * e + 3), ACT.Exp)
                        elif step == "em":
                            after(g_dve, f"{e}d", i)
                            last = act.activation(em[e][:], em[e][:], ACT.Exp)
                        elif step in ("kt", "kbt", "qt"):
                            dst, b = {"kt": (kt, 0), "kbt": (kbt, 1), "qt": (qt, 2)}[step]
                            after(g_pe, f"{e}turned", i)
                            last = act.activation(dst[e][:], bank(4 * e + b), ACT.Copy)
                        elif step[:2] == "ti":
                            after(g_pe, f"{e}t{step[2]}", i)
                            last = act.activation(ti[e][:], bank(4 * e + 2), ACT.Copy)
                        elif step == "nkc":
                            after(g_pe, f"{e}nk", i)
                            last = act.activation(nkc[e][:], bank(4 * e + 3), ACT.Copy, scale=-1.0)
                        else:
                            c = int(step[2])
                            after(g_pe, f"{e}v{c}", i)
                            last = act.activation(vn[e][:, c * P:(c + 1) * P], ps[:, 4 * e, c * P:(c + 1) * P], ACT.Copy)
                        last.then_inc(g_act.sem, g_act.mark(f"{e}{step}"))
            after(g_dve, "1ot", 3)
            for n in ch:
                if n >= 2:
                    after(gn_dve, f"red{n - 2}")
                act.activation(osq[:, n % 2, :], ot[:, n, :], ACT.Square).then_inc(*gmark(f"q{n}"))
            after(gn_dve, "orc")
            act.activation(oss2[:], oss[:], ACT.Sqrt).then_inc(*gmark("or"))
            for k in k8:
                after(gn_dve, f"f{k}")
                act.activation(ayh[:, k, :], ayf[:, k % 2, :], ACT.Copy).then_inc(*gmark(f"h{k}"))
            splits_only("a_out")
            norm(4, 4)
            upper(3, uh)
            ffn(1)

            norm(5, 5)
            act.dma_start(vbias[:], kv_b_2[256:512].partition_broadcast(P)).then_inc(vbias_landed, 16)
            upper(4, uh)
            upper(5, ubh)
            split1(0, PLAN["kv_k"].first + 1)
            split1(0, PLAN["kv_v"].first + 1)
            splits_only("q2")
            for p in range(2):
                act.wait_ge(lin_free[p], std_value("q2", p, 1))
            after(kv_dve, "k7")
            with act.Fori(0, KV_HEADS) as i:
                for step in BA:
                    if step == "st":
                        after(b_pe, "s3", i - 1)
                        act.activation(qst[:], q2[:, bass.ds(2 * i, 2), :], ACT.Copy)
                        last = act.activation(kst[:], kk[:, bass.ds(i, 1), :].rearrange("p a b -> p (a b)"), ACT.Copy)
                    elif step[0] == "p":
                        u = int(step[1])
                        after(b_dve, f"ng{u}", i)
                        if u >= 2:
                            after(b_pe, f"t{u - 2}", i)
                        else:
                            after(b_pe, f"t{u + 2}", i - 1)
                        for n in range(NT):
                            lo = P if n == 0 else 0
                            act.activation(pr2[:, u % 2, n, lo:], sm2[:, u % 2, n, lo:], ACT.Exp, bias=st2[:, 8 * u + n:8 * u + n + 1],
                                           accum_out=st2[:, 8 * u + 4 + n:8 * u + 5 + n])
                        last = act.activation(st2[:, 32 + 4 * u:36 + 4 * u], st2[:, 8 * u:8 * u + 4], ACT.Exp,
                                              bias=sinks[:, bass.ds(4 * i + u, 1)])
                    else:
                        u = int(step[1])
                        after(b_pe, f"t{u}", i)
                        if u:
                            after(b_pe, f"o{u - 1}", i)
                        else:
                            after(b_pe, "o3", i - 1)
                        last = act.activation(pt2[:].rearrange("p a b -> p (a b)"), ps[:, 4:6, :].rearrange("p a b -> p (a b)")[:, 0:7 * P],
                                              ACT.Copy)
                    last.then_inc(b_act.sem, b_act.mark(step))
            for k in k8:
                after(bo_pe, f"t{k}")
                act.activation(uh[:, k, :], bank(4 + k % 4), ACT.Copy).then_inc(bo_act.sem, bo_act.mark(f"h{k}"))
            splits_only("o2")
            norm(6, 6)
            upper(6, uh)
            ffn(2)
            norm(7, 7)

        @block.tensor
        def _(pe):
            def three(o, j, col, width, moving, k, start, stop, hi_moving=True):
                mh, ml = moving
                a = whi[:, j, col:col + width]
                pe.matmul(o, a, mh[:, k, :], start=start, stop=False, skip_group_check=True)
                pe.matmul(o, a, ml[:, k, :], start=False, stop=False, skip_group_check=True)
                return pe.matmul(o, wlo[:, j, col:col + width], mh[:, k, :], start=False, stop=stop,
                                 skip_group_check=True)

            def quad(ph, i, g, pair, turn, moving, ready=None):
                pe.wait_ge(lin_free[pair], 2 * turn + (2 * PLAN[ph].fills[pair] + 2))
                for j in range(4):
                    pe.wait_ge(lo_ready, 8 * i + (4 * (PLAN[ph].first + g) + j + 5))
                    for a in range(2):
                        k = 2 * j + a
                        if ready is not None:
                            pe.wait_ge(ready[0].sem, ready[0].value(f"{ready[1]}{k}", ready[2]))
                        for c in range(2):
                            last = three(bank(2 * pair + c), j, 256 * a + 128 * c, P, moving, k, k == 0, k == KT - 1)
                    last.then_inc(pe_used, 1)

            def quad_tok(ph, i, g, pair, turn, moving):
                pe.wait_ge(lin_free[pair], 2 * turn + (2 * PLAN[ph].fills[pair] + 2))
                for j in range(4):
                    pe.wait_ge(lo_ready, 8 * i + (4 * (PLAN[ph].first + g) + j + 5))
                    for a in range(2):
                        k = 2 * j + a
                        for n in range(NT):
                            o = ps[:, 2 * pair + n // 2, 256 * (n % 2):256 * (n % 2) + 256]
                            for w, m, first in ((whi, moving[0], True), (whi, moving[1], False), (wlo, moving[0], False)):
                                last = pe.matmul(o, m[:, k, n * P:(n + 1) * P], w[:, j, 256 * a:256 * a + 256],
                                                 start=first and k == 0 and n % 2 == 0, stop=k == KT - 1,
                                                 skip_group_check=True)
                    last.then_inc(pe_used, 1)

            def std(ph, moving, ready=None):
                with pe.Fori(0, PLAN[ph].quads // 2) as i:
                    for g in range(2):
                        quad(ph, i, g, g, i, moving, ready if g == 0 else None)

            def half(ph, moving):
                with pe.Fori(0, PLAN[ph].quads) as i:
                    for j in range(4):
                        pair = j // 2
                        if j % 2 == 0:
                            pe.wait_ge(lin_free[pair], 2 * i + (2 * PLAN[ph].fills[pair] + 2))
                        pe.wait_ge(lo_ready, 4 * i + (4 * PLAN[ph].first + j + 5))
                        for a in range(2):
                            k = 2 * (j % 2) + a
                            for c in range(2):
                                last = three(bank(2 * pair + c), j, 256 * a + 128 * c, P, moving, k, k == 0, k == 3)
                        last.then_inc(pe_used, 1)

            def sum_squares(n):
                for k in k8:
                    pe.wait_ge(norm_act.sem, norm_act.value(f"sq{k}", n))
                    pe.matmul(bank(4), ones[:], sq[:, k % 2, :], start=k == 0, stop=k == KT - 1)\
                        .then_inc(norm_pe.sem, norm_pe.mark(f"sum{k}"))

            def small(n, m):
                if n == 0:
                    pe.wait_ge(prep_dve.sem, prep_dve.value("wsl"))
                else:
                    pe.wait_ge(prep_dve2.sem, prep_dve2.value("wsl"))
                for k in k8:
                    pe.wait_ge(u_dve.sem, u_dve.value(f"ul{k}", m))
                    pe.matmul(ps[0:48, 5, :], wsh[:, k, :], uh[:, k, :], start=k == 0, stop=False)
                    pe.matmul(ps[0:48, 5, :], wsh[:, k, :], ul[:, k, :], start=False, stop=False)
                    last = pe.matmul(ps[0:48, 5, :], wsl[:, k, :], uh[:, k, :], start=False, stop=k == KT - 1)
                last.then_inc(sc_pe.sem, sc_pe.mark("logits"))

            def turn_scalars(n):
                pe.wait_ge(sc_dve.sem, sc_dve.value("sums", n))
                for w, src in enumerate((cs[:], sc[:, 9, :])):
                    for c in ch:
                        last = pe.transpose(ps[:, 5, 192 * w + 48 * c:192 * w + 48 * c + 48], src[:, c * P:(c + 1) * P],
                                            ident[0:48, 0:48])
                last.then_inc(sc_pe.sem, sc_pe.mark("turned"))
                pe.wait_ge(sc_dve.sem, sc_dve.value("tok", n))
                pe.matmul(ps[:, 6, 0:192], last_row[:], tok[:, 0, :, :].rearrange("p a b -> p (a b)"), start=True,
                          stop=True).then_inc(sc_pe.sem, sc_pe.mark("last"))

            pe.wait_ge(consts_ready, 1)
            pe.wait_ge(par_landed, 16 * sum(len(r) for r in ROWS))
            for b in range(3):
                for n in range(4 * b, min(4 * b + 4, 9)):
                    last = pe.transpose(ps[:, 5 + b, 128 * (n % 4):128 * (n % 4) + 128], par_in[:, n, :], ident[:])
                last.then_inc(x_pe.sem, x_pe.mark(f"par{b}"))
            pe.wait_ge(x_landed, 16 * NT)
            for k in k8:
                if k >= 4:
                    pe.wait_ge(x_ready, k - 3)
                for n in ch:
                    last = pe.transpose(ps[:, k % 4, n * P:(n + 1) * P], x_in[:, n, k * P:(k + 1) * P], ident[:])
                last.then_inc(x_pe.sem, x_pe.mark(f"x{k}"))

            sum_squares(0)
            small(0, 0)
            std("xbc", (uh, ul))
            turn_scalars(0)
            pe.wait_ge(conv_act.sem, conv_act.value("s3", 2))
            pe.wait_ge(sc_act.sem, sc_act.value("chunk", 0))
            for g in range(SSD_GROUPS):
                for c in ch:
                    last = pe.matmul(ps[:, 4 + g, c * P:(c + 1) * P], xc[:, 8 + g, c * P:(c + 1) * P],
                                     xc[:, 10 + g, c * P:(c + 1) * P], start=True, stop=True)
                last.then_inc(ssd_pe.sem, ssd_pe.mark(f"cb{g}"))
            for c in ch:
                pe.wait_ge(ssd_dve.sem, ssd_dve.value("cb1" if c == 0 else f"xd{c - 1}"))
                for k in k8:
                    last = pe.transpose(ps[:, 4 + k // 4, P * (k % 4):P * (k % 4) + P], xc[:, k, c * P:(c + 1) * P], ident[:])
                last.then_inc(ssd_pe.sem, ssd_pe.mark(f"x{c}"))
                if c == 3:
                    break
                if c:
                    pe.wait_ge(ssd_dve.sem, ssd_dve.value(f"st{c - 1}"))
                for g in range(2):
                    last = pe.transpose(ps[:, 6, P * g:P * g + P], xc[:, 8 + g, c * P:(c + 1) * P], ident[:])
                last.then_inc(ssd_pe.sem, ssd_pe.mark(f"b{c}"))
                pe.wait_ge(ssd_dve.sem, ssd_dve.value(f"xdd{c}"))
                for g in range(2):
                    pe.matmul(bank(6 + g), bt[:, P * g:P * g + P], xdd[:, 512 * g:512 * g + 512], start=True, stop=True)\
                        .then_inc(ssd_pe.sem, ssd_pe.mark(f"state{c}_{g}"))
            std("z", (uh, ul))
            pe.wait_ge(ssd_dve.sem, ssd_dve.value("xd3"))
            for grp in range(SSD_GROUPS):
                with pe.Fori(0, 4) as i:
                    turn = i + 4 * grp
                    for e in range(2):
                        pe.wait_ge(sh_dve.sem, sh_dve.value(f"oh{e}", turn))
                        pe.wait_ge(sh_act.sem, sh_act.value(f"r{e}", turn - 1))
                        pe.matmul(bank(4 + e), ones[0:48, :], oh[:, e, :], start=True, stop=True)\
                            .then_inc(sh_pe.sem, sh_pe.mark(f"row{e}"))
                    for e in range(2):
                        pe.wait_ge(sh_dve.sem, sh_dve.value(f"c{e}", turn))
                        pe.wait_ge(sh_act.sem, sh_act.value(f"y{e}", turn - 1))
                        head = bass.ds(128 * i + (512 * grp + 64 * e), HD)
                        for c in ch:
                            o = ps[:, 6 + e, HD * c:HD * c + HD]
                            last = pe.matmul(o, mt[:, e, c * P:(c + 1) * P], xd[:, c, head], start=True, stop=c == 0)
                            if c:
                                last = pe.matmul(o, ce[:, e, c * P:(c + 1) * P], st[:, c - 1, head], start=False, stop=True)
                        last.then_inc(sh_pe.sem, sh_pe.mark(f"y{e}"))

            def y_turn(k):
                pe.wait_ge(*((sh_act.sem, sh_act.value("y1", 7)) if k < 2 else (sy_dve.sem, sy_dve.value(f"w{k - 2}"))))
                for n in ch:
                    last = pe.transpose(ps[:, 4 + k % 2, n * P:(n + 1) * P], y_tok[:, n, k * P:(k + 1) * P], ident[:])
                last.then_inc(sy_pe.sem, sy_pe.mark(f"t{k}"))

            y_turn(0)
            y_turn(1)
            for k in k8:
                if k < 6:
                    y_turn(k + 2)
                pe.wait_ge(sy_act.sem, sy_act.value(f"sq{k}"))
                pe.matmul(bank(6 + k // 4), ones[:], ysq[:, k % 2, :], start=k % 4 == 0, stop=k % 4 == 3)\
                    .then_inc(sy_pe.sem, sy_pe.mark(f"sum{k}"))
            std("pool", (uh, ul))
            std("qk", (uh, ul))
            with pe.Fori(0, 1) as i:
                for g in range(2):
                    quad_tok("v", i, g, g, i, (uh, ul))
            pe.wait_ge(mix_landed, 16)
            for g in range(4):
                pe.wait_ge(po_dve.sem, po_dve.value(f"e{g}"))
                if g >= 2:
                    pass
                pe.matmul(bank(4 + g), mix[:, g, :], dp[:, g, :], start=True, stop=True)\
                    .then_inc(po_pe.sem, po_pe.mark(f"y{g}"))
            pe.wait_ge(lin_free[1], std_value("v", 1, 0))
            pe.wait_ge(po_dve.sem, po_dve.value("l3"))
            with pe.Fori(0, 4) as i:
                for e in range(2):
                    for ev in AT_PE:
                        if ev == "bc":
                            pe.wait_ge(at_dve.sem, at_dve.value(f"{e}oh", i))
                            pe.wait_ge(at_act.sem, step_back(at_act, "c", 4 * e, 1, i))
                            last = pe.matmul(bank(6), ones[0:48, :], ohc[:], start=True, stop=True)
                            last.then_inc(at_pe.sem, at_pe.mark(f"{e}bc"))
                            continue
                        n, u = int(ev[1]), 4 * e + int(ev[1])
                        if ev[0] == "s":
                            pe.wait_ge(at_act.sem, at_act.value("ks", i))
                            pe.wait_ge(at_dve.sem, step_back(at_dve, "s", u, 2, i))
                            b = ps[:, 4 + u % 2, 0:P * (n + 1)]
                            r = slice(HD * e, HD * e + HD)
                            pe.matmul(b, qs[r, n * P:(n + 1) * P],
                                      ks[r, 0:P * (n + 1)],
                                      start=True, stop=False, skip_group_check=True)
                            last = pe.matmul(ps[:, 4 + u % 2, n * P:(n + 1) * P], ident_bf[:], mask_q[:],
                                             start=False, stop=True, skip_group_check=True)
                        elif ev[0] == "t":
                            pe.wait_ge(at_act.sem, at_act.value(f"{e}p{n}", i))
                            pe.wait_ge(at_act.sem, step_back(at_act, "c", u, 1, i))
                            pe.wait_ge(at_dve.sem, at_dve.value(f"{e}nb", i))
                            for j in range(n + 1):
                                last = pe.transpose(ps[:, 6, j * P:(j + 1) * P], pe_[:, u % 2, j * P:(j + 1) * P], ident[:])
                        else:
                            pe.wait_ge(at_act.sem, at_act.value(f"{e}c{n}", i))
                            pe.wait_ge(at_dve.sem, step_back(at_dve, "o", u, 1, i))
                            for j in range(n + 1):
                                last = pe.matmul(ps[:, 7, 64 * u:64 * u + 64], pt[:, u % 2, j * P:(j + 1) * P],
                                                 v[:, j, bass.ds(128 * i + 64 * e, HD)], start=j == 0, stop=j == n)
                        last.then_inc(at_pe.sem, at_pe.mark(f"{e}{ev}"))
            for k in range(4):
                pe.wait_ge(at_dve.sem, at_dve.value("1o3", 3))
                for n in ch:
                    last = pe.transpose(ps[:, 4 + k, n * P:(n + 1) * P], oa[:, n, k * P:(k + 1) * P], ident[:])
                last.then_inc(ay_pe.sem, ay_pe.mark(f"t{k}"))
            std("gate0", (uh, ul))
            half("proj_pool", (yph, ypl))
            std("gate1", (uh, ul))
            pe.wait_ge(ay_dve.sem, ay_dve.value("l3"))
            half("proj_attn", (yah, yal))
            std("gate2", (uh, ul))
            std("proj_ssd", (ysh, ysl))
            for k in k8:
                pass
            pe.wait_ge(mg_low.sem, 8)
            std("w_out", (uh, ul))

            def ffn(f, m):
                std(f"up{f}", (uh, ul), (u_dve, "ul", m))
                ph = PLAN[f"down{f}"]

                def down_quad(q, first, last):
                    pe.wait_ge(ffn_dve.sem, ffn_dve.value("fl1", q + 11 * f))
                    for j in range(4):
                        k, b = 2 * q + j // 2, 4 * (j % 2)
                        pe.wait_ge(lo_ready, 4 * q + (4 * ph.first + j + 5))
                        for c in range(4):
                            for w, x_ in ((whi, fh), (whi, fl), (wlo, fh)):
                                start = first and j < 2 and w is whi and x_ is fh
                                mm = pe.matmul(bank(b + c), w[:, j, c * P:c * P + P],
                                               x_[:, bass.ds(k, 1), :].rearrange("p a b -> p (a b)") if not isinstance(k, int) else x_[:, k, :],
                                               start=start, stop=last and j >= 2 and w is wlo, skip_group_check=True)
                        mm.then_inc(pe_used, 1)

                for p in range(2):
                    pe.wait_ge(lin_free[p], 2 * ph.fills[p] + 2)
                down_quad(0, True, False)
                with pe.Fori(0, 9) as i:
                    down_quad(i + 1, False, False)
                down_quad(10, False, True)
                pe.wait_ge(h_high, 4 * f + 1)

            sum_squares(1)
            ffn(0, 1)
            sum_squares(2)

            sum_squares(3)
            small(1, 2)
            std("a_qkv", (uh, ul))
            turn_scalars(1)
            std("a_gate", (uh, ul))

            def after(events, name, turn=0):
                pe.wait_ge(events.sem, events.value(name, turn))

            after(sc_act, "chunk", 1)
            for t in range(16):
                after(gn_act, f"sq{t}")
                for c in ch:
                    last = pe.matmul(ps[:, 4, 4 * t + c:4 * t + c + 1], asq[:, t % 2, c * P:(c + 1) * P], ones[:, 0:1],
                                     start=True, stop=True)
                last.then_inc(gn_pe.sem, gn_pe.mark(f"n{t}"))
            after(gn_dve, "bege")
            for p in range(2):
                pe.wait_ge(lin_free[p], 2 * PLAN["a_out"].fills[p] + 2)
            with pe.Fori(0, DN_HEADS // 2) as i:
                for step in GP:
                    for e in range(2):
                        B = [ps[:, 4 * e + b, :] for b in range(4)]

                        def cc(t, c):
                            return t[:, c * P:(c + 1) * P]

                        def chunks(out_, left, right, transposed=False):
                            for c in ch:
                                if transposed:
                                    r = pe.transpose(cc(out_, c), cc(left, c), ident[:])
                                else:
                                    r = pe.matmul(cc(out_, c), cc(left, c), cc(right, c), start=True, stop=True)
                            return r

                        if step == "raw":
                            after(g_act, f"{e}stq", i)
                            after(g_dve, f"{e}ot", i - 1)
                            for b, src in enumerate((kf, vf, qf)):
                                last = chunks(B[b], src[e], None, True)
                        elif step == "row":
                            after(g_dve, f"{e}goh", i)
                            last = pe.matmul(B[3], ones[0:48, :], goh[:, e, :], start=True, stop=True)
                        elif step == "turned":
                            after(g_dve, f"{e}kb", i)
                            for b, src in enumerate((kn, kb, qn)):
                                last = chunks(B[b], src[e], None, True)
                        elif step == "prod":
                            after(g_act, f"{e}qt", i)
                            chunks(B[0], kt[e], kbt[e])
                            last = chunks(B[1], kt[e], qt[e])
                        elif step == "t0":
                            after(g_dve, f"{e}tt0", i)
                            last = chunks(B[2], tt[e], None, True)
                        elif step[0] == "x":
                            k = int(step[1])
                            after(g_dve, f"{e}ltk{k}", i)
                            after(g_act, f"{e}ti{k - 1}", i)
                            last = chunks(B[3], ltk[e], ti[e])
                        elif step[:2] == "tt":
                            after(g_dve, f"{e}xi{step[2]}", i)
                            last = chunks(B[0], xi[e], tt[e])
                        elif step[0] == "t":
                            after(g_dve, f"{e}xi{step[1]}", i)
                            last = chunks(B[2], tt[e], xi[e])
                        elif step == "nk":
                            after(g_dve, f"{e}tt6", i)
                            last = chunks(B[3], kbe[e], tt[e])
                        elif step[0] == "v":
                            c = int(step[1])
                            if c:
                                after(g_act, f"{e}nkc", i)
                                after(g_dve, f"{e}s{c - 1}", i)
                            last = pe.matmul(cc(B[0], c), cc(tt[e], c), cc(vb[e], c), start=True, stop=c == 0)
                            if c:
                                last = pe.matmul(cc(B[0], c), cc(nkc[e], c), sg[e][:], start=False, stop=True)
                        elif step[0] == "o":
                            c = int(step[1])
                            if c:
                                pe.matmul(cc(B[1], c), cc(eg[e], c), sg[e][:], start=True, stop=False)
                            after(g_act, f"{e}vn{c}", i)
                            last = pe.matmul(cc(B[1], c), cc(an[e], c), cc(vn[e], c), start=c == 0, stop=True)
                        else:
                            c = int(step[1])
                            last = pe.matmul(cc(B[2], c), cc(kd[e], c), cc(vn[e], c), start=True, stop=True)
                        last.then_inc(g_pe.sem, g_pe.mark(f"{e}{step}"))
            for k in k8:
                after(gn_dve, "sc3")
                if k >= 4:
                    after(gn_dve, f"f{k - 4}")
                for n in ch:
                    last = pe.transpose(ps[:, 4 + k % 4, n * P:(n + 1) * P], ot[:, n, k * P:(k + 1) * P], ident[:])
                last.then_inc(gn_pe.sem, gn_pe.mark(f"t{k}"))
            after(gn_dve, "l7")
            std("a_out", (ayh, ayl))
            sum_squares(4)
            ffn(1, 3)

            sum_squares(5)
            quad("kv_k", 0, 0, 0, 0, (uh, ul), (u_dve, "ul", 4))
            quad_tok("kv_v", 0, 0, 1, 0, (uh, ul))
            std("q2", (ubh, ubl), (u_dve, "ul", 5))
            for p in range(2):
                pe.wait_ge(lin_free[p], 2 * PLAN["o2"].fills[p] + 2)
            with pe.Fori(0, KV_HEADS) as i:
                for step in BP:
                    u = int(step[1])
                    if step[0] == "s":
                        after(b_act, "st", i)
                        if u >= 2:
                            after(b_dve, f"sb{u - 2}", i)
                        else:
                            after(b_dve, f"sb{u + 2}", i - 1)
                        r = slice(HD * (u % 2), HD * (u % 2) + HD)
                        for n in range(NT):
                            lo = P if n == 0 else 0
                            o = ps[:, 2 * (u % 2) + n // 2, 256 * (n % 2) + lo:256 * (n % 2) + 256]
                            last = pe.matmul(o, qst[r, u // 2, n * P:(n + 1) * P], kst[r, max(n - 1, 0) * P:(n + 1) * P],
                                             start=True, stop=True)
                    elif step[0] == "t":
                        after(b_act, f"p{u}", i)
                        if u:
                            after(b_act, f"c{u - 1}", i)
                        else:
                            after(b_act, "c3", i - 1)
                        for x_ in range(7):
                            n, lo = (x_ + 1) // 2, P * ((x_ + 1) % 2)
                            last = pe.transpose(ps[:, 4 + x_ // 4, P * (x_ % 4):P * (x_ % 4) + P],
                                                pr2[:, u % 2, n, lo:lo + P], ident[:])
                    else:
                        after(b_act, f"c{u}", i)
                        if u >= 2:
                            after(b_dve, f"o{u - 2}", i)
                        else:
                            after(b_dve, f"o{u + 2}", i - 1)
                        for n in range(NT):
                            o = ps[:, 6 + u % 2, HD * n:HD * n + HD]
                            if n:
                                pe.matmul(o, pt2[:, 2 * n - 1, :], vv[:, n - 1, bass.ds(HD * i, HD)], start=True, stop=False)
                            last = pe.matmul(o, pt2[:, 2 * n, :], vv[:, n, bass.ds(HD * i, HD)], start=n == 0, stop=True)
                    last.then_inc(b_pe.sem, b_pe.mark(step))
            for k in k8:
                after(b_dve, "o3", 3)
                if k >= 4:
                    after(bo_dve, f"l{k - 4}")
                for n in ch:
                    last = pe.transpose(ps[:, 4 + k % 4, n * P:(n + 1) * P], o_tok[:, n, k * P:(k + 1) * P], ident[:])
                last.then_inc(bo_pe.sem, bo_pe.mark(f"t{k}"))
            after(bo_dve, "l7")
            std("o2", (uh, ul))
            sum_squares(6)
            ffn(2, 6)
            sum_squares(7)

            for n in ch:
                pe.wait_ge(out_made, 8)
                if n >= 2:
                    pe.wait_ge(fin_dve.sem, fin_dve.value(f"c{n - 2}"))
                for k in k8:
                    last = pe.transpose(ps[:, 4 + 2 * (n % 2) + k // 4, P * (k % 4):P * (k % 4) + P],
                                        out_t[:, k, n * P:(n + 1) * P], ident[:])
                last.then_inc(fin_pe.sem, fin_pe.mark(f"t{n}"))

        @block.vector
        def _(dve):
            def norm(n):
                dve.wait_ge(norm_pe.sem, norm_pe.value("sum7", n))
                dve.tensor_scalar(ms[:], bank(4), 1.0 / D, EPS, ALU.mult, ALU.add).then_inc(norm_dve.sem, norm_dve.mark("ms"))
                dve.wait_ge(norm_dve.sem, norm_dve.value("ms", n))
                dve.reciprocal(rc[:], ms[:]).then_inc(norm_dve.sem, norm_dve.mark("rc"))

            def normed(n, m, gain, dst):
                def full(k):
                    if k == 0:
                        dve.wait_ge(norm_act.sem, norm_act.value("rs", n))
                    if k >= 2:
                        dve.wait_ge(u_act.sem, u_act.value(f"uh{k - 2}", m))
                        dve.wait_ge(u_dve.sem, u_dve.value(f"ul{k - 2}", m))
                    dve.scalar_tensor_tensor(out=uf[:, k % 2, :], in0=h[:, k, :], scalar=column(gain, k), in1=rs[:],
                                             op0=ALU.mult, op1=ALU.mult).then_inc(u_dve.sem, u_dve.mark(f"u{k}"))
                full(0)
                for k in k8:
                    if k < 7:
                        full(k + 1)
                    dve.wait_ge(u_act.sem, u_act.value(f"uh{k}", m))
                    dve.wait_ge(u_dve.sem, u_dve.value(f"u{k}", m))
                    dve.tensor_tensor(dst[:, k, :], uf[:, k % 2, :], uh_of(dst)[:, k, :].bitcast(F32), ALU.subtract)\
                       .then_inc(u_dve.sem, u_dve.mark(f"ul{k}"))

            def uh_of(low):
                return uh if low is ul else ubh

            def scalars(n):
                w8 = lambda name: dve.wait_ge(sc_dve.sem, sc_dve.value(name, n))
                dve.wait_ge(sc_pe.sem, sc_pe.value("logits", n))
                dve.wait_ge(prep_dve.sem, prep_dve.value("a_neg"))
                dve.tensor_scalar(sc[:, 0, :], ps[0:48, 5, :], sgn[:], sgn_bias[:, n:n + 1], ALU.mult, ALU.add)\
                   .then_inc(sc_dve.sem, sc_dve.mark("t"))
                w8("t")
                dve.scalar_tensor_tensor(out=sc[:, 1, :], in0=sc[:, 0, :], scalar=-1.0, in1=sc[:, 0, :], op0=ALU.mult,
                                         op1=ALU.max).then_inc(sc_dve.sem, sc_dve.mark("abs"))
                dve.wait_ge(sc_act.sem, sc_act.value("exp", n))
                dve.tensor_scalar(sc[:, 3, :], sc[:, 2, :], 1.0, None, ALU.add).then_inc(sc_dve.sem, sc_dve.mark("one"))
                w8("one")
                dve.tensor_scalar(sc[:, 4, :], sc[:, 3, :], -1.0, None, ALU.add).then_inc(sc_dve.sem, sc_dve.mark("w"))
                w8("w")
                dve.tensor_scalar(sc[:, 6, :], sc[:, 4, :], 0.0, None, ALU.is_equal).then_inc(sc_dve.sem, sc_dve.mark("eq"))
                w8("eq")
                dve.tensor_tensor(sc[:, 7, :], sc[:, 4, :], sc[:, 6, :], ALU.add).then_inc(sc_dve.sem, sc_dve.mark("den"))
                w8("den")
                dve.reciprocal(sc[:, 8, :], sc[:, 7, :]).then_inc(sc_dve.sem, sc_dve.mark("inv"))
                dve.wait_ge(sc_act.sem, sc_act.value("ln", n))
                dve.tensor_tensor(sc[:, 1, :], sc[:, 5, :], sc[:, 6, :], ALU.add).then_inc(sc_dve.sem, sc_dve.mark("num"))
                w8("num")
                dve.tensor_tensor(sc[:, 3, :], sc[:, 1, :], sc[:, 8, :], ALU.mult).then_inc(sc_dve.sem, sc_dve.mark("q"))
                w8("q")
                dve.tensor_tensor(sc[:, 4, :], sc[:, 3, :], sc[:, 2, :], ALU.mult).then_inc(sc_dve.sem, sc_dve.mark("r"))
                w8("r")
                sp_at, scaled_at = (9, 6) if n == 0 else (5, 9)
                dve.scalar_tensor_tensor(out=sc[:, sp_at, :], in0=sc[:, 0, :], scalar=0.0, in1=sc[:, 4, :],
                                         op0=ALU.max, op1=ALU.add).then_inc(sc_dve.sem, sc_dve.mark("sp"))
                w8("sp")
                dve.tensor_scalar(sc[:, scaled_at, :], sc[:, sp_at, :], row_scale[:, n:n + 1], None, ALU.mult)\
                   .then_inc(sc_dve.sem, sc_dve.mark("scaled"))
                w8("scaled")
                dve.tensor_tensor_scan(cs[:], keep[:], sc[:, scaled_at, :], 0.0, ALU.mult, ALU.add)\
                   .then_inc(sc_dve.sem, sc_dve.mark("sums"))

            def scalars_by_token(n):
                dve.wait_ge(sc_pe.sem, sc_pe.value("turned", n))
                dve.tensor_copy(tok[:].rearrange("p a b c -> p (a b c)"), ps[:, 5, 0:384])\
                   .then_inc(sc_dve.sem, sc_dve.mark("tok"))
                dve.wait_ge(sc_dve.sem, sc_dve.value("tok", n))
                dve.wait_ge(sc_pe.sem, sc_pe.value("last", n))
                dve.tensor_tensor(decay_end[:].rearrange("p a b -> p (a b)"), ps[:, 6, 0:192],
                                  tok[:, 0, :, :].rearrange("p a b -> p (a b)"), ALU.subtract)\
                   .then_inc(sc_dve.sem, sc_dve.mark("end"))

            def conv4(ph, w_name, turn0, buf):
                with dve.Fori(0, PLAN[ph].quads // 2) as i:
                    turn = i + turn0
                    for g in range(2):
                        for c in range(2):
                            b, t = 2 * g + c, 4 * i + 2 * g + c
                            dve.wait_ge(conv_act.sem, conv_act.value(f"t{b}", turn))
                            dve.scalar_tensor_tensor(out=buf[:, b, 1:S], in0=ps[:, b, 0:S - 1], scalar=column(w_name, t + 2 * TAPS[ph]),
                                                     in1=buf[:, b, 1:S], op0=ALU.mult, op1=ALU.add)\
                               .then_inc(conv_dve.sem, conv_dve.mark(f"a{b}"))
                        for c in range(2):
                            b, t = 2 * g + c, 4 * i + 2 * g + c
                            dve.wait_ge(conv_dve.sem, conv_dve.value(f"a{b}", turn))
                            dve.scalar_tensor_tensor(out=buf[:, b, 2:S], in0=ps[:, b, 0:S - 2], scalar=column(w_name, t + TAPS[ph]),
                                                     in1=buf[:, b, 2:S], op0=ALU.mult, op1=ALU.add)\
                               .then_inc(conv_dve.sem, conv_dve.mark(f"b{b}"))
                        for c in range(2):
                            b, t = 2 * g + c, 4 * i + 2 * g + c
                            dve.wait_ge(conv_dve.sem, conv_dve.value(f"b{b}", turn))
                            dve.scalar_tensor_tensor(out=buf[:, b, 3:S], in0=ps[:, b, 0:S - 3], scalar=column(w_name, t),
                                                     in1=buf[:, b, 3:S], op0=ALU.mult, op1=ALU.add)\
                               .then_inc(lin_free[g], 1)

            def added(ph, bias=None):
                with dve.Fori(0, PLAN[ph].quads // 2) as i:
                    for g in range(2):
                        dve.wait_ge(pe_used, 8 * i + (4 * (PLAN[ph].first + g) + 8))
                        for c in range(2):
                            t = bass.ds(4 * i + 2 * g + c, 1)
                            src = ps[:, 2 * g + c:2 * g + c + 1, :]
                            if bias:
                                dve.scalar_tensor_tensor(out=h[:, t, :], in0=src, scalar=column(bias, 4 * i + 2 * g + c),
                                                         in1=h[:, t, :], op0=ALU.add, op1=ALU.add).then_inc(lin_free[g], 1)
                            else:
                                dve.tensor_tensor(h[:, t, :], src, h[:, t, :], ALU.add).then_inc(lin_free[g], 1)

            dve.wait_ge(consts_ready, 1)
            for b in range(3):
                n = min(4, 9 - 4 * b)
                dve.wait_ge(x_pe.sem, x_pe.value(f"par{b}"))
                dve.tensor_copy(par[:, 4 * b:4 * b + n, :].rearrange("p a b -> p (a b)"), ps[:, 5 + b, 0:P * n])\
                   .then_inc(prep_dve.sem, prep_dve.mark(f"par{b}"))
            for k in k8:
                dve.wait_ge(x_pe.sem, x_pe.value(f"x{k}"))
                dve.tensor_copy(h[:, k, :], bank(k % 4)).then_inc(x_ready, 1)
            dve.wait_ge(small_landed, 16 * 9)
            dve.tensor_copy(wsh[:], ws[:]).then_inc(prep_dve.sem, prep_dve.mark("wsh"))
            dve.wait_ge(prep_dve.sem, prep_dve.value("wsh"))
            dve.tensor_tensor(wsl[:], ws[:], wsh[:].bitcast(F32), ALU.subtract).then_inc(prep_dve.sem, prep_dve.mark("wsl"))
            dve.tensor_scalar(sgn_bias[:], raw_bias[:], sgn[:], None, ALU.mult).then_inc(prep_dve.sem, prep_dve.mark("sgn_bias"))
            dve.wait_ge(prep_act.sem, prep_act.value("a_exp"))
            dve.tensor_scalar(row_scale[:], row_scale[:], -1.0, None, ALU.mult).then_inc(prep_dve.sem, prep_dve.mark("a_neg"))
            dve.wait_ge(prep_dve.sem, prep_dve.value("a_neg"))
            norm(0)
            normed(0, 0, "norm_mix", ul)
            scalars(0)
            conv4("xbc", "ssd_conv_w", 0, cv)
            scalars_by_token(0)

            def heads16(t):
                return t.unsqueeze(2).to_broadcast([P, SSD_HEADS, HD])

            def by_head(t):
                return t.rearrange("p (h d) -> p h d", d=HD)

            def own(name):
                dve.wait_ge(ssd_dve.sem, ssd_dve.value(name))

            def mark(name):
                return ssd_dve.sem, ssd_dve.mark(name)

            for g in range(SSD_GROUPS):
                dve.wait_ge(ssd_pe.sem, ssd_pe.value(f"cb{g}"))
                dve.tensor_tensor(cb[:, g, :].rearrange("p (c l) -> p c l", c=NT), ps[:, 4 + g, :].rearrange("p (c l) -> p c l", c=NT),
                                  upto[:].unsqueeze(1).to_broadcast([P, NT, P]), ALU.mult).then_inc(*mark(f"cb{g}"))
            dve.wait_ge(sc_act.sem, sc_act.value("chunk", 0))
            for c in ch:
                dve.wait_ge(ssd_pe.sem, ssd_pe.value(f"x{c}"))
                dve.tensor_tensor(by_head(xd[:, c, :]), by_head(ps[:, 4:6, :].rearrange("p a b -> p (a b)")),
                                  heads16(tok[:, 1, c, 32:48]), ALU.mult).then_inc(*mark(f"xd{c}"))
                if c == 3:
                    break
                dve.wait_ge(ssd_pe.sem, ssd_pe.value(f"b{c}"))
                if c:
                    dve.wait_ge(ssd_pe.sem, ssd_pe.value(f"state{c - 1}_1"))
                dve.tensor_copy(bt[:], ps[:, 6, 0:2 * P]).then_inc(*mark(f"b{c}"))
                own(f"xd{c}")
                dve.tensor_tensor(by_head(xdd[:]), by_head(xd[:, c, :]), heads16(decay_end[:, c, 32:48]), ALU.mult)\
                   .then_inc(*mark(f"xdd{c}"))
                if c:
                    dve.tensor_tensor(by_head(stq[:]), by_head(st[:, c - 1, :]), heads16(chunk_decay[:, c, 32:48]), ALU.mult)\
                       .then_inc(*mark(f"dec{c}"))
                    own(f"dec{c}")
                dve.wait_ge(ssd_pe.sem, ssd_pe.value(f"state{c}_1"))
                src = ps[:, 6:8, :].rearrange("p a b -> p (a b)")
                if c:
                    dve.tensor_tensor(st[:, c, :], src, stq[:], ALU.add).then_inc(*mark(f"st{c}"))
                else:
                    dve.tensor_copy(st[:, 0, :], src).then_inc(*mark("st0"))
            own("xd3")
            for grp in range(SSD_GROUPS):
                with dve.Fori(0, 4) as i:
                    turn = i + 4 * grp
                    for e in range(2):
                        dve.tensor_scalar(oh[:, e, :], cs[:], ident[0:48, bass.ds(2 * i + (32 + 8 * grp + e), 1)], None, ALU.mult)\
                           .then_inc(sh_dve.sem, sh_dve.mark(f"oh{e}"))
                    for e in range(2):
                        dve.wait_ge(sh_pe.sem, sh_pe.value(f"row{e}", turn))
                        for c in ch:
                            last = dve.tensor_scalar(dd[:, e, c * P:(c + 1) * P], ps[:, 4 + e, c * P:(c + 1) * P],
                                                     tok[:, 0, c, bass.ds(2 * i + (32 + 8 * grp + e), 1)], 0.0,
                                                     ALU.subtract, ALU.min)
                        last.then_inc(sh_dve.sem, sh_dve.mark(f"d{e}"))
                    for e in range(2):
                        dve.wait_ge(sh_act.sem, sh_act.value(f"e{e}", turn))
                        dve.wait_ge(sh_pe.sem, sh_pe.value(f"y{e}", turn - 1))
                        dve.tensor_tensor(mt[:, e, :], dd[:, e, :], cb[:, grp, :], ALU.mult)\
                           .then_inc(sh_dve.sem, sh_dve.mark(f"m{e}"))
                        dve.wait_ge(sh_act.sem, sh_act.value(f"r{e}", turn))
                        dve.tensor_tensor(ce[:, e, :], xc[:, 10 + grp, :], ec[:, e, :], ALU.mult)\
                           .then_inc(sh_dve.sem, sh_dve.mark(f"c{e}"))
            for k in k8:
                dve.wait_ge(sy_pe.sem, sy_pe.value(f"t{k}"))
                dve.scalar_tensor_tensor(out=yf[:, k % 2, :], in0=xc[:, k, :], scalar=d_skip[:, k:k + 1], in1=bank(4 + k % 2),
                                         op0=ALU.mult, op1=ALU.add).then_inc(sy_dve.sem, sy_dve.mark(f"w{k}"))
                dve.wait_ge(sy_dve.sem, sy_dve.value(f"w{k}"))
                if k == 0:
                    for p in range(2):
                        dve.wait_ge(lin_free[p], std_value("z", p, 1))
                dve.tensor_tensor(zs[:, k, :], yf[:, k % 2, :], zs[:, k, :], ALU.mult).then_inc(sy_dve.sem, sy_dve.mark(f"g{k}"))
            for g in range(2):
                dve.wait_ge(sy_pe.sem, sy_pe.value(f"sum{4 * g + 3}"))
                dve.tensor_scalar(yms[:, g, :], bank(6 + g), 1.0 / 512, EPS, ALU.mult, ALU.add).then_inc(sy_dve.sem, sy_dve.mark(f"ms{g}"))
                dve.wait_ge(sy_dve.sem, sy_dve.value(f"ms{g}"))
                dve.reciprocal(yrs[:, g, :], yms[:, g, :]).then_inc(sy_dve.sem, sy_dve.mark(f"rc{g}"))

            def y_normed(k):
                dve.wait_ge(sy_act.sem, sy_act.value(f"rs{k // 4}"))
                if k >= 2:
                    dve.wait_ge(sy_act.sem, sy_act.value(f"h{k - 2}"))
                    dve.wait_ge(sy_dve.sem, sy_dve.value(f"l{k - 2}"))
                dve.scalar_tensor_tensor(out=yf[:, k % 2, :], in0=zs[:, k, :], scalar=column("ssd_norm", k), in1=yms[:, k // 4, :],
                                         op0=ALU.mult, op1=ALU.mult).then_inc(sy_dve.sem, sy_dve.mark(f"f{k}"))

            y_normed(0)
            for k in k8:
                if k < 7:
                    y_normed(k + 1)
                dve.wait_ge(sy_act.sem, sy_act.value(f"h{k}"))
                dve.tensor_tensor(ysl[:, k, :], yf[:, k % 2, :], ysh[:, k, :].bitcast(F32), ALU.subtract)\
                   .then_inc(sy_dve.sem, sy_dve.mark(f"l{k}"))

            def pmark(name):
                return po_dve.sem, po_dve.mark(name)

            def pown(name):
                dve.wait_ge(po_dve.sem, po_dve.value(name))

            dve.memset(pv[:, :, 0:PADV], 0.0).then_inc(*pmark("pad"))
            for g in range(4):
                dve.wait_ge(lin_free[g // 2], std_value("pool", g // 2, 0, 1))
                src, W = pv[:, g, :], PADV + S
                pown(f"e{g - 1}" if g else "pad")
                for n in range(g + 1):
                    dst, lag = win[:, n % 2, :], 1 << n
                    lo = 2 * lag - 1
                    if n:
                        pown(f"s{g}_{n - 1}")
                    dve.tensor_tensor(dst[:, lo:W], src[:, lo:W], src[:, lo - lag:W - lag], ALU.add).then_inc(*pmark(f"s{g}_{n}"))
                    src = dst
                pown(f"s{g}_{g}")
                w = WINDOWS[g]
                dve.scalar_tensor_tensor(out=dp[:, g, :], in0=src[:, PADV:W], scalar=1.0 / w, in1=pv[:, g, PADV:W],
                                         op0=ALU.mult, op1=ALU.subtract).then_inc(*pmark(f"d{g}"))
                pown(f"d{g}")
                dve.tensor_tensor(src[:, PADV:PADV + w - 1], src[:, PADV:PADV + w - 1], inv_count[:, 0:w - 1], ALU.mult)\
                   .then_inc(*pmark(f"q{g}"))
                pown(f"q{g}")
                dve.tensor_tensor(dp[:, g, 0:w - 1], src[:, PADV:PADV + w - 1], pv[:, g, PADV:PADV + w - 1], ALU.subtract)\
                   .then_inc(*pmark(f"e{g}"))
            for g in range(4):
                dve.wait_ge(po_act.sem, g + 1)
                dve.scalar_tensor_tensor(out=ypl[:, g, :], in0=bank(4 + g), scalar=column("pool_scale", g),
                                         in1=yph[:, g, :].bitcast(F32), op0=ALU.mult, op1=ALU.subtract).then_inc(*pmark(f"l{g}"))
            pown("l3")
            with dve.Fori(0, 4) as i:
                for e in range(2):
                    for ev in AT_DVE:
                        if ev == "oh":
                            last = dve.tensor_scalar(ohc[:], cs[:], ident[0:48, bass.ds(2 * i + e, 1)], -1.0, ALU.mult, ALU.mult)
                        elif ev == "nb":
                            dve.wait_ge(at_pe.sem, at_pe.value(f"{e}bc", i))
                            last = dve.tensor_copy(nb[:, e, :], bank(6))
                        else:
                            n, u = int(ev[1]), 4 * e + int(ev[1])
                            L = P * (n + 1)
                            if ev[0] == "s":
                                dve.wait_ge(at_pe.sem, at_pe.value(f"{e}s{n}", i))
                                dve.wait_ge(at_act.sem, step_back(at_act, "p", u, 2, i))
                                dve.wait_ge(at_dve.sem, at_dve.value(f"{e}nb", i))
                                last = dve.tensor_tensor(sm[:, u % 2, 0:L], ps[:, 4 + u % 2, 0:L], nb[:, e, 0:L], ALU.add)
                            elif ev[0] == "x":
                                dve.wait_ge(at_dve.sem, at_dve.value(f"{e}s{n}", i))
                                last = dve.tensor_reduce(stat[:, u:u + 1], sm[:, u % 2, 0:L], AX_X, ALU.max)
                            elif ev[0] == "m":
                                dve.wait_ge(at_dve.sem, at_dve.value(f"{e}x{n}", i))
                                last = dve.tensor_scalar(stat[:, 8 + u:9 + u], stat[:, u:u + 1], -1.0, None, ALU.mult)
                            elif ev[0] == "r":
                                dve.wait_ge(at_act.sem, at_act.value(f"{e}p{n}", i))
                                last = dve.reciprocal(stat[:, 24 + u:25 + u], stat[:, 16 + u:17 + u])
                            else:
                                dve.wait_ge(at_dve.sem, at_dve.value(f"{e}r{n}", i))
                                dve.wait_ge(at_pe.sem, at_pe.value(f"{e}o{n}", i))
                                last = dve.tensor_scalar(oa[:, n, bass.ds(128 * i + 64 * e, HD)], ps[:, 7, 64 * u:64 * u + 64],
                                                         stat[:, 24 + u:25 + u], None, ALU.mult)
                        last.then_inc(at_dve.sem, at_dve.mark(f"{e}{ev}"))
            for k in range(4):
                dve.wait_ge(ay_act.sem, ay_act.value(f"h{k}"))
                dve.tensor_tensor(yal[:, k, :], bank(4 + k), yah[:, k, :].bitcast(F32), ALU.subtract)\
                   .then_inc(ay_dve.sem, ay_dve.mark(f"l{k}"))
            for ph in ("proj_pool", "proj_attn"):
                with dve.Fori(0, 2) as i:
                    for p in range(2):
                        dve.wait_ge(pe_used, 4 * i + (4 * PLAN[ph].first + 2 * p + 6))
                        if p == 0 and i is not None:
                            gate = "gate0" if ph == "proj_pool" else "gate1"
                            for pp in range(2):
                                dve.wait_ge(lin_free[pp], std_value(gate, pp, 1))
                        for c in range(2):
                            t = bass.ds(4 * i + 2 * p + c, 1)
                            b = 2 * p + c
                            if ph == "proj_pool":
                                dve.tensor_tensor(mg[:, t, :], ps[:, b:b + 1, :], gt[:, t, :], ALU.mult).then_inc(lin_free[p], 1)
                                continue
                            if b >= 2:
                                dve.wait_ge(mg_dve.sem, mg_dve.value(f"m{b - 2}", i))
                            else:
                                dve.wait_ge(mg_dve.sem, mg_dve.value(f"m{b + 2}", i - 1))
                            dve.tensor_tensor(tmp[:, c:c + 1, :], ps[:, b:b + 1, :], gt[:, t, :], ALU.mult).then_inc(lin_free[p], 1)
                            dve.wait_ge(lin_free[p], 2 * i + (2 * PLAN[ph].fills[p] + 3 + c))
                            dve.tensor_tensor(mg[:, t, :], tmp[:, c:c + 1, :], mg[:, t, :], ALU.add)\
                               .then_inc(mg_dve.sem, mg_dve.mark(f"m{b}"))
            with dve.Fori(0, 2) as i:
                for g in range(2):
                    dve.wait_ge(pe_used, 8 * i + (4 * (PLAN["proj_ssd"].first + g) + 8))
                    if g == 0:
                        for pp in range(2):
                            dve.wait_ge(lin_free[pp], std_value("gate2", pp, 1))
                    for c in range(2):
                        t = bass.ds(4 * i + 2 * g + c, 1)
                        b = 2 * g + c
                        dve.wait_ge(mg_dve.sem, mg_dve.value(f"m{b - 2}", i + 2) if b >= 2 else mg_dve.value(f"m{b + 2}", i + 1))
                        dve.tensor_tensor(tmp[:, c:c + 1, :], ps[:, b:b + 1, :], gt[:, t, :], ALU.mult).then_inc(lin_free[g], 1)
                        dve.wait_ge(lin_free[g], std_value("proj_ssd", g, i, c))
                        dve.tensor_tensor(mg[:, t, :], tmp[:, c:c + 1, :], mg[:, t, :], ALU.add)\
                           .then_inc(mg_dve.sem, mg_dve.mark(f"m{b}"))
                    for c in range(2):
                        t = bass.ds(4 * i + 2 * g + c, 1)
                        dve.wait_ge(mg_act.sem, 4 * i + (2 * g + c + 1))
                        dve.wait_ge(mg_dve.sem, mg_dve.value(f"m{2 * g + c}", i + 2))
                        dve.tensor_tensor(ul[:, t, :], mg[:, t, :], uh[:, t, :].bitcast(F32), ALU.subtract).then_inc(mg_low.sem, 1)
            added("w_out")

            def ffn(f):
                up, w = f"up{f}", f"f{f}w"
                with dve.Fori(0, FT // 2) as i:
                    turn = i + (FT // 2) * f
                    own = lambda name, back=0: dve.wait_ge(ffn_dve.sem, ffn_dve.value(name, turn - back if back else turn))
                    for g in range(2):
                        for c in range(2):
                            b, t = 2 * g + c, 2 * i + (FT * g + c)
                            dve.wait_ge(ffn_act.sem, ffn_act.value(f"t{b}", turn))
                            dve.scalar_tensor_tensor(out=fc[:, b, 1:S], in0=ps[:, b, 0:S - 1], scalar=column(w, t + 2 * FT),
                                                     in1=fc[:, b, 1:S], op0=ALU.mult, op1=ALU.add)\
                               .then_inc(ffn_dve.sem, ffn_dve.mark(f"a{b}"))
                        for c in range(2):
                            b, t = 2 * g + c, 2 * i + (FT * g + c)
                            own(f"a{b}")
                            dve.scalar_tensor_tensor(out=fc[:, b, 2:S], in0=ps[:, b, 0:S - 2], scalar=column(w, t),
                                                     in1=fc[:, b, 2:S], op0=ALU.mult, op1=ALU.add).then_inc(lin_free[g], 1)
                    for c in range(2):
                        dve.wait_ge(ffn_act.sem, ffn_act.value(f"s{c}", turn))
                        dve.wait_ge(ffn_act.sem, ffn_act.value(f"fh{c}", turn - 1))
                        own(f"fl{c}", 1)
                        dve.wait_ge(lin_free[1], std_value(up, 1, i, c))
                        dve.tensor_tensor(ff[:, c, :], fg[:, c, :], fc[:, 2 + c, :], ALU.mult)\
                           .then_inc(ffn_dve.sem, ffn_dve.mark(f"hf{c}"))
                    for c in range(2):
                        t = bass.ds(2 * i + c, 1)
                        dve.wait_ge(ffn_act.sem, ffn_act.value(f"fh{c}", turn))
                        own(f"hf{c}")
                        dve.tensor_tensor(fl[:, t, :], ff[:, c:c + 1, :], fh[:, t, :].bitcast(F32), ALU.subtract)\
                           .then_inc(ffn_dve.sem, ffn_dve.mark(f"fl{c}"))
                ph = PLAN[f"down{f}"]
                dve.wait_ge(pe_used, 4 * (ph.first + ph.quads) + 4)
                for t in (4, 0, 1, 2, 3, 5, 6, 7):
                    last = dve.tensor_tensor(h[:, t, :], bank(t), h[:, t, :], ALU.add)
                    last.then_inc(lin_free[t // 2] if t < 4 else h_high, 1)

            norm(1)
            normed(1, 1, "norm_ffn", ul)
            ffn(0)
            norm(2)
            for k in k8:
                dve.wait_ge(norm_act.sem, norm_act.value("rs", 2))
                h_wait(dve, 2, k)
                dve.scalar_tensor_tensor(out=h[:, k, :], in0=h[:, k, :], scalar=column("norm_final", k), in1=rs[:],
                                         op0=ALU.mult, op1=ALU.mult).then_inc(renormed, 1)

            dve.memset(ws[:], 0.0).then_inc(prep_dve2.sem, prep_dve2.mark("zero"))
            norm(3)
            normed(3, 2, "a_norm", ul)
            dve.wait_ge(small_landed, 16 * 11)
            dve.tensor_copy(wsh[:], ws[:]).then_inc(prep_dve2.sem, prep_dve2.mark("wsh"))
            dve.wait_ge(prep_dve2.sem, prep_dve2.value("wsh"))
            dve.tensor_tensor(wsl[:], ws[:], wsh[:].bitcast(F32), ALU.subtract).then_inc(prep_dve2.sem, prep_dve2.mark("wsl"))
            scalars(1)
            conv4("a_qkv", "a_conv_w", 3, acv)
            scalars_by_token(1)

            def gmark(name):
                return gn_dve.sem, gn_dve.mark(name)

            def after(events, name, turn=0):
                dve.wait_ge(events.sem, events.value(name, turn))

            dve.wait_ge(pe_used, 4 * PLAN["a_out"].first + 4)
            dve.tensor_copy(cs2[:], cs[:]).then_inc(*gmark("cs"))
            after(gn_pe, "n15")
            dve.tensor_scalar(rn2[:].rearrange("p a b -> p (a b)"), ps[:, 4, 0:64], EPS, None, ALU.add).then_inc(*gmark("ns"))
            after(gn_dve, "ns")
            dve.reciprocal(rn[:], rn2[:]).then_inc(*gmark("nr"))
            after(gn_act, "rt")
            dve.tensor_scalar(rn2[:, 0:8, :], rn2[:, 0:8, :], float(P) ** -0.5, None, ALU.mult).then_inc(*gmark("qs"))
            dve.tensor_tensor(bege[:], beta[:], egc[:], ALU.mult).then_inc(*gmark("bege"))
            after(gn_dve, "bege")

            def by_chunk(t):
                return t.rearrange("p (c d) -> p c d", c=NT)

            with dve.Fori(0, DN_HEADS // 2) as i:
                for step in GD:
                    for e in range(2):
                        B = [ps[:, 4 * e + b, :] for b in range(4)]
                        head = bass.ds(2 * i + e, 1)

                        def scaled(dst, src, factor):
                            return dve.tensor_tensor(by_chunk(dst), by_chunk(src), factor.to_broadcast([P, NT, P]), ALU.mult)

                        def own(name):
                            after(g_dve, f"{e}{name}", i)

                        if step == "goh":
                            last = dve.tensor_scalar(goh[:, e, :], cs2[:], ident[0:48, bass.ds(2 * i + (32 + e), 1)], None, ALU.mult)
                        elif step == "kn":
                            after(g_pe, f"{e}raw", i)
                            last = scaled(kn[e][:], B[0], rn2[:, bass.ds(2 * i + (8 + e), 1), :].rearrange("p a b -> p b a"))
                        elif step == "vb":
                            last = scaled(vb[e][:], B[1], beta[:, :, head])
                        elif step == "qn":
                            last = scaled(qn[e][:], B[2], rn2[:, head, :].rearrange("p a b -> p b a"))
                        elif step == "kb":
                            own("kn")
                            last = scaled(kb[e][:], kn[e][:], beta[:, :, head])
                        elif step == "d":
                            after(g_act, f"{e}eg", i)
                            for c in ch:
                                last = dve.tensor_scalar(em[e][:, c * P:(c + 1) * P], B[3][:, c * P:(c + 1) * P],
                                                         tok[:, 0, c, bass.ds(2 * i + (32 + e), 1)], 0.0, ALU.subtract, ALU.min)
                        elif step == "kbe":
                            last = scaled(kbe[e][:], kn[e][:], bege[:, :, head])
                        elif step == "kd":
                            last = scaled(kd[e][:], kn[e][:], decay_end[:, :, bass.ds(2 * i + (32 + e), 1)])
                        elif step == "mask":
                            after(g_act, f"{e}em", i)
                            last = dve.tensor_tensor(by_chunk(em[e][:]), by_chunk(em[e][:]),
                                                     upto[:].unsqueeze(1).to_broadcast([P, NT, P]), ALU.mult)
                        elif step == "qd":
                            after(g_act, f"{e}qt", i)
                            last = dve.tensor_tensor(eg[e][:], qt[e][:], eg[e][:], ALU.mult)
                        elif step in ("lt", "an"):
                            if step == "lt":
                                after(g_pe, f"{e}prod", i)
                                own("mask")
                            dst, b = (lt, 0) if step == "lt" else (an, 1)
                            last = dve.tensor_tensor(dst[e][:], B[b], em[e][:], ALU.mult)
                        elif step == "i0":
                            own("lt")
                            last = dve.tensor_tensor(by_chunk(tt[e][:]), by_chunk(lt[e][:]),
                                                     level[:, 0, :].unsqueeze(1).to_broadcast([P, NT, P]), ALU.mult)
                        elif step == "tt0":
                            own("i0")
                            last = dve.tensor_tensor(by_chunk(tt[e][:]), by_chunk(tt[e][:]),
                                                     ident[:].unsqueeze(1).to_broadcast([P, NT, P]), ALU.add)
                        elif step[:3] == "ltk":
                            k = int(step[3])
                            if k > 1:
                                after(g_pe, f"{e}x{k - 1}", i)
                            else:
                                own("kd")
                            last = dve.tensor_tensor(by_chunk(ltk[e][:]), by_chunk(lt[e][:]),
                                                     level[:, k, :].unsqueeze(1).to_broadcast([P, NT, P]), ALU.mult)
                        elif step[:2] == "xi":
                            after(g_pe, f"{e}x{step[2]}", i)
                            own("an")
                            last = dve.tensor_tensor(by_chunk(xi[e][:]), by_chunk(B[3]),
                                                     ident[:].unsqueeze(1).to_broadcast([P, NT, P]), ALU.add)
                        elif step[:2] == "tt":
                            after(g_pe, f"{e}tt{step[2]}", i)
                            last = dve.tensor_copy(tt[e][:], B[0])
                        elif step == "ot":
                            after(g_pe, f"{e}o3", i)
                            last = dve.tensor_copy(ot[:, :, bass.ds(256 * i + P * e, P)], by_chunk(B[1]))
                        else:
                            c = int(step[1])
                            after(g_pe, f"{e}s{c}", i)
                            src = B[2][:, c * P:(c + 1) * P]
                            if c == 0:
                                last = dve.tensor_copy(sg[e][:], src)
                            else:
                                last = dve.scalar_tensor_tensor(out=sg[e][:], in0=sg[e][:],
                                                                scalar=chunk_decay[:, c, bass.ds(2 * i + (32 + e), 1)],
                                                                in1=src, op0=ALU.mult, op1=ALU.add)
                        last.then_inc(g_dve.sem, g_dve.mark(f"{e}{step}"))
            for n in ch:
                after(gn_act, f"q{n}")
                dve.tensor_reduce(oss[:, n, :], osq[:, n % 2, :].rearrange("p (h d) -> p h d", d=P), AX_X, ALU.add)\
                   .then_inc(*gmark(f"red{n}"))
            after(gn_dve, "red3")
            dve.tensor_scalar(oss2[:], oss[:], 1.0 / P, EPS, ALU.mult, ALU.add).then_inc(*gmark("om"))
            after(gn_dve, "om")
            dve.reciprocal(oss[:], oss2[:]).then_inc(*gmark("orc"))
            after(gn_act, "or")
            for n in ch:
                v_ = ot[:, n, :].rearrange("p (h d) -> p h d", d=P)
                dve.tensor_tensor(v_, v_, oss2[:, n, :].unsqueeze(2).to_broadcast([P, 8, P]), ALU.mult).then_inc(*gmark(f"sc{n}"))
            for k in k8:
                after(gn_pe, f"t{k}")
                if k >= 2:
                    after(gn_dve, f"l{k - 2}")
                dve.scalar_tensor_tensor(out=ayf[:, k % 2, :], in0=bank(4 + k % 4), scalar=column("onorm", 0), in1=ga[:, k, :],
                                         op0=ALU.mult, op1=ALU.mult).then_inc(*gmark(f"f{k}"))
                after(gn_act, f"h{k}")
                after(gn_dve, f"f{k}")
                dve.tensor_tensor(ayl[:, k, :], ayf[:, k % 2, :], ayh[:, k, :].bitcast(F32), ALU.subtract).then_inc(*gmark(f"l{k}"))
            added("a_out")
            norm(4)
            normed(4, 3, "f_norm0", ul)
            ffn(1)

            norm(5)
            normed(5, 4, "kv_norm", ul)
            dve.wait_ge(u_dve.sem, u_dve.value("ul7", 4))
            normed(5, 5, "b_norm", ubl)
            dve.memset(sm2[:, :, 0, 0:P], MASKED).then_inc(kv_dve.sem, kv_dve.mark("far"))
            dve.wait_ge(pe_used, 4 * PLAN["kv_k"].first + 8)
            for c in range(2):
                dve.tensor_scalar(kraw[:, c, :], bank(c), column("kv_b", c), None, ALU.add).then_inc(lin_free[0], 1)
            dve.wait_ge(pe_used, 4 * PLAN["kv_v"].first + 8)
            dve.wait_ge(vbias_landed, 16)
            dve.tensor_tensor(vv[:], ps[:, 2:4, :].rearrange("p a (b c) -> p (a b) c", b=2),
                              vbias[:].unsqueeze(1).to_broadcast([P, NT, 256]), ALU.add).then_inc(lin_free[1], 2)
            dve.wait_ge(lin_free[0], std_value("kv_k", 0, 0))
            for j in range(KV_HEADS):
                for half_ in range(2):
                    dve.tensor_copy(kk[HD * half_:HD * half_ + HD, j, :], kraw[HD * (j % 2):HD * (j % 2) + HD, j // 2, :])\
                       .then_inc(kv_dve.sem, kv_dve.mark(f"k{2 * j + half_}"))
            with dve.Fori(0, 2) as i:
                for g in range(2):
                    dve.wait_ge(pe_used, 8 * i + (4 * (PLAN["q2"].first + g) + 8))
                    for c in range(2):
                        dve.tensor_scalar(q2[:, bass.ds(4 * i + 2 * g + c, 1), :], ps[:, 2 * g + c:2 * g + c + 1, :],
                                          column("b_q", 4 * i + 2 * g + c), HD ** -0.5, ALU.add, ALU.mult).then_inc(lin_free[g], 1)
            dve.wait_ge(sinks_landed, 16)
            dve.wait_ge(later_ready, 1)
            dve.wait_ge(kv_dve.sem, kv_dve.value("far"))
            with dve.Fori(0, KV_HEADS) as i:
                for step in BD:
                    u, kind = int(step[-1]), step[:-1]

                    def own(name, turn):
                        after(b_dve, name, turn)

                    neg = st2[:, 8 * u:8 * u + 4]
                    if kind == "ab":
                        if u >= 2:
                            own(f"sb{u - 2}", i)
                        else:
                            own(f"sb{u + 2}", i - 1)
                        last = dve.scalar_tensor_tensor(out=ab[:, u % 2, :], in0=dist[:], scalar=minus_slope[:, bass.ds(4 * i + u, 1)],
                                                        in1=far[:], op0=ALU.mult, op1=ALU.add)
                    elif kind == "sa":
                        after(b_pe, f"s{u}", i)
                        own(f"ab{u}", i)
                        if u >= 2:
                            after(b_act, f"p{u - 2}", i)
                        else:
                            after(b_act, f"p{u + 2}", i - 1)
                        last = dve.tensor_tensor(sm2[:, u % 2, 0, P:], ps[:, 2 * (u % 2), P:2 * P], ab[:, u % 2, P:], ALU.add)
                    elif kind == "sb":
                        last = dve.tensor_tensor(sm2[:, u % 2, 1:, :], ps[:, 2 * (u % 2):2 * (u % 2) + 2, :]
                                                 .rearrange("p a (b c) -> p (a b) c", b=2)[:, 1:, :],
                                                 ab[:, u % 2, :].unsqueeze(1).to_broadcast([P, 3, 256]), ALU.add)
                    elif kind == "mx":
                        own(f"sb{u}", i)
                        last = dve.tensor_reduce(st2[:, 48 + u % 2 * 4:52 + u % 2 * 4], sm2[:, u % 2, :, :], AX_X, ALU.max)
                    elif kind == "ng":
                        own(f"mx{u}", i)
                        last = dve.tensor_scalar(neg, st2[:, 48 + u % 2 * 4:52 + u % 2 * 4], sinks[:, bass.ds(4 * i + u, 1)], -1.0,
                                                 ALU.max, ALU.mult)
                    elif kind == "den":
                        after(b_act, f"p{u}", i)
                        last = dve.tensor_tensor(st2[:, 56:60], st2[:, 8 * u + 4:8 * u + 8], st2[:, 32 + 4 * u:36 + 4 * u], ALU.add)
                    elif kind == "rec":
                        own(f"den{u}", i)
                        last = dve.reciprocal(st2[:, 60:64], st2[:, 56:60])
                    else:
                        after(b_pe, f"o{u}", i)
                        own(f"rec{u}", i)
                        last = dve.tensor_tensor(o_tok[:, :, bass.ds(256 * i + HD * u, HD)],
                                                 ps[:, 6 + u % 2, 0:256].rearrange("p (n d) -> p n d", n=NT),
                                                 st2[:, 60:64].unsqueeze(2).to_broadcast([P, NT, HD]), ALU.mult)
                    last.then_inc(b_dve.sem, b_dve.mark(step))
            for k in k8:
                after(bo_act, f"h{k}")
                dve.tensor_tensor(ul[:, k, :], bank(4 + k % 4), uh[:, k, :].bitcast(F32), ALU.subtract)\
                   .then_inc(bo_dve.sem, bo_dve.mark(f"l{k}"))
            added("o2", "b_o")
            norm(6)
            normed(6, 6, "f_norm1", ul)
            ffn(2)
            norm(7)
            for k in k8:
                dve.wait_ge(norm_act.sem, norm_act.value("rs", 7))
                h_wait(dve, 7, k)
                dve.scalar_tensor_tensor(out=out_t[:, k, :], in0=h[:, k, :], scalar=column("final_norm", k), in1=rs[:],
                                         op0=ALU.mult, op1=ALU.mult).then_inc(out_made, 1)

            for n in ch:
                dve.wait_ge(fin_pe.sem, fin_pe.value(f"t{n}"))
                dve.tensor_copy(x_in[:, n, :], ps[:, 4 + 2 * (n % 2):6 + 2 * (n % 2), :].rearrange("p a b -> p (a b)"))\
                   .then_inc(fin_dve.sem, fin_dve.mark(f"c{n}"))


_INS = ["x", "norm_mix", "w_in", "pool_mix", "pool_scale", "f_bias", "ssd_conv_w", "ssd_conv_b",
        "ssd_dt_bias", "ssd_a_log", "ssd_d", "ssd_norm", "p_pool", "p_attn", "p_ssd", "w_out",
        "norm_ffn", "ffn_up", "ffn_conv_w", "ffn_conv_b", "ffn_down", "norm_final",
        "a_norm_2", "a_w_in_2", "a_conv_w_2", "a_A_log_2", "a_dt_bias_2", "a_onorm_2", "a_w_out_2",
        "kv_norm_2", "kv_w_2", "kv_b_2", "b_norm_2", "b_w_q_2", "b_b_q_2", "b_sinks_2",
        "b_w_o_2", "b_b_o_2", "f_norm_2", "f_w_up_2", "f_conv_w_2", "f_conv_b_2", "f_w_down_2",
        "final_norm_2"]
_OUTS = [((1, S, D), "float32")]


def kernel(**inputs):
    import numpy as _np
    import concourse.bacc as _bacc
    from concourse import mybir as _mybir
    from concourse.bass_utils import run_bass_kernel_spmd as _run

    nc = _bacc.Bacc("TRN2", target_bir_lowering=False, num_devices=1)
    arrays, args = {}, []
    for name in _INS:
        a = _np.ascontiguousarray(inputs[name])
        arrays[f"in_{name}_dram"] = a
        args.append(nc.dram_tensor(f"in_{name}_dram", a.shape, _mybir.dt.from_np(a.dtype), kind="ExternalInput").ap())
    for i, (shape, dtype) in enumerate(_OUTS):
        dt = _mybir.dt.from_np(_np.dtype(dtype))
        args.append(nc.dram_tensor(f"out_{i}_dram", shape, dt, kind="ExternalOutput").ap())
    layered_mixers(nc, *args)
    r = _run(nc, [arrays], core_ids=[0])
    got = tuple(r.results[0][f"out_{i}_dram"] for i in range(len(_OUTS)))
    return got[0]
```

```python
from contextlib import ExitStack

import concourse.bass as bass
import concourse.mybir as mybir

F32 = mybir.dt.float32
F32R = mybir.dt.float32r
BF16 = mybir.dt.bfloat16
ALU = mybir.AluOpType
ACT = mybir.ActivationFunctionType
AX_X = mybir.AxisListType.X

P = 128
S = 512
D = 1024
KT = D // P
NT = S // P
EPS = 1e-6
MASKED = -1e30

POOL_W, ATT_W, SSD_W = 512, 512, 1024
ATT_HEADS, SSD_HEADS, SSD_GROUPS, HD = 8, 16, 2, 64
WINDOWS = (2, 4, 8, 16)
PADV = 16
XBC = SSD_W + 2 * SSD_GROUPS * P
XT = XBC // P
C_POOL, C_Q, C_V, C_F = 0, 512, 1536, 2048
C_Z = 2056
C_XBC = C_Z + SSD_W
C_DT = C_XBC + XBC
C_GATE = C_DT + SSD_HEADS
FFN = 2816
FT = FFN // P
DN_HEADS = 8
A_QKV, A_V = 3072, 1024
SWA_HEADS, KV_HEADS = 16, 4

PHASES = (
    ("xbc", 6, "std"), ("z", 4, "std"), ("pool", 2, "std"), ("qk", 4, "std"), ("v", 2, "tok"),
    ("gate0", 4, "std"), ("proj_pool", 2, "half"), ("gate1", 4, "std"), ("proj_attn", 2, "half"),
    ("gate2", 4, "std"), ("proj_ssd", 4, "std"), ("w_out", 4, "std"),
    ("up0", 22, "std"), ("down0", 11, "down"),
    ("a_qkv", 12, "std"), ("a_gate", 4, "std"), ("a_out", 4, "std"),
    ("up1", 22, "std"), ("down1", 11, "down"),
    ("kv_k", 1, "std"), ("kv_v", 1, "tok"), ("q2", 4, "std"), ("o2", 4, "std"),
    ("up2", 22, "std"), ("down2", 11, "down"),
)


class Phase:

    def __init__(self, name, quads, kind, first, fills):
        self.name, self.quads, self.kind, self.first, self.fills = name, quads, kind, first, fills


def plan():
    out, first, fills = {}, 0, 0
    pair = 0
    counts = [0, 0]
    for name, quads, kind in PHASES:
        out[name] = Phase(name, quads, kind, first, tuple(counts))
        first += quads
        if kind == "half":
            counts = [counts[0] + quads, counts[1] + quads]
        elif kind == "down":
            counts = [counts[0] + 1, counts[1] + 1]
        elif quads == 1:
            counts[1 if name == "kv_v" else 0] += 1
        else:
            counts = [counts[0] + quads // 2, counts[1] + quads // 2]
    return out, first


PLAN, QUADS = plan()


class Events:

    def __init__(self, sem, names, seed=0):
        self.sem, self.names, self.seed, self.next = sem, list(names), seed, 0
        self.at = {n: i for i, n in enumerate(self.names)}
        assert len(self.at) == len(self.names)

    def mark(self, name):
        assert self.names[self.next] == name, (self.names[self.next], name)
        self.next = (self.next + 1) % len(self.names)
        return 1

    def value(self, name, turn=0):
        return turn * len(self.names) + (self.seed + self.at[name] + 1)


def layered_mixers(nc, x, norm_mix, w_in, pool_mix, pool_scale, f_bias, ssd_conv_w, ssd_conv_b,
                   ssd_dt_bias, ssd_a_log, ssd_d, ssd_norm, p_pool, p_attn, p_ssd, w_out,
                   norm_ffn, ffn_up, ffn_conv_w, ffn_conv_b, ffn_down, norm_final,
                   a_norm_2, a_w_in_2, a_conv_w_2, a_A_log_2, a_dt_bias_2, a_onorm_2, a_w_out_2,
                   kv_norm_2, kv_w_2, kv_b_2, b_norm_2, b_w_q_2, b_b_q_2, b_sinks_2,
                   b_w_o_2, b_b_o_2, f_norm_2, f_w_up_2, f_conv_w_2, f_conv_b_2, f_w_down_2,
                   final_norm_2, out):
    ctx = ExitStack()
    with ctx:
        def sem(name):
            return ctx.enter_context(nc.semaphore(name))

        place, place_of = [nc.sbuf_base], {}
        place[0] = (place[0] + 63) // 64 * 64

        def fixed(name, shape, dt=F32):
            size = 2 if dt == BF16 else 4
            for n in shape[1:]:
                size *= n
            place_of[name] = place[0]
            t = nc.alloc_sbuf_tensor_at(name, shape, dt, offset=place[0])
            place[0] += (size + 31) // 32 * 32
            return t

        raw = fixed("raw", [P, 4, 512])
        whi = fixed("whi", [P, 4, 512], F32R)
        wlo = fixed("wlo", [P, 4, 512], F32R)
        h = fixed("h", [P, KT, S])
        uh = fixed("uh", [P, KT, S], F32R)
        ul = fixed("ul", [P, KT, S], F32R)
        ident = fixed("ident", [P, P])
        ones = fixed("ones", [P, P])
        ident_bf = fixed("ident_bf", [P, P], BF16)
        mask_q = fixed("mask_q", [P, P], BF16)
        upto = fixed("upto", [P, P])
        last_row = fixed("last_row", [P, P])
        keep = fixed("keep", [48, S])
        par = fixed("par", [P, 9, P])
        inv_count = fixed("inv_count", [P, 16])
        sgn = fixed("sgn", [48, 1])
        sgn_bias = fixed("sgn_bias", [48, 2])
        raw_bias = fixed("raw_bias", [48, 2])
        a_log = fixed("a_log", [48, 2])
        row_scale = fixed("row_scale", [48, 2])
        d_skip = fixed("d_skip", [P, KT])
        tok = fixed("tok", [P, 2, NT, 48])
        decay_end = fixed("decay_end", [P, NT, 48])
        chunk_decay = fixed("chunk_decay", [P, NT, 48])
        stat = fixed("stat", [P, 64])
        rc, rs = stat[:, 44:48], stat[:, 48:52]
        level = fixed("level", [P, 7, P], BF16)
        dist = fixed("dist", [P, 2 * P], BF16)
        far = fixed("far", [P, 2 * P], BF16)
        minus_slope = fixed("minus_slope", [P, SWA_HEADS])
        sinks = fixed("sinks", [P, SWA_HEADS])
        seed = fixed("seed", [1, 64])
        area = place[0]
        room = nc.sbuf_usable_end - area

        def at(name, shape, kb, dt=F32):
            size = 2 if dt == BF16 else 4
            for n in shape[1:]:
                size *= n
            off = int(kb * 1024)
            assert off + size <= room, (name, off + size, room)
            return nc.alloc_sbuf_tensor_at(name, shape, dt, offset=area + off)

        sq = at("sq", [P, KT, S], 104)
        uf = at("uf", [P, 2, S], 10)
        mean = at("mean", [1, S], 14)
        ws = at("ws", [P, KT, 48], 80)
        wsh = at("wsh", [P, KT, 48], 82, F32R)
        wsl = at("wsl", [P, KT, 48], 84, F32R)
        sc = at("sc", [48, 10, S], 56)
        cs = at("cs", [48, S], 117)
        x_in = at("x_in", [P, NT, D], 24)
        out_t = at("out_t", [P, KT, S], 40)
        par_in = at("par_in", [P, 9, P], 60)

        cv = at("cv", [P, 4, S], 92)
        xc = at("xc", [P, XT, S], 0)
        xd = at("xd", [P, NT, SSD_W], 24)
        xdd = at("xdd", [P, SSD_W], 40)
        st = at("st", [P, 3, SSD_W], 44)
        bt = at("bt", [P, 2 * P], 56)
        stq = at("stq", [P, SSD_W], 57)
        y_tok = at("y_tok", [P, NT, SSD_W], 61)
        zs = at("zs", [P, KT, S], 77)
        cb = at("cb", [P, SSD_GROUPS, S], 93)
        dd = at("dd", [P, 2, S], 97)
        mt = at("mt", [P, 2, S], 101)
        ec = at("ec", [P, 2, S], 105)
        ce = at("ce", [P, 2, S], 109)
        oh = at("oh", [48, 2, S], 113)
        ysh = at("ysh", [P, KT, S], 24, F32R)
        ysl = at("ysl", [P, KT, S], 40, F32R)
        ysq = at("ysq", [P, 2, S], 97)
        yms = at("yms", [P, 2, S], 101)
        yrs = at("yrs", [P, 2, S], 105)
        yf = at("yf", [P, 2, S], 109)
        pv = at("pv", [P, 4, PADV + S], 0)
        win = at("win", [P, 2, PADV + S], 9)
        dp = at("dp", [P, 4, S], 16)
        yph = at("yph", [P, 4, S], 100, F32R)
        ypl = at("ypl", [P, 4, S], 108, F32R)
        mix = at("mix", [P, 4, P], 58)
        qk = at("qk", [P, KT, S], 62)
        v = at("v", [P, NT, ATT_W], 78)
        oa = at("oa", [P, NT, ATT_W], 86)
        qs = at("qs", [P, S], 0)
        ks = at("ks", [P, S], 96)
        nb = at("nb", [P, 2, S], 2)
        sm = at("sm", [P, 2, S], 6)
        pe_ = at("probs", [P, 2, S], 10)
        pt = at("pt", [P, 2, S], 56)
        ohc = at("ohc", [48, S], 14)
        yah = at("yah", [P, 4, S], 16, F32R)
        yal = at("yal", [P, 4, S], 78, F32R)
        gt = at("gt", [P, KT, S], 0)
        mg = at("mg", [P, KT, S], 62)
        tmp = at("tmp", [P, 2, S], 56)

        fh = at("fh", [P, FT, S], 0, F32R)
        fl = at("fl", [P, FT, S], 44, F32R)
        fc = at("fc", [P, 4, S], 88)
        fg = at("fg", [P, 2, S], 96)
        ff = at("ff", [P, 2, S], 100)

        ac = at("ac", [P, 24, S], 0)
        ga = at("ga", [P, KT, S], 48)
        acv = at("acv", [P, 4, S], 88)
        asq = at("asq", [P, 8, S], 96)
        qk_sums = at("qk_sums", [16, S], 112)
        pick = at("pick", [P, 31], 114)

        def head_tiles(name, start, cols=S):
            return [at(f"{name}{e}", [P, cols], start + 28 * e) for e in range(2)]

        kf, vf, qf = head_tiles("kf", 64), head_tiles("vf", 66), head_tiles("qf", 68)
        kn, vb, qn = head_tiles("kn", 70), head_tiles("vb", 72), head_tiles("qn", 74)
        kb, kbe, kd = head_tiles("kb", 76), head_tiles("kbe", 78), head_tiles("kd", 80)
        em, eg = head_tiles("em", 82), head_tiles("eg", 84)
        ti, tt, vn = head_tiles("ti", 86), head_tiles("tt", 88), head_tiles("vn", 90)
        kt, kbt, qt, ltk, an, lt, xi, nkc = kf, vf, qf, vn, qn, kb, em, vf
        over_uh, over_ul = place_of["uh"], place_of["ul"]

        def over(name, shape, offset):
            return nc.alloc_sbuf_tensor_at(name, shape, F32, offset=over_ul + offset)

        ot = nc.alloc_sbuf_tensor_at("ot", [P, NT, A_V], F32, offset=over_uh)
        goh, cs2 = over("goh", [48, 2, S], 0), over("cs2", [48, S], 4096)
        beta, egc, bege = (over(n, [P, NT, 8], 6144 + 128 * i) for i, n in enumerate(("beta", "egc", "bege")))
        rn, rn2 = over("rn", [P, NT, 16], 6528), over("rn2", [P, NT, 16], 6784)
        oss, oss2 = over("oss", [P, NT, 8], 7040), over("oss2", [P, NT, 8], 7168)
        sg = [over(f"sg{e}", [P, P], 7296 + 512 * e) for e in range(2)]
        osq = at("osq", [P, 2, A_V], 64)
        ayf = at("ayf", [P, 2, S], 72)
        ayh = at("ayh", [P, KT, S], 0, F32R)
        ayl = at("ayl", [P, KT, S], 16, F32R)

        ubh = at("ubh", [P, KT, S], 16, F32R)
        ubl = at("ubl", [P, KT, S], 32, F32R)
        kk = at("kk", [P, KV_HEADS, S], 48)
        vv = at("vv", [P, NT, 256], 56)
        q2 = at("q2", [P, KT, S], 60)
        o_tok = at("o_tok", [P, NT, D], 76)
        qst = at("qst", [P, 2, S], 92)
        kst = at("kst", [P, S], 96)
        sm2 = at("sm2", [P, 2, NT, 256], 98)
        pr2 = at("pr2", [P, 2, NT, 256], 106)
        pt2 = at("pt2", [P, 7, P], 114)
        kraw = at("kraw", [P, 2, S], 114)
        ab = at("ab", [P, 2, 256], 10)
        vbias = at("vbias", [P, 256], 14)
        st2 = at("st2", [P, 64], 15)
        ps = ctx.enter_context(nc.psum_tensor("ps", [P, 8, 512], F32))

        raw_landed = [sem(f"raw_landed{j}") for j in range(4)]
        hi_ready, lo_ready, pe_used = sem("hi_ready"), sem("lo_ready"), sem("pe_used")
        lin_free = [sem("lin_free0"), sem("lin_free1")]
        consts_ready, later_ready, seeded = sem("consts_ready"), sem("later_ready"), sem("seeded")
        x_landed, par_landed, small_landed, mix_landed = (
            sem("x_landed"), sem("par_landed"), sem("small_landed"), sem("mix_landed"))
        stored, sinks_landed = sem("stored"), sem("sinks_landed")
        k8 = range(KT)
        prep_dve = Events(sem("prep_dve"), ["par0", "par1", "par2", "wsh", "wsl", "sgn_bias", "a_neg"])
        prep_act = Events(sem("prep_act"), ["a_exp"])
        x_pe = Events(sem("x_pe"), ["par0", "par1", "par2"] + [f"x{k}" for k in k8])
        x_ready, renormed = sem("x_ready"), sem("renormed")
        h_low = sem("h_low")
        norm_act = Events(sem("norm_act"), [f"sq{k}" for k in k8] + ["rs"])
        norm_pe = Events(sem("norm_pe"), [f"sum{k}" for k in k8] + ["turned", "row"])
        norm_dve = Events(sem("norm_dve"), ["mean", "rc"])
        u_act = Events(sem("u_act"), [f"uh{k}" for k in k8])
        u_dve = Events(sem("u_dve"), ["u0"] + sum([[f"u{k + 1}", f"ul{k}"] for k in range(KT - 1)], []) + ["ul7"])
        sc_pe = Events(sem("sc_pe"), ["logits", "turned", "last"])
        sc_act = Events(sem("sc_act"), ["exp", "ln", "decay", "chunk"])
        sc_dve = Events(sem("sc_dve"), ["t", "abs", "one", "w", "eq", "den", "inv", "num", "q", "r",
                                        "sp", "scaled", "sums", "tok", "end"])
        conv_act = Events(sem("conv_act"), ["t0", "t1", "s0", "s1", "t2", "t3", "s2", "s3"], seed=8)
        conv_dve = Events(sem("conv_dve"), ["a0", "a1", "b0", "b1", "a2", "a3", "b2", "b3"], seed=8)
        ffn_act = Events(sem("ffn_act"), ["t0", "t1", "s0", "s1", "t2", "t3", "fh0", "fh1"], seed=8)
        ffn_dve = Events(sem("ffn_dve"), ["a0", "a1", "a2", "a3", "hf0", "hf1", "fl0", "fl1"], seed=8)
        ch = range(NT)
        ssd_pe = Events(sem("ssd_pe"), ["cb0", "cb1"] + sum([[f"x{c}", f"b{c}", f"state{c}_0", f"state{c}_1"]
                                                             for c in range(3)], []) + ["x3"])
        ssd_dve = Events(sem("ssd_dve"), ["cb0", "cb1", "xd0", "b0", "xdd0", "st0"]
                         + ["xd1", "b1", "xdd1", "dec1", "st1", "xd2", "b2", "xdd2", "dec2", "st2", "xd3"])
        sh_pe = Events(sem("sh_pe"), ["row0", "row1", "y0", "y1"], seed=4)
        sh_act = Events(sem("sh_act"), ["e0", "r0", "e1", "r1", "y0", "y1"], seed=6)
        sh_dve = Events(sem("sh_dve"), ["oh0", "oh1", "d0", "d1", "m0", "c0", "m1", "c1"], seed=8)
        sy_pe = Events(sem("sy_pe"), ["t0", "t1"] + sum([[f"t{k + 2}", f"sum{k}"] for k in range(6)], [])
                       + ["sum6", "sum7"])
        sy_act = Events(sem("sy_act"), [f"sq{k}" for k in k8] + ["rs0", "rs1"] + [f"h{k}" for k in k8])
        sy_dve = Events(sem("sy_dve"), sum([[f"w{k}", f"g{k}"] for k in k8], []) + ["ms0", "rc0", "ms1", "rc1"]
                        + ["f0"] + sum([[f"f{k + 1}", f"l{k}"] for k in range(7)], []) + ["l7"])
        po_act = Events(sem("po_act"), [f"h{g}" for g in range(4)])
        po_dve = Events(sem("po_dve"), ["pad"] + sum([[f"s{g}_{n}" for n in range(g + 1)] + [f"d{g}", f"q{g}", f"e{g}"]
                                             for g in range(4)], []) + [f"l{g}" for g in range(4)])
        po_pe = Events(sem("po_pe"), [f"y{g}" for g in range(4)])
        at_names = lambda kinds, u: [f"{u // 4}{k}{u % 4}" for k in kinds]
        AT_PE = (["0bc"] + at_names("s", 0) + at_names("s", 1) + at_names("s", 2) + ["1bc"] + at_names("t", 0) + at_names("s", 3)
                 + sum([at_names("t", u) + at_names("o", u - 1) + (at_names("s", u + 3) if u < 5 else []) for u in range(1, 8)], [])
                 + at_names("o", 7))
        AT_ACT = at_names("p", 0) + sum([at_names("p", u) + at_names("c", u - 1) for u in range(1, 8)], []) + at_names("c", 7)
        AT_DVE = (["0oh", "0nb", "1oh"] + at_names("sxm", 0) + at_names("sxm", 1) + ["1nb"]
                  + sum([at_names("sxm", u) + at_names("ro", u - 2) for u in range(2, 8)], [])
                  + at_names("ro", 6) + at_names("ro", 7))
        at_pe = Events(sem("at_pe"), AT_PE, seed=len(AT_PE))
        at_act = Events(sem("at_act"), ["qs", "ks"] + AT_ACT, seed=2 + len(AT_ACT))
        at_dve = Events(sem("at_dve"), AT_DVE, seed=len(AT_DVE))
        ay_pe = Events(sem("ay_pe"), [f"t{k}" for k in range(4)])
        ay_act = Events(sem("ay_act"), [f"h{k}" for k in range(4)])
        ay_dve = Events(sem("ay_dve"), [f"l{k}" for k in range(4)])
        mg_dve = Events(sem("mg_dve"), ["m0", "m1", "m2", "m3"], seed=4)
        mg_act = Events(sem("mg_act"), ["h0", "h1"])
        mg_low = Events(sem("mg_low"), ["l0", "l1"])

        fin_pe = Events(sem("fin_pe"), [f"t{n}" for n in ch])
        fin_dve = Events(sem("fin_dve"), [f"c{n}" for n in ch])
        made = sem("made")
        TAPS = {"xbc": XT}
        prep_dve2 = Events(sem("prep_dve2"), ["zero", "wsh", "wsl"])
        GP = (["row", "rk", "rv", "rq", "tk", "tb", "tq", "prod", "prq", "t0"]
              + sum([[f"x{k}", f"t{k}", f"tt{k}"] for k in range(1, 6)], [])
              + ["x6", "tt6", "nk", "v0", "o0", "s0", "v1", "o1", "s1", "v2", "o2", "s2", "v3", "o3"])
        GA = (["stk", "stv", "stq", "eg", "vb", "em", "kt", "kbt", "qt", "ti0"] + [f"ti{k}" for k in range(1, 6)]
              + ["nkc", "vn0", "vn1", "vn2", "vn3"])
        GD = (["goh", "kn", "kb", "qn", "d", "lt", "i0", "tt0", "ltk1", "mask", "an"]
              + sum([[f"xi{k}"] + ([f"ltk{k + 1}"] if k < 6 else []) + [f"tt{k}"] + {1: ["kbe"], 2: ["kd"], 3: ["qd"]}.get(k, [])
                     for k in range(1, 7)], []) + ["s0", "s1", "s2", "ot"])
        def halves(t, k, which):
            return t.rearrange("p (n two b) -> p n two b", two=2, b=1 << k)[:, :, which, :]

        both = lambda steps: [f"{e}{s}" for s in steps for e in range(2)]
        g_pe = Events(sem("g_pe"), both(GP), seed=2 * len(GP))
        g_act = Events(sem("g_act"), both(GA), seed=2 * len(GA))
        g_dve = Events(sem("g_dve"), both(GD), seed=2 * len(GD))
        gn_pe = Events(sem("gn_pe"), [f"n{t}" for t in range(16)] + ["nt"] + [f"t{k}" for k in k8])
        gn_act = Events(sem("gn_act"), [f"sq{t}" for t in range(16)] + ["beta", "egc", "rt"] + [f"q{n}" for n in ch] + ["or"]
                        + [f"h{k}" for k in k8])
        gn_dve = Events(sem("gn_dve"), ["zeros", "pick", "cs", "ns", "nr", "qs", "bege"] + [f"red{n}" for n in ch] + ["om", "orc"]
                        + [f"sc{n}" for n in ch] + ["f0"] + sum([[f"f{k + 1}", f"l{k}"] for k in range(7)], []) + ["l7"])
        NH = 8
        BP = ["s0", "s1", "t0", "s2"] + sum([[f"t{u}", f"o{u - 1}"] + ([f"s{u + 2}"] if u < 6 else []) for u in range(1, 8)], []) + ["o7"]
        BA = ["st0", "p0"] + sum([[f"p{u}", f"c{u - 1}"] + (["st1"] if u == 2 else []) for u in range(1, 8)], []) + ["c7"]
        score = lambda u: [f"ab{u}", f"sa{u}", f"sb{u}", f"mx{u}", f"ng{u}"]
        finish = lambda u: [f"den{u}", f"rec{u}", f"o{u}"]
        BD = score(0) + score(1) + sum([score(u) + finish(u - 2) for u in range(2, 8)], []) + finish(6) + finish(7)
        b_pe = Events(sem("b_pe"), BP, seed=len(BP))
        b_act = Events(sem("b_act"), BA, seed=len(BA))
        b_dve = Events(sem("b_dve"), BD, seed=len(BD))
        kv_dve = Events(sem("kv_dve"), ["far"] + [f"k{n}" for n in range(8)])
        bo_pe = Events(sem("bo_pe"), [f"t{k}" for k in k8])
        bo_act = Events(sem("bo_act"), [f"h{k}" for k in k8])
        bo_dve = Events(sem("bo_dve"), [f"l{k}" for k in k8])
        vbias_landed = sem("vbias_landed")
        out_made = sem("out_made")
        TAPS["a_qkv"] = 24

        def as_rows(src):
            if len(src.shape) == 1:
                return src.rearrange("(r c) -> r c", c=P)
            return src.rearrange("a (r c) -> a r c", c=P).rearrange("a r c -> (a r) c")

        def std_value(ph, p, turn, c=1):
            return 2 * turn + (2 * PLAN[ph].fills[p] + 3 + c)

        def h_wait(eng, update, k):
            name = ("x", "w_out", "down0", "renormed", "a_out", "down1", "o2", "down2")[update]
            if update == 0:
                eng.wait_ge(x_ready, k + 1)
            elif name == "renormed":
                eng.wait_ge(renormed, k + 1)
            elif name.startswith("down"):
                if k < 4:
                    eng.wait_ge(h_low, 4 * int(name[4]) + k + 1)
                else:
                    eng.wait_ge(lin_free[k // 2 - 2], std_value(name, k // 2 - 2, 0, k % 2))
            else:
                g = k // 2
                eng.wait_ge(lin_free[g % 2], std_value(name, g % 2, g // 2, k % 2))

        ROWS = (
            (("norm_mix", norm_mix[0], 8), ("norm_ffn", norm_ffn[0], 8), ("norm_final", norm_final, 8),
             ("ssd_norm", ssd_norm[0], 8), ("pool_scale", pool_scale[0], 4), ("ssd_conv_b", ssd_conv_b[0], XT),
             ("ssd_conv_w", ssd_conv_w[0], 4 * XT)),
            (("a_norm", a_norm_2[0], 8), ("kv_norm", kv_norm_2, 8), ("b_norm", b_norm_2[0], 8),
             ("f_norm0", f_norm_2[0], 8), ("f_norm1", f_norm_2[1], 8), ("final_norm", final_norm_2, 8),
             ("kv_b", kv_b_2, 4), ("b_q", b_b_q_2[0], 8), ("b_o", b_b_o_2[0], 8), ("onorm", a_onorm_2[0], 1)),
            (("a_conv_w", a_conv_w_2[0], 96),),
            (("f0w", ffn_conv_w[0, 0:2], 88),), (("f0b", ffn_conv_w[0, 2], 44), ("f0c", ffn_conv_b[0], 44)),
            (("f1w", f_conv_w_2[0, 0:2], 88),), (("f1b", f_conv_w_2[0, 2], 44), ("f1c", f_conv_b_2[0], 44)),
            (("f2w", f_conv_w_2[1, 0:2], 88),), (("f2b", f_conv_w_2[1, 2], 44), ("f2c", f_conv_b_2[1], 44)),
        )
        COL = {}
        for n, rows in enumerate(ROWS):
            r0 = 0
            for name, _, rows_n in rows:
                COL[name] = (n, r0)
                r0 += rows_n

        def column(name, t):
            n, r0 = COL[name]
            return par[:, n, r0 + t:r0 + t + 1] if isinstance(t, int) else par[:, n, bass.ds(t + r0, 1)]

        def bank(b):
            return ps[:, b, :]

        seeded_events = [conv_act, conv_dve, ffn_act, ffn_dve, sh_pe, sh_act, sh_dve, at_pe, at_act, at_dve, mg_dve]
        seeded_events += [g_pe, g_act, g_dve, b_pe, b_act, b_dve]
        block = ctx.enter_context(nc.Block())

        @block.sync
        def _(sp):
            def std(ph, w, col):
                with sp.Fori(0, PLAN[ph].quads) as i:
                    for j in range(4):
                        sp.wait_ge(lo_ready, 4 * i + (4 * PLAN[ph].first + j + 1))
                        src = w[256 * j:256 * (j + 1), bass.ds(256 * i + col, 256)]
                        sp.dma_start(raw[:, j, :].rearrange("p (a c) -> p a c", a=2),
                                     src.rearrange("(a p) c -> p a c", p=P)).then_inc(raw_landed[j], 16)

            def half(ph, w):
                with sp.Fori(0, PLAN[ph].quads) as i:
                    for j in range(4):
                        sp.wait_ge(lo_ready, 4 * i + (4 * PLAN[ph].first + j + 1))
                        r = 256 * (j % 2)
                        src = w[r:r + 256, bass.ds(512 * i + 256 * (j // 2), 256)]
                        sp.dma_start(raw[:, j, :].rearrange("p (a c) -> p a c", a=2),
                                     src.rearrange("(a p) c -> p a c", p=P)).then_inc(raw_landed[j], 16)

            def down(ph, w):
                with sp.Fori(0, PLAN[ph].quads) as i:
                    for j in range(4):
                        sp.wait_ge(lo_ready, 4 * i + (4 * PLAN[ph].first + j + 1))
                        src = w[bass.ds(256 * i + P * (j % 2), P), 512 * (j // 2):512 * (j // 2) + 512]
                        sp.dma_start(raw[:, j, :], src).then_inc(raw_landed[j], 16)

            def up(ph, w):
                with sp.Fori(0, PLAN[ph].quads // 2) as i:
                    for g in range(2):
                        for j in range(4):
                            sp.wait_ge(lo_ready, 8 * i + (4 * (PLAN[ph].first + g) + j + 1))
                            src = w[256 * j:256 * (j + 1), bass.ds(256 * i + FFN * g, 256)]
                            sp.dma_start(raw[:, j, :].rearrange("p (a c) -> p a c", a=2),
                                         src.rearrange("(a p) c -> p a c", p=P)).then_inc(raw_landed[j], 16)

            sp.wait_ge(seeded, 1)
            for n in range(NT):
                sp.dma_start(x_in[:, n, :], x[0, n * P:(n + 1) * P, :]).then_inc(x_landed, 16)
            w = w_in[0]
            std("xbc", w, C_XBC)
            std("z", w, C_Z)
            std("pool", w, C_POOL)
            std("qk", w, C_Q)
            std("v", w, C_V)
            std("gate0", w, C_GATE)
            half("proj_pool", p_pool[0])
            std("gate1", w, C_GATE + D)
            half("proj_attn", p_attn[0])
            std("gate2", w, C_GATE + 2 * D)
            std("proj_ssd", p_ssd[0], 0)
            std("w_out", w_out[0], 0)
            up("up0", ffn_up[0])
            down("down0", ffn_down[0])
            std("a_qkv", a_w_in_2[0], 0)
            std("a_gate", a_w_in_2[0], A_QKV)
            std("a_out", a_w_out_2[0], 0)
            up("up1", f_w_up_2[0])
            down("down1", f_w_down_2[0])
            std("kv_k", kv_w_2, 0)
            std("kv_v", kv_w_2, 256)
            std("q2", b_w_q_2[0], 0)
            std("o2", b_w_o_2[0], 0)
            up("up2", f_w_up_2[1])
            down("down2", f_w_down_2[1])
            sp.wait_ge(fin_dve.sem, fin_dve.value("c3"))
            sp.dma_start(out[0].rearrange("(n p) c -> p n c", p=P), x_in[:]).then_inc(stored, 16)
            sp.wait_ge(stored, 16)

        @block.gpsimd
        def _(pool):
            for at_, (s, n) in enumerate(((lo_ready, 4), (pe_used, 4), (lin_free[0], 2), (lin_free[1], 2),
                         *((e.sem, e.seed) for e in seeded_events))):
                pool.memset(seed[:, at_:at_ + 1], 0.0).then_inc(s, n)
            pool.memset(seed[:, 62:63], 0.0).then_inc(seeded, 1)

            def chosen(t, pattern, base, mult, op, fill, source=None):
                pool.affine_select(out=t, in_=t if source is None else source, pattern=pattern, base=base,
                                   channel_multiplier=mult, compare_op=op, fill=fill).then_inc(made, 1)

            made_n = 0
            pool.memset(ident[:], 0.0).then_inc(made, 1)
            pool.memset(ident_bf[:], 0.0).then_inc(made, 1)
            pool.memset(mask_q[:], 0.0).then_inc(made, 1)
            pool.memset(upto[:], 1.0).then_inc(made, 1)
            pool.memset(last_row[:], 1.0).then_inc(made, 1)
            pool.memset(ones[:], 1.0).then_inc(made, 1)
            pool.memset(keep[:], 1.0).then_inc(made, 1)
            pool.memset(sgn[:], 1.0).then_inc(made, 1)
            pool.memset(raw_bias[:], 0.0).then_inc(made, 1)
            pool.memset(a_log[:], 0.0).then_inc(made, 1)
            pool.memset(par_in[:], 0.0).then_inc(made, 1)
            pool.memset(ws[:], 0.0).then_inc(made, 1)
            pool.wait_ge(made, 12)
            chosen(ident[:], [[-1, P]], 0, 1, ALU.not_equal, 1.0)
            chosen(ident_bf[:], [[-1, P]], 0, 1, ALU.not_equal, 1.0)
            chosen(mask_q[:], [[-1, P]], 0, 1, ALU.is_ge, MASKED)
            chosen(upto[:], [[1, P]], 0, -1, ALU.is_ge, 0.0)
            chosen(last_row[:], [[0, P]], 1 - P, 1, ALU.is_ge, 0.0)
            pool.wait_ge(made, 12 + 5)
            pool.memset(keep[32:48, 0:S:P], 0.0).then_inc(made, 1)
            pool.wait_ge(made, 12 + 6)
            pool.memset(sgn[0:8, :], -1.0).then_inc(made, 1)
            pool.wait_ge(made, 12 + 7)
            for j in range(16):
                pool.memset(inv_count[:, j:j + 1], 1.0 / (j + 1)).then_inc(made, 1)
            pool.wait_ge(made, 12 + 7 + 16)
            pool.memset(seed[:, 63:64], 0.0).then_inc(consts_ready, 1)

            pool.memset(level[:], 0.0).then_inc(made, 1)
            pool.iota(dist[:], pattern=[[-1, 2 * P]], base=P, channel_multiplier=1,
                      allow_small_or_imprecise_dtypes=True).then_inc(made, 1)
            pool.memset(far[:], 0.0).then_inc(made, 1)
            pool.wait_ge(made, 35 + 3)
            for k in range(7):
                b = 1 << k
                part = level[:, k, :].rearrange("p (n two b) -> p n two b", two=2, b=b)[:, :, 1, :]
                pool.memset(part, -1.0).then_inc(made, 1)
                pool.wait_ge(made, 35 + 4 + 3 * k)
                chosen(part, [[-2 * b, P // (2 * b)], [0, b]], 0, 1, ALU.is_ge, 0.0)
                pool.wait_ge(made, 35 + 5 + 3 * k)
                chosen(part, [[2 * b, P // (2 * b)], [0, b]], b - 1, -1, ALU.is_ge, 0.0)
                pool.wait_ge(made, 35 + 6 + 3 * k)
            chosen(far[:], [[-1, 2 * P]], P, 1, ALU.is_ge, MASKED)
            pool.wait_ge(made, 35 + 25)
            chosen(far[:], [[1, 2 * P]], -1, -1, ALU.is_ge, MASKED)
            pool.wait_ge(made, 35 + 26)
            for n in range(SWA_HEADS):
                pool.memset(minus_slope[:, n:n + 1], -2.0 ** (-8.0 * (n + 1) / SWA_HEADS)).then_inc(made, 1)
            pool.wait_ge(made, 35 + 26 + 16)
            pool.memset(seed[:, 61:62], 0.0).then_inc(later_ready, 1)

            with pool.Fori(0, QUADS) as q:
                for j in range(4):
                    pool.wait_ge(hi_ready, 4 * q + (j + 1))
                    pool.wait_ge(pe_used, 4 * q + (j + 1))
                    pool.tensor_tensor(wlo[:, j, :], raw[:, j, :], whi[:, j, :].bitcast(F32),
                                       ALU.subtract).then_inc(lo_ready, 1)

        def step_back(events, name, u, back, turn):
            if u >= back:
                w = u - back
                return events.value(f"{w // 4}{name}{w % 4}", turn)
            w = u - back + 8
            return events.value(f"{w // 4}{name}{w % 4}", turn - 1)

        @block.scalar
        def _(act):
            def split(i, off):
                for j in range(4):
                    act.wait_ge(raw_landed[j], 32 * i + 16 * (off + 1))
                    act.wait_ge(pe_used, 8 * i + (4 * off + j + 1))
                    act.activation(whi[:, j, :], raw[:, j, :], ACT.Copy).then_inc(hi_ready, 1)

            def split1(i, off):
                for j in range(4):
                    act.wait_ge(raw_landed[j], 16 * i + 16 * (off + 1))
                    act.wait_ge(pe_used, 4 * i + (4 * off + j + 1))
                    act.activation(whi[:, j, :], raw[:, j, :], ACT.Copy).then_inc(hi_ready, 1)

            def used(i, off):
                act.wait_ge(pe_used, 8 * i + (4 * off + 8))

            def squares(n, update, tiles=k8):
                for k in tiles:
                    h_wait(act, update, k)
                    act.activation(sq[:, k, :], h[:, k, :], ACT.Square).then_inc(norm_act.sem, norm_act.mark(f"sq{k}"))

            def root(n):
                act.wait_ge(norm_dve.sem, norm_dve.value("rc", n))
                act.activation(rs, rc, ACT.Sqrt).then_inc(norm_act.sem, norm_act.mark("rs"))

            def split_unit(quad_, j):
                act.wait_ge(raw_landed[j], 16 * (quad_ + 1))
                act.wait_ge(pe_used, 4 * quad_ + j + 1)
                act.activation(whi[:, j, :], raw[:, j, :], ACT.Copy).then_inc(hi_ready, 1)

            def splits_and_squares(ph, n):
                for q in range(4):
                    split_unit(PLAN[ph].first + q + 1, 0)
                    if q:
                        squares(n, n, (2 * q - 2, 2 * q - 1))
                    for j in range(1, 4):
                        split_unit(PLAN[ph].first + q + 1, j)
                squares(n, n, (6, 7))

            def upper(m, dst):
                for k in k8:
                    act.wait_ge(u_dve.sem, u_dve.value(f"u{k}", m))
                    act.activation(dst[:, k, :], uf[:, k % 2, :], ACT.Copy).then_inc(u_act.sem, u_act.mark(f"uh{k}"))

            def scalars(n):
                act.wait_ge(sc_dve.sem, sc_dve.value("abs", n))
                act.activation(sc[:, 2, :], sc[:, 1, :], ACT.Exp, scale=-1.0).then_inc(sc_act.sem, sc_act.mark("exp"))
                act.wait_ge(sc_dve.sem, sc_dve.value("one", n))
                act.activation(sc[:, 5, :], sc[:, 3, :], ACT.Ln).then_inc(sc_act.sem, sc_act.mark("ln"))

            def scalar_decays(n):
                act.wait_ge(sc_dve.sem, sc_dve.value("end", n))
                act.activation(decay_end[:], decay_end[:], ACT.Exp).then_inc(sc_act.sem, sc_act.mark("decay"))
                act.activation(chunk_decay[:].rearrange("p a b -> p (a b)"), ps[:, 6, 0:192],
                               ACT.Exp).then_inc(sc_act.sem, sc_act.mark("chunk"))

            def conv(ph, w_name, tap, b_name, silu_only_first, dst, turn0, buf):
                with act.Fori(0, PLAN[ph].quads // 2) as i:
                    for g in range(2):
                        split(i, PLAN[ph].first + g + 1)
                        used(i, PLAN[ph].first + g)
                        for c in range(2):
                            t = 4 * i + 2 * g + c
                            bias = column(b_name, t) if b_name else 0.0
                            act.activation(buf[:, 2 * g + c, :], bank(2 * g + c), ACT.Identity, bias=bias,
                                           scale=column(w_name, t + tap)).then_inc(conv_act.sem, conv_act.mark(f"t{2 * g + c}"))
                        for c in range(2):
                            t = 4 * i + 2 * g + c
                            act.wait_ge(lin_free[g], std_value(ph, g, i, c))
                            act.activation(dst[:, bass.ds(t, 1), :], buf[:, 2 * g + c, :].unsqueeze(1), ACT.Silu)\
                               .then_inc(conv_act.sem, conv_act.mark(f"s{2 * g + c}"))

            def out_of_banks(ph, put):
                with act.Fori(0, PLAN[ph].quads // 2) as i:
                    for g in range(2):
                        split(i, PLAN[ph].first + g + 1)
                        used(i, PLAN[ph].first + g)
                        put(ps[:, 2 * g:2 * g + 2, :], 2 * i + g).then_inc(lin_free[g], 2)

            def splits_only(ph, last=False):
                with act.Fori(0, PLAN[ph].quads - last) as i:
                    split1(i, PLAN[ph].first + 1)

            act.wait_ge(consts_ready, 1)
            for n, rows in enumerate(ROWS):
                r0 = 0
                for name, src, count in rows:
                    act.dma_start(par_in[r0:r0 + count, n, :], as_rows(src)).then_inc(par_landed, 16)
                    r0 += count
            fw, dw = w_in[0][:, C_F:C_F + 8], w_in[0][:, C_DT:C_DT + SSD_HEADS]
            act.dma_start(ws[:, :, 0:8], fw.rearrange("(k p) c -> p k c", p=P)).then_inc(small_landed, 16)
            act.dma_start(ws[:, :, 32:48], dw.rearrange("(k p) c -> p k c", p=P)).then_inc(small_landed, 16)
            act.dma_start(raw_bias[0:8, 0:1], f_bias.rearrange("a p -> p a")).then_inc(small_landed, 16)
            act.dma_start(raw_bias[32:48, 0:1], ssd_dt_bias.rearrange("a p -> p a")).then_inc(small_landed, 16)
            act.dma_start(raw_bias[32:40, 1:2], a_dt_bias_2.rearrange("a p -> p a")).then_inc(small_landed, 16)
            act.dma_start(a_log[32:48, 0:1], ssd_a_log.rearrange("a p -> p a")).then_inc(small_landed, 16)
            act.dma_start(a_log[32:40, 1:2], a_A_log_2.rearrange("a p -> p a")).then_inc(small_landed, 16)
            for e in range(2):
                act.dma_start(d_skip[64 * e:64 * e + 64, :], ssd_d[0, e:SSD_HEADS:2].partition_broadcast(64),
                              allow_slow_non_contiguous=True).then_inc(small_landed, 16)
            act.dma_start(sinks[:], b_sinks_2[0].partition_broadcast(P)).then_inc(sinks_landed, 16)
            act.wait_ge(small_landed, 16 * 9)
            act.activation(row_scale[:], a_log[:], ACT.Exp).then_inc(prep_act.sem, prep_act.mark("a_exp"))
            split(0, 0)

            squares(0, 0)
            root(0)
            upper(0, uh)
            scalars(0)
            conv("xbc", "ssd_conv_w", 3 * XT, "ssd_conv_b", None, xc, 0, cv)
            scalar_decays(0)
            for grp in range(SSD_GROUPS):
                with act.Fori(0, 2) as i:
                    z1 = PLAN["z"].first + 2 * grp
                    for s_ in range(2):
                        turn = 2 * i + (s_ + 4 * grp)
                        for e in range(2):
                            act.wait_ge(sh_dve.sem, sh_dve.value(f"d{e}", turn))
                            act.activation(dd[:, e, :], dd[:, e, :], ACT.Exp).then_inc(sh_act.sem, sh_act.mark(f"e{e}"))
                            act.wait_ge(sh_pe.sem, sh_pe.value(f"row{e}", turn))
                            act.wait_ge(sh_dve.sem, sh_dve.value(f"c{e}", turn - 1))
                            act.activation(ec[:, e, :], bank(4 + e), ACT.Exp).then_inc(sh_act.sem, sh_act.mark(f"r{e}"))
                        for e in range(2):
                            act.wait_ge(sh_pe.sem, sh_pe.value(f"y{e}", turn))
                            act.activation(y_tok[:, :, bass.ds(256 * i + (512 * grp + 128 * s_ + 64 * e), HD)],
                                           ps[:, 6 + e, 0:256].rearrange("p (n d) -> p n d", n=NT),
                                           ACT.Copy).then_inc(sh_act.sem, sh_act.mark(f"y{e}"))
                        for j in (2 * s_, 2 * s_ + 1):
                            act.wait_ge(raw_landed[j], 16 * i + 16 * (z1 + 2))
                            act.wait_ge(pe_used, 4 * i + (4 * (z1 + 1) + j + 1))
                            act.activation(whi[:, j, :], raw[:, j, :], ACT.Copy).then_inc(hi_ready, 1)
                    act.wait_ge(pe_used, 4 * i + (4 * z1 + 8))
                    act.activation(zs[:, bass.ds(2 * i + 4 * grp, 2), :], ps[:, 2 * grp:2 * grp + 2, :], ACT.Silu)\
                       .then_inc(lin_free[grp], 2)
            for k in k8:
                act.wait_ge(sy_dve.sem, sy_dve.value(f"g{k}"))
                if k >= 2:
                    act.wait_ge(sy_pe.sem, sy_pe.value(f"sum{k - 2}"))
                act.activation(ysq[:, k % 2, :], zs[:, k, :], ACT.Square).then_inc(sy_act.sem, sy_act.mark(f"sq{k}"))
            for g in range(2):
                act.wait_ge(sy_dve.sem, sy_dve.value(f"rc{g}"))
                act.activation(yms[:, g, :], yrs[:, g, :], ACT.Sqrt).then_inc(sy_act.sem, sy_act.mark(f"rs{g}"))
            for k in k8:
                act.wait_ge(sy_dve.sem, sy_dve.value(f"f{k}"))
                act.activation(ysh[:, k, :], yf[:, k % 2, :], ACT.Copy).then_inc(sy_act.sem, sy_act.mark(f"h{k}"))
            act.wait_ge(sy_dve.sem, sy_dve.value("w7"))
            act.dma_start(mix[:], pool_mix[0].rearrange("g c d -> c g d")).then_inc(mix_landed, 16)
            out_of_banks("pool", lambda src, q: act.activation(pv[:, bass.ds(2 * q, 2), PADV:PADV + S], src, ACT.Copy))
            act.wait_ge(sy_dve.sem, sy_dve.value("l7"))
            out_of_banks("qk", lambda src, q: act.activation(qk[:, bass.ds(2 * q, 2), :], src, ACT.Copy))
            out_of_banks("v", lambda src, q: act.activation(
                v[:, :, bass.ds(256 * q, 256)],
                src.rearrange("p a (b c) -> p (a b) c", b=2), ACT.Copy))
            for g in range(4):
                act.wait_ge(po_pe.sem, po_pe.value(f"y{g}"))
                act.activation(yph[:, g, :], bank(4 + g), ACT.Copy, scale=column("pool_scale", g))\
                   .then_inc(po_act.sem, po_act.mark(f"h{g}"))
            act.wait_ge(po_dve.sem, po_dve.value("l3"))
            with act.Fori(0, 4) as i:
                act.wait_ge(at_pe.sem, at_pe.value("1s3", i - 1))
                act.activation(qs[:], qk[:, bass.ds(i, 1), :].rearrange("p a b -> p (a b)"), ACT.Copy, scale=HD ** -0.5)\
                   .then_inc(at_act.sem, at_act.mark("qs"))
                act.activation(ks[:], qk[:, bass.ds(i + 4, 1), :].rearrange("p a b -> p (a b)"), ACT.Copy)\
                   .then_inc(at_act.sem, at_act.mark("ks"))
                for ev in AT_ACT:
                    e, n = int(ev[0]), int(ev[2])
                    u = 4 * e + n
                    L = P * (n + 1)
                    if ev[1] == "p":
                        act.wait_ge(at_dve.sem, at_dve.value(f"{e}m{n}", i))
                        act.wait_ge(at_pe.sem, step_back(at_pe, "t", u, 2, i))
                        act.activation(pe_[:, u % 2, 0:L], sm[:, u % 2, 0:L], ACT.Exp, bias=stat[:, 8 + u:9 + u],
                                       accum_out=stat[:, 16 + u:17 + u]).then_inc(at_act.sem, at_act.mark(ev))
                    else:
                        act.wait_ge(at_pe.sem, at_pe.value(f"{e}t{n}", i))
                        act.wait_ge(at_pe.sem, step_back(at_pe, "o", u, 2, i))
                        act.activation(pt[:, u % 2, 0:L], ps[:, 6, 0:L], ACT.Copy).then_inc(at_act.sem, at_act.mark(ev))
            for k in range(4):
                act.wait_ge(ay_pe.sem, ay_pe.value(f"t{k}"))
                act.activation(yah[:, k, :], bank(4 + k), ACT.Copy).then_inc(ay_act.sem, ay_act.mark(f"h{k}"))
            for b, proj in enumerate(("proj_pool", "proj_attn", "proj_ssd")):
                out_of_banks(f"gate{b}", lambda src, q: act.activation(gt[:, bass.ds(2 * q, 2), :], src, ACT.Sigmoid))
                if b < 2:
                    splits_only(proj)
                    for p in range(2):
                        act.wait_ge(lin_free[p], 2 + 2 * PLAN[f"gate{b + 1}"].fills[p])
                else:
                    with act.Fori(0, 2) as i:
                        for g in range(2):
                            split(i, PLAN[proj].first + g + 1)
                            for c in range(2):
                                act.wait_ge(mg_dve.sem, mg_dve.value(f"m{2 * g + c}", i + 2))
                                t = 4 * i + 2 * g + c
                                act.activation(uh[:, bass.ds(t, 1), :], mg[:, bass.ds(t, 1), :], ACT.Copy)\
                                   .then_inc(mg_act.sem, 1)
            splits_and_squares("w_out", 1)

            def ffn(f):
                up, first = f"up{f}", PLAN[f"up{f}"].first
                with act.Fori(0, FT // 2) as i:
                    turn = i + (FT // 2) * f
                    for g in range(2):
                        split(i, first + g + 1)
                        used(i, first + g)
                        for c in range(2):
                            t = 2 * i + (FT * g + c)
                            if g:
                                act.wait_ge(ffn_dve.sem, ffn_dve.value(f"hf{c}", turn - 1))
                            act.activation(fc[:, 2 * g + c, :], bank(2 * g + c), ACT.Identity, bias=column(f"f{f}c", t),
                                           scale=column(f"f{f}b", t)).then_inc(ffn_act.sem, ffn_act.mark(f"t{2 * g + c}"))
                        if g == 0:
                            for c in range(2):
                                act.wait_ge(lin_free[0], std_value(up, 0, i, c))
                                act.wait_ge(ffn_dve.sem, ffn_dve.value(f"hf{c}", turn - 1))
                                act.activation(fg[:, c, :], fc[:, c, :], ACT.Silu).then_inc(ffn_act.sem, ffn_act.mark(f"s{c}"))
                    for c in range(2):
                        act.wait_ge(ffn_dve.sem, ffn_dve.value(f"hf{c}", turn))
                        act.activation(fh[:, bass.ds(2 * i + c, 1), :], ff[:, c, :].unsqueeze(1), ACT.Copy)\
                           .then_inc(ffn_act.sem, ffn_act.mark(f"fh{c}"))
                ph = PLAN[f"down{f}"]
                with act.Fori(0, ph.quads - 1) as i:
                    split1(i, ph.first + 1)
                n = (2, 5, 7)[f]
                if f < 2:
                    split_unit(ph.first + ph.quads, 0)
                    split_unit(ph.first + ph.quads, 1)
                squares(n, n, range(4))
                if f < 2:
                    split_unit(ph.first + ph.quads, 2)
                    split_unit(ph.first + ph.quads, 3)
                squares(n, n, range(4, KT))
                root(n)

            root(1)
            upper(1, uh)
            ffn(0)

            act.wait_ge(prep_dve2.sem, prep_dve2.value("zero"))
            aw = a_w_in_2[0]
            for n, col in ((0, A_QKV + A_V), (32, A_QKV + A_V + DN_HEADS)):
                act.dma_start(ws[:, :, n:n + 8], aw[:, col:col + 8].rearrange("(k p) c -> p k c", p=P))\
                   .then_inc(small_landed, 16)
            squares(3, 3)
            root(3)
            upper(2, uh)
            scalars(1)
            conv("a_qkv", "a_conv_w", 72, None, None, ac, 3, acv)
            scalar_decays(1)

            def gmark(name):
                return gn_act.sem, gn_act.mark(name)

            def after(events, name, turn=0):
                act.wait_ge(events.sem, events.value(name, turn))

            first = PLAN["a_gate"].first
            for q in range(4):
                for j in range(4):
                    split_unit(first + q + 1, j)
                    t = 4 * q + j
                    if q >= 2:
                        after(gn_pe, f"n{t - 8}")
                    act.activation(asq[:, t % 8, :], ac[:, t, :], ACT.Square).then_inc(*gmark(f"sq{t}"))
                act.wait_ge(pe_used, 4 * (first + q) + 8)
                act.activation(ga[:, 2 * q:2 * q + 2, :], ps[:, 2 * (q % 2):2 * (q % 2) + 2, :], ACT.Silu).then_inc(lin_free[q % 2], 2)
            act.activation(beta[:], tok[:, 1, :, 0:8], ACT.Exp).then_inc(*gmark("beta"))
            act.activation(egc[:], tok[:, 0, :, 32:40], ACT.Exp).then_inc(*gmark("egc"))
            after(gn_dve, "nr")
            act.activation(rn2[:], rn[:], ACT.Sqrt).then_inc(*gmark("rt"))

            with act.Fori(0, DN_HEADS // 2) as i:
                for step in GA:
                    for e in range(2):
                        if step[:2] == "st":
                            n = {"k": 8, "v": 16, "q": 0}[step[2]]
                            dst = {"k": kf, "v": vf, "q": qf}[step[2]][e]
                            after(g_pe, f"{e}o3", i - 1)
                            last = act.activation(dst[:], ac[:, bass.ds(2 * i + (n + e), 1), :].rearrange("p a b -> p (a b)"),
                                                  ACT.Copy)
                        elif step == "eg":
                            after(g_pe, f"{e}row", i)
                            last = act.activation(eg[e][:], bank(4 * e + 3), ACT.Exp)
                        elif step == "em":
                            after(g_dve, f"{e}d", i)
                            last = act.activation(em[e][:], em[e][:], ACT.Exp)
                        elif step == "vb":
                            after(g_pe, f"{e}rv", i)
                            for c in ch:
                                last = act.activation(vb[e][:, c * P:(c + 1) * P], ps[:, 4 * e + 1, c * P:(c + 1) * P], ACT.Copy,
                                                      scale=beta[:, c, bass.ds(2 * i + e, 1)])
                        elif step in ("kt", "kbt", "qt"):
                            dst, b, turned = {"kt": (kt, 0, "tk"), "kbt": (kbt, 1, "tb"), "qt": (qt, 2, "tq")}[step]
                            after(g_pe, f"{e}{turned}", i)
                            last = act.activation(dst[e][:], bank(4 * e + b), ACT.Copy)
                        elif step[:2] == "ti":
                            after(g_pe, f"{e}t{step[2]}", i)
                            k = int(step[2])
                            if k == 0:
                                last = act.activation(ti[e][:], bank(4 * e + 2), ACT.Copy)
                            else:
                                last = act.activation(halves(ti[e][:], k, 0), halves(bank(4 * e + 2), k, 0), ACT.Copy)
                        elif step == "nkc":
                            after(g_pe, f"{e}nk", i)
                            last = act.activation(nkc[e][:], bank(4 * e + 3), ACT.Copy, scale=-1.0)
                        else:
                            c = int(step[2])
                            after(g_pe, f"{e}v{c}", i)
                            last = act.activation(vn[e][:, c * P:(c + 1) * P], ps[:, 4 * e, c * P:(c + 1) * P], ACT.Copy)
                        last.then_inc(g_act.sem, g_act.mark(f"{e}{step}"))
            after(g_dve, "1ot", 3)
            for n in ch:
                if n >= 2:
                    after(gn_dve, f"red{n - 2}")
                act.activation(osq[:, n % 2, :], ot[:, n, :], ACT.Square).then_inc(*gmark(f"q{n}"))
            after(gn_dve, "orc")
            act.activation(oss2[:], oss[:], ACT.Sqrt).then_inc(*gmark("or"))
            for k in k8:
                after(gn_dve, f"f{k}")
                act.activation(ayh[:, k, :], ayf[:, k % 2, :], ACT.Copy).then_inc(*gmark(f"h{k}"))
            splits_and_squares("a_out", 4)
            root(4)
            upper(3, uh)
            ffn(1)

            act.dma_start(vbias[:], kv_b_2[256:512].partition_broadcast(P)).then_inc(vbias_landed, 16)
            upper(4, uh)
            upper(5, ubh)
            split1(0, PLAN["kv_k"].first + 1)
            split1(0, PLAN["kv_v"].first + 1)
            splits_only("q2")
            for p in range(2):
                act.wait_ge(lin_free[p], std_value("q2", p, 1))
            after(kv_dve, "k7")
            def back(events, name, u, lag, turn):
                return events.value(f"{name}{u - lag}", turn) if u >= lag else events.value(f"{name}{u - lag + NH}", turn - 1)

            with act.Fori(0, SWA_HEADS // NH) as i:
                for step in BA:
                    u = int(step[-1])
                    if step[:2] == "st":
                        act.wait_ge(b_pe.sem, b_pe.value("s3", i) if u else b_pe.value("s7", i - 1))
                        act.activation(qst[:], q2[:, bass.ds(4 * i + 2 * u, 2), :], ACT.Copy)
                        last = act.activation(kst[:], kk[:, bass.ds(2 * i + u, 1), :].rearrange("p a b -> p (a b)"), ACT.Copy)
                    elif step[0] == "p":
                        after(b_dve, f"ng{u}", i)
                        act.wait_ge(b_pe.sem, back(b_pe, "t", u, 2, i))
                        s_ = 8 * (u % 4)
                        for n in range(NT):
                            lo = P if n == 0 else 0
                            act.activation(pr2[:, u % 2, n, lo:], sm2[:, u % 2, n, lo:], ACT.Exp, bias=st2[:, s_ + n:s_ + n + 1],
                                           accum_out=st2[:, s_ + 4 + n:s_ + 5 + n])
                        last = act.activation(st2[:, 32 + 4 * (u % 4):36 + 4 * (u % 4)], st2[:, s_:s_ + 4], ACT.Exp,
                                              bias=sinks[:, bass.ds(NH * i + u, 1)])
                    else:
                        after(b_pe, f"t{u}", i)
                        act.wait_ge(b_pe.sem, back(b_pe, "o", u, 1, i))
                        last = act.activation(pt2[:].rearrange("p a b -> p (a b)"),
                                              ps[:, 4:6, :].rearrange("p a b -> p (a b)")[:, 0:7 * P], ACT.Copy)
                    last.then_inc(b_act.sem, b_act.mark(step))
            for k in k8:
                after(bo_pe, f"t{k}")
                act.activation(uh[:, k, :], bank(4 + k % 4), ACT.Copy).then_inc(bo_act.sem, bo_act.mark(f"h{k}"))
            splits_and_squares("o2", 6)
            root(6)
            upper(6, uh)
            ffn(2)

        @block.tensor
        def _(pe):
            def three(o, j, col, width, moving, k, start, stop, hi_moving=True):
                mh, ml = moving
                a = whi[:, j, col:col + width]
                pe.matmul(o, a, mh[:, k, :], start=start, stop=False, skip_group_check=True)
                pe.matmul(o, a, ml[:, k, :], start=False, stop=False, skip_group_check=True)
                return pe.matmul(o, wlo[:, j, col:col + width], mh[:, k, :], start=False, stop=stop,
                                 skip_group_check=True)

            def quad(ph, i, g, pair, turn, moving, ready=None):
                pe.wait_ge(lin_free[pair], 2 * turn + (2 * PLAN[ph].fills[pair] + 2))
                for j in range(4):
                    pe.wait_ge(lo_ready, 8 * i + (4 * (PLAN[ph].first + g) + j + 5))
                    for a in range(2):
                        k = 2 * j + a
                        if ready is not None:
                            pe.wait_ge(ready[0].sem, ready[0].value(f"{ready[1]}{k}", ready[2]))
                        for c in range(2):
                            last = three(bank(2 * pair + c), j, 256 * a + 128 * c, P, moving, k, k == 0, k == KT - 1)
                    last.then_inc(pe_used, 1)

            def quad_tok(ph, i, g, pair, turn, moving):
                pe.wait_ge(lin_free[pair], 2 * turn + (2 * PLAN[ph].fills[pair] + 2))
                for j in range(4):
                    pe.wait_ge(lo_ready, 8 * i + (4 * (PLAN[ph].first + g) + j + 5))
                    for a in range(2):
                        k = 2 * j + a
                        for n in range(NT):
                            o = ps[:, 2 * pair + n // 2, 256 * (n % 2):256 * (n % 2) + 256]
                            for w, m, first in ((whi, moving[0], True), (whi, moving[1], False), (wlo, moving[0], False)):
                                last = pe.matmul(o, m[:, k, n * P:(n + 1) * P], w[:, j, 256 * a:256 * a + 256],
                                                 start=first and k == 0 and n % 2 == 0, stop=k == KT - 1,
                                                 skip_group_check=True)
                    last.then_inc(pe_used, 1)

            def std(ph, moving, ready=None):
                with pe.Fori(0, PLAN[ph].quads // 2) as i:
                    for g in range(2):
                        quad(ph, i, g, g, i, moving, ready if g == 0 else None)

            def half(ph, moving):
                with pe.Fori(0, PLAN[ph].quads) as i:
                    for j in range(4):
                        pair = j // 2
                        if j % 2 == 0:
                            pe.wait_ge(lin_free[pair], 2 * i + (2 * PLAN[ph].fills[pair] + 2))
                        pe.wait_ge(lo_ready, 4 * i + (4 * PLAN[ph].first + j + 5))
                        for a in range(2):
                            k = 2 * (j % 2) + a
                            for c in range(2):
                                last = three(bank(2 * pair + c), j, 256 * a + 128 * c, P, moving, k, k == 0, k == 3)
                        last.then_inc(pe_used, 1)

            def sum_squares(n):
                for k in k8:
                    pe.wait_ge(norm_act.sem, norm_act.value(f"sq{k}", n))
                    pe.matmul(ps[0:1, 4, :], ones[:, 0:1], sq[:, k, :], start=k == 0, stop=k == KT - 1)\
                        .then_inc(norm_pe.sem, norm_pe.mark(f"sum{k}"))
                pe.wait_ge(norm_dve.sem, norm_dve.value("mean", n))
                for c in ch:
                    last = pe.matmul(ps[:, 5, c:c + 1], mean[:, c * P:(c + 1) * P], ones[0:1, 0:1], start=True, stop=True)
                last.then_inc(norm_pe.sem, norm_pe.mark("turned"))
                pe.wait_ge(norm_act.sem, norm_act.value("rs", n))
                for c in ch:
                    last = pe.matmul(ps[:, 7, c * P:(c + 1) * P], rs[:, c:c + 1].to_broadcast([P, P]), ident[:], start=True, stop=True)
                last.then_inc(norm_pe.sem, norm_pe.mark("row"))

            def small(n, m):
                if n == 0:
                    pe.wait_ge(prep_dve.sem, prep_dve.value("wsl"))
                else:
                    pe.wait_ge(prep_dve2.sem, prep_dve2.value("wsl"))
                for k in k8:
                    pe.wait_ge(u_dve.sem, u_dve.value(f"ul{k}", m))
                    pe.matmul(ps[0:48, 5, :], wsh[:, k, :], uh[:, k, :], start=k == 0, stop=False)
                    pe.matmul(ps[0:48, 5, :], wsh[:, k, :], ul[:, k, :], start=False, stop=False)
                    last = pe.matmul(ps[0:48, 5, :], wsl[:, k, :], uh[:, k, :], start=False, stop=k == KT - 1)
                last.then_inc(sc_pe.sem, sc_pe.mark("logits"))

            def turn_scalars(n):
                pe.wait_ge(sc_dve.sem, sc_dve.value("sums", n))
                for w, src in enumerate((cs[:], sc[:, 9, :])):
                    for c in ch:
                        last = pe.transpose(ps[:, 5, 192 * w + 48 * c:192 * w + 48 * c + 48], src[:, c * P:(c + 1) * P],
                                            ident[0:48, 0:48])
                last.then_inc(sc_pe.sem, sc_pe.mark("turned"))
                pe.wait_ge(sc_dve.sem, sc_dve.value("tok", n))
                pe.matmul(ps[:, 6, 0:192], last_row[:], tok[:, 0, :, :].rearrange("p a b -> p (a b)"), start=True,
                          stop=True).then_inc(sc_pe.sem, sc_pe.mark("last"))

            pe.wait_ge(consts_ready, 1)
            pe.wait_ge(par_landed, 16 * sum(len(r) for r in ROWS))
            for b in range(3):
                for n in range(4 * b, min(4 * b + 4, 9)):
                    last = pe.transpose(ps[:, 5 + b, 128 * (n % 4):128 * (n % 4) + 128], par_in[:, n, :], ident[:])
                last.then_inc(x_pe.sem, x_pe.mark(f"par{b}"))
            pe.wait_ge(x_landed, 16 * NT)
            for k in k8:
                if k >= 4:
                    pe.wait_ge(x_ready, k - 3)
                for n in ch:
                    last = pe.transpose(ps[:, k % 4, n * P:(n + 1) * P], x_in[:, n, k * P:(k + 1) * P], ident[:])
                last.then_inc(x_pe.sem, x_pe.mark(f"x{k}"))

            sum_squares(0)
            small(0, 0)
            std("xbc", (uh, ul))
            turn_scalars(0)
            pe.wait_ge(conv_act.sem, conv_act.value("s3", 2))
            pe.wait_ge(sc_act.sem, sc_act.value("chunk", 0))
            for g in range(SSD_GROUPS):
                for c in ch:
                    last = pe.matmul(ps[:, 4 + g, c * P:(c + 1) * P], xc[:, 8 + g, c * P:(c + 1) * P],
                                     xc[:, 10 + g, c * P:(c + 1) * P], start=True, stop=True)
                last.then_inc(ssd_pe.sem, ssd_pe.mark(f"cb{g}"))
            for c in ch:
                pe.wait_ge(ssd_dve.sem, ssd_dve.value("cb1" if c == 0 else f"xd{c - 1}"))
                for k in k8:
                    last = pe.transpose(ps[:, 4 + k // 4, P * (k % 4):P * (k % 4) + P], xc[:, k, c * P:(c + 1) * P], ident[:])
                last.then_inc(ssd_pe.sem, ssd_pe.mark(f"x{c}"))
                if c == 3:
                    break
                if c:
                    pe.wait_ge(ssd_dve.sem, ssd_dve.value(f"st{c - 1}"))
                for g in range(2):
                    last = pe.transpose(ps[:, 6, P * g:P * g + P], xc[:, 8 + g, c * P:(c + 1) * P], ident[:])
                last.then_inc(ssd_pe.sem, ssd_pe.mark(f"b{c}"))
                pe.wait_ge(ssd_dve.sem, ssd_dve.value(f"xdd{c}"))
                for g in range(2):
                    pe.matmul(bank(6 + g), bt[:, P * g:P * g + P], xdd[:, 512 * g:512 * g + 512], start=True, stop=True)\
                        .then_inc(ssd_pe.sem, ssd_pe.mark(f"state{c}_{g}"))
            pe.wait_ge(ssd_dve.sem, ssd_dve.value("xd3"))
            for grp in range(SSD_GROUPS):
                with pe.Fori(0, 2) as i:
                    for s_ in range(2):
                        turn = 2 * i + (s_ + 4 * grp)
                        for e in range(2):
                            pe.wait_ge(sh_dve.sem, sh_dve.value(f"oh{e}", turn))
                            pe.wait_ge(sh_act.sem, sh_act.value(f"r{e}", turn - 1))
                            pe.matmul(bank(4 + e), ones[0:48, :], oh[:, e, :], start=True, stop=True)\
                                .then_inc(sh_pe.sem, sh_pe.mark(f"row{e}"))
                        if s_ == 0:
                            pe.wait_ge(lin_free[grp], 2 * i + (2 * PLAN["z"].fills[grp] + 2))
                        for j in (2 * s_, 2 * s_ + 1):
                            pe.wait_ge(lo_ready, 4 * i + (4 * (PLAN["z"].first + 2 * grp) + j + 5))
                            for a in range(2):
                                for c in range(2):
                                    last = three(bank(2 * grp + c), j, 256 * a + 128 * c, P, (uh, ul), 2 * j + a,
                                                 2 * j + a == 0, 2 * j + a == KT - 1)
                            last.then_inc(pe_used, 1)
                        for e in range(2):
                            pe.wait_ge(sh_dve.sem, sh_dve.value(f"c{e}", turn))
                            pe.wait_ge(sh_act.sem, sh_act.value(f"y{e}", turn - 1))
                            head = bass.ds(256 * i + (512 * grp + 128 * s_ + 64 * e), HD)
                            for c in ch:
                                o = ps[:, 6 + e, HD * c:HD * c + HD]
                                last = pe.matmul(o, mt[:, e, c * P:(c + 1) * P], xd[:, c, head], start=True, stop=c == 0)
                                if c:
                                    last = pe.matmul(o, ce[:, e, c * P:(c + 1) * P], st[:, c - 1, head], start=False, stop=True)
                            last.then_inc(sh_pe.sem, sh_pe.mark(f"y{e}"))

            def y_turn(k):
                pe.wait_ge(*((sh_act.sem, sh_act.value("y1", 7)) if k < 2 else (sy_dve.sem, sy_dve.value(f"w{k - 2}"))))
                for n in ch:
                    last = pe.transpose(ps[:, 4 + k % 2, n * P:(n + 1) * P], y_tok[:, n, k * P:(k + 1) * P], ident[:])
                last.then_inc(sy_pe.sem, sy_pe.mark(f"t{k}"))

            y_turn(0)
            y_turn(1)
            for k in k8:
                if k < 6:
                    y_turn(k + 2)
                pe.wait_ge(sy_act.sem, sy_act.value(f"sq{k}"))
                pe.matmul(bank(6 + k // 4), ones[:], ysq[:, k % 2, :], start=k % 4 == 0, stop=k % 4 == 3)\
                    .then_inc(sy_pe.sem, sy_pe.mark(f"sum{k}"))
            std("pool", (uh, ul))
            std("qk", (uh, ul))
            with pe.Fori(0, 1) as i:
                for g in range(2):
                    quad_tok("v", i, g, g, i, (uh, ul))
            pe.wait_ge(mix_landed, 16)
            for g in range(4):
                pe.wait_ge(po_dve.sem, po_dve.value(f"e{g}"))
                if g >= 2:
                    pass
                pe.matmul(bank(4 + g), mix[:, g, :], dp[:, g, :], start=True, stop=True)\
                    .then_inc(po_pe.sem, po_pe.mark(f"y{g}"))
            for p in range(2):
                pe.wait_ge(lin_free[p], std_value("v", p, 0))
            pe.wait_ge(po_dve.sem, po_dve.value("l3"))
            with pe.Fori(0, 4) as i:
                for ev in AT_PE:
                    e = int(ev[0])
                    if ev[1:] == "bc":
                        pe.wait_ge(at_dve.sem, at_dve.value(f"{e}oh", i))
                        pe.wait_ge(at_dve.sem, at_dve.value("0nb", i) if e else at_dve.value("1nb", i - 1))
                        pe.matmul(bank(0), ones[0:48, :], ohc[:], start=True, stop=True).then_inc(at_pe.sem, at_pe.mark(ev))
                        continue
                    n = int(ev[2])
                    u = 4 * e + n
                    if ev[1] == "s":
                        pe.wait_ge(at_act.sem, at_act.value("ks", i))
                        pe.wait_ge(at_dve.sem, step_back(at_dve, "s", u, 4, i))
                        b = ps[:, 2 + u % 4, 0:P * (n + 1)]
                        r = slice(HD * e, HD * e + HD)
                        pe.matmul(b, qs[r, n * P:(n + 1) * P], ks[r, 0:P * (n + 1)], start=True, stop=False,
                                  skip_group_check=True)
                        last = pe.matmul(ps[:, 2 + u % 4, n * P:(n + 1) * P], ident_bf[:], mask_q[:],
                                         start=False, stop=True, skip_group_check=True)
                    elif ev[1] == "t":
                        pe.wait_ge(at_act.sem, at_act.value(f"{e}p{n}", i))
                        pe.wait_ge(at_act.sem, step_back(at_act, "c", u, 1, i))
                        for j in range(n + 1):
                            last = pe.transpose(ps[:, 6, j * P:(j + 1) * P], pe_[:, u % 2, j * P:(j + 1) * P], ident[:])
                    else:
                        pe.wait_ge(at_act.sem, at_act.value(f"{e}c{n}", i))
                        pe.wait_ge(at_dve.sem, step_back(at_dve, "o", u, 2, i))
                        for j in range(n + 1):
                            last = pe.matmul(ps[:, (7, 1)[u % 2], 64 * u:64 * u + 64], pt[:, u % 2, j * P:(j + 1) * P],
                                             v[:, j, bass.ds(128 * i + 64 * e, HD)], start=j == 0, stop=j == n)
                    last.then_inc(at_pe.sem, at_pe.mark(ev))
            for k in range(4):
                pe.wait_ge(at_dve.sem, at_dve.value("1o3", 3))
                for n in ch:
                    last = pe.transpose(ps[:, 4 + k, n * P:(n + 1) * P], oa[:, n, k * P:(k + 1) * P], ident[:])
                last.then_inc(ay_pe.sem, ay_pe.mark(f"t{k}"))
            std("gate0", (uh, ul))
            half("proj_pool", (yph, ypl))
            std("gate1", (uh, ul))
            pe.wait_ge(ay_dve.sem, ay_dve.value("l3"))
            half("proj_attn", (yah, yal))
            std("gate2", (uh, ul))
            std("proj_ssd", (ysh, ysl))
            for k in k8:
                pass
            pe.wait_ge(mg_low.sem, 8)
            std("w_out", (uh, ul))

            def ffn(f, m):
                std(f"up{f}", (uh, ul), (u_dve, "ul", m))
                ph = PLAN[f"down{f}"]

                def down_quad(q, first, last):
                    pe.wait_ge(ffn_dve.sem, ffn_dve.value("fl1", q + 11 * f))
                    for j in range(4):
                        b = 4 * (1 - j // 2)
                        k = 2 * q + j % 2
                        if first and j == 2:
                            for p in range(2):
                                pe.wait_ge(lin_free[p], 2 * ph.fills[p] + 2)
                        pe.wait_ge(lo_ready, 4 * q + (4 * ph.first + j + 5))
                        for c in range(4):
                            for w, x_ in ((whi, fh), (whi, fl), (wlo, fh)):
                                moving = x_[:, k, :] if isinstance(k, int) else x_[:, bass.ds(k, 1), :].rearrange("p a b -> p (a b)")
                                mm = pe.matmul(bank(b + c), w[:, j, c * P:c * P + P], moving,
                                               start=first and j % 2 == 0 and w is whi and x_ is fh,
                                               stop=last and j % 2 == 1 and w is wlo, skip_group_check=True)
                        mm.then_inc(pe_used, 1)

                down_quad(0, True, False)
                with pe.Fori(0, 9) as i:
                    down_quad(i + 1, False, False)
                down_quad(10, False, True)

            sum_squares(1)
            ffn(0, 1)
            sum_squares(2)

            sum_squares(3)
            small(1, 2)
            std("a_qkv", (uh, ul))
            turn_scalars(1)

            def after(events, name, turn=0):
                pe.wait_ge(events.sem, events.value(name, turn))

            after(gn_dve, "pick")
            for q in range(5):
                if q < 4:
                    quad("a_gate", 0, q, q % 2, q // 2, (uh, ul))
                if q:
                    for t in range(4 * q - 4, 4 * q):
                        after(gn_act, f"sq{t}")
                        pe.matmul(ps[0:16, 4, :], pick[:, 15 - t:31 - t], asq[:, t % 8, :], start=t == 0, stop=t == 15)\
                            .then_inc(gn_pe.sem, gn_pe.mark(f"n{t}"))
            after(gn_dve, "ns")
            for c in ch:
                last = pe.transpose(ps[:, 4, 16 * c:16 * c + 16], qk_sums[:, c * P:(c + 1) * P], ident[0:16, 0:16])
            last.then_inc(gn_pe.sem, gn_pe.mark("nt"))
            after(gn_dve, "bege")
            for p in range(2):
                pe.wait_ge(lin_free[p], 2 * PLAN["a_out"].fills[p] + 2)
            with pe.Fori(0, DN_HEADS // 2) as i:
                for step in GP:
                    for e in range(2):
                        B = [ps[:, 4 * e + b, :] for b in range(4)]

                        def cc(t, c):
                            return t[:, c * P:(c + 1) * P]

                        def chunks(out_, left, right, transposed=False):
                            for c in ch:
                                if transposed:
                                    r = pe.transpose(cc(out_, c), cc(left, c), ident[:])
                                else:
                                    r = pe.matmul(cc(out_, c), cc(left, c), cc(right, c), start=True, stop=True)
                            return r

                        if step == "row":
                            after(g_dve, f"{e}goh", i)
                            last = pe.matmul(B[3], ones[0:48, :], goh[:, e, :], start=True, stop=True)
                        elif step in ("rk", "rv", "rq"):
                            after(g_act, f"{e}st{step[1]}", i)
                            if step != "rk":
                                after(g_dve, f"{e}ot", i - 1)
                            b, src = {"k": (0, kf), "v": (1, vf), "q": (2, qf)}[step[1]]
                            last = chunks(B[b], src[e], None, True)
                        elif step in ("tk", "tb", "tq"):
                            b, src, made_ = {"k": (0, kn, "kn"), "b": (1, kb, "kb"), "q": (2, qn, "qn")}[step[1]]
                            after(g_dve, f"{e}{made_}", i)
                            if step == "tb":
                                after(g_act, f"{e}vb", i)
                            last = chunks(B[b], src[e], None, True)
                        elif step == "prod":
                            after(g_act, f"{e}kbt", i)
                            last = chunks(B[0], kt[e], kbt[e])
                        elif step == "prq":
                            after(g_act, f"{e}qt", i)
                            last = chunks(B[1], kt[e], qt[e])
                        elif step == "t0":
                            after(g_dve, f"{e}tt0", i)
                            last = chunks(B[2], tt[e], None, True)
                        elif step[0] == "x":
                            k = int(step[1])
                            after(g_dve, f"{e}ltk{k}", i)
                            after(g_act, f"{e}ti{k - 1}", i)
                            last = chunks(B[3], ltk[e], ti[e])
                        elif step[:2] == "tt":
                            k = int(step[2])
                            after(g_dve, f"{e}xi{k}", i)
                            for c in ch:
                                last = pe.matmul(halves(cc(B[0], c), k, 1), cc(xi[e], c), halves(cc(tt[e], c), k, 1), start=True, stop=True)
                        elif step[0] == "t":
                            k = int(step[1])
                            after(g_dve, f"{e}xi{k}", i)
                            for c in ch:
                                last = pe.matmul(halves(cc(B[2], c), k, 0), cc(tt[e], c), halves(cc(xi[e], c), k, 0), start=True, stop=True)
                        elif step == "nk":
                            after(g_dve, f"{e}tt6", i)
                            last = chunks(B[3], kbe[e], tt[e])
                        elif step[0] == "v":
                            c = int(step[1])
                            if c:
                                after(g_act, f"{e}nkc", i)
                                after(g_dve, f"{e}s{c - 1}", i)
                            last = pe.matmul(cc(B[0], c), cc(tt[e], c), cc(vb[e], c), start=True, stop=c == 0)
                            if c:
                                last = pe.matmul(cc(B[0], c), cc(nkc[e], c), sg[e][:], start=False, stop=True)
                        elif step[0] == "o":
                            c = int(step[1])
                            if c:
                                pe.matmul(cc(B[1], c), cc(eg[e], c), sg[e][:], start=True, stop=False)
                            after(g_act, f"{e}vn{c}", i)
                            last = pe.matmul(cc(B[1], c), cc(an[e], c), cc(vn[e], c), start=c == 0, stop=True)
                        else:
                            c = int(step[1])
                            last = pe.matmul(cc(B[2], c), cc(kd[e], c), cc(vn[e], c), start=True, stop=True)
                        last.then_inc(g_pe.sem, g_pe.mark(f"{e}{step}"))
            for n in ch:
                after(gn_dve, f"sc{n}")
                for k in k8:
                    last = pe.transpose(ps[:, k, n * P:(n + 1) * P], ot[:, n, k * P:(k + 1) * P], ident[:])
                    if n == NT - 1:
                        last.then_inc(gn_pe.sem, gn_pe.mark(f"t{k}"))
            for k in range(4):
                after(gn_dve, f"f{k}")
            std("a_out", (ayh, ayl), (gn_dve, "l", 0))
            sum_squares(4)
            ffn(1, 3)

            sum_squares(5)
            quad("kv_k", 0, 0, 0, 0, (uh, ul), (u_dve, "ul", 4))
            quad_tok("kv_v", 0, 0, 1, 0, (uh, ul))
            std("q2", (ubh, ubl), (u_dve, "ul", 5))
            for p in range(2):
                pe.wait_ge(lin_free[p], 2 * PLAN["o2"].fills[p] + 2)
            def back(events, name, u, lag, turn):
                return events.value(f"{name}{u - lag}", turn) if u >= lag else events.value(f"{name}{u - lag + NH}", turn - 1)

            with pe.Fori(0, SWA_HEADS // NH) as i:
                for step in BP:
                    u = int(step[1])
                    if step[0] == "s":
                        after(b_act, f"st{u // 4}", i)
                        pe.wait_ge(b_dve.sem, back(b_dve, "sb", u, 2, i))
                        r = slice(HD * (u % 2), HD * (u % 2) + HD)
                        for n in range(NT):
                            lo = P if n == 0 else 0
                            o = ps[:, 2 * (u % 2) + n // 2, 256 * (n % 2) + lo:256 * (n % 2) + 256]
                            last = pe.matmul(o, qst[r, u % 4 // 2, n * P:(n + 1) * P], kst[r, max(n - 1, 0) * P:(n + 1) * P],
                                             start=True, stop=True)
                    elif step[0] == "t":
                        after(b_act, f"p{u}", i)
                        pe.wait_ge(b_act.sem, back(b_act, "c", u, 1, i))
                        for x_ in range(7):
                            n, lo = (x_ + 1) // 2, P * ((x_ + 1) % 2)
                            last = pe.transpose(ps[:, 4 + x_ // 4, P * (x_ % 4):P * (x_ % 4) + P],
                                                pr2[:, u % 2, n, lo:lo + P], ident[:])
                    else:
                        after(b_act, f"c{u}", i)
                        pe.wait_ge(b_dve.sem, back(b_dve, "o", u, 2, i))
                        cols = bass.ds(2 * HD * i + HD * (u // 4), HD)
                        for n in range(NT):
                            o = ps[:, 6 + u % 2, HD * n:HD * n + HD]
                            if n:
                                pe.matmul(o, pt2[:, 2 * n - 1, :], vv[:, n - 1, cols], start=True, stop=False)
                            last = pe.matmul(o, pt2[:, 2 * n, :], vv[:, n, cols], start=n == 0, stop=True)
                    last.then_inc(b_pe.sem, b_pe.mark(step))
            for k in k8:
                after(b_dve, "o7", 1)
                if k >= 4:
                    after(bo_dve, f"l{k - 4}")
                for n in ch:
                    last = pe.transpose(ps[:, 4 + k % 4, n * P:(n + 1) * P], o_tok[:, n, k * P:(k + 1) * P], ident[:])
                last.then_inc(bo_pe.sem, bo_pe.mark(f"t{k}"))
            after(bo_dve, "l7")
            std("o2", (uh, ul))
            sum_squares(6)
            ffn(2, 6)
            sum_squares(7)

            for n in ch:
                pe.wait_ge(out_made, 8)
                if n >= 2:
                    pe.wait_ge(fin_dve.sem, fin_dve.value(f"c{n - 2}"))
                for k in k8:
                    last = pe.transpose(ps[:, 4 + 2 * (n % 2) + k // 4, P * (k % 4):P * (k % 4) + P],
                                        out_t[:, k, n * P:(n + 1) * P], ident[:])
                last.then_inc(fin_pe.sem, fin_pe.mark(f"t{n}"))

        @block.vector
        def _(dve):
            def norm(n):
                dve.wait_ge(norm_pe.sem, norm_pe.value("sum7", n))
                dve.tensor_scalar(mean[:], ps[0:1, 4, :], 1.0 / D, EPS, ALU.mult, ALU.add).then_inc(norm_dve.sem, norm_dve.mark("mean"))
                dve.wait_ge(norm_pe.sem, norm_pe.value("turned", n))
                dve.reciprocal(rc, ps[:, 5, 0:NT]).then_inc(norm_dve.sem, norm_dve.mark("rc"))

            def normed(n, m, gain, dst):
                def full(k):
                    if k == 0:
                        dve.wait_ge(norm_pe.sem, norm_pe.value("row", n))
                    if k >= 2:
                        dve.wait_ge(u_act.sem, u_act.value(f"uh{k - 2}", m))
                        dve.wait_ge(u_dve.sem, u_dve.value(f"ul{k - 2}", m))
                    dve.scalar_tensor_tensor(out=uf[:, k % 2, :], in0=h[:, k, :], scalar=column(gain, k), in1=bank(7),
                                             op0=ALU.mult, op1=ALU.mult).then_inc(u_dve.sem, u_dve.mark(f"u{k}"))
                full(0)
                for k in k8:
                    if k < 7:
                        full(k + 1)
                    dve.wait_ge(u_act.sem, u_act.value(f"uh{k}", m))
                    dve.wait_ge(u_dve.sem, u_dve.value(f"u{k}", m))
                    dve.tensor_tensor(dst[:, k, :], uf[:, k % 2, :], uh_of(dst)[:, k, :].bitcast(F32), ALU.subtract)\
                       .then_inc(u_dve.sem, u_dve.mark(f"ul{k}"))

            def uh_of(low):
                return uh if low is ul else ubh

            def scalars(n):
                w8 = lambda name: dve.wait_ge(sc_dve.sem, sc_dve.value(name, n))
                dve.wait_ge(sc_pe.sem, sc_pe.value("logits", n))
                dve.wait_ge(prep_dve.sem, prep_dve.value("a_neg"))
                dve.tensor_scalar(sc[:, 0, :], ps[0:48, 5, :], sgn[:], sgn_bias[:, n:n + 1], ALU.mult, ALU.add)\
                   .then_inc(sc_dve.sem, sc_dve.mark("t"))
                w8("t")
                dve.scalar_tensor_tensor(out=sc[:, 1, :], in0=sc[:, 0, :], scalar=-1.0, in1=sc[:, 0, :], op0=ALU.mult,
                                         op1=ALU.max).then_inc(sc_dve.sem, sc_dve.mark("abs"))
                dve.wait_ge(sc_act.sem, sc_act.value("exp", n))
                dve.tensor_scalar(sc[:, 3, :], sc[:, 2, :], 1.0, None, ALU.add).then_inc(sc_dve.sem, sc_dve.mark("one"))
                w8("one")
                dve.tensor_scalar(sc[:, 4, :], sc[:, 3, :], -1.0, None, ALU.add).then_inc(sc_dve.sem, sc_dve.mark("w"))
                w8("w")
                dve.tensor_scalar(sc[:, 6, :], sc[:, 4, :], 0.0, None, ALU.is_equal).then_inc(sc_dve.sem, sc_dve.mark("eq"))
                w8("eq")
                dve.tensor_tensor(sc[:, 7, :], sc[:, 4, :], sc[:, 6, :], ALU.add).then_inc(sc_dve.sem, sc_dve.mark("den"))
                w8("den")
                dve.reciprocal(sc[:, 8, :], sc[:, 7, :]).then_inc(sc_dve.sem, sc_dve.mark("inv"))
                dve.wait_ge(sc_act.sem, sc_act.value("ln", n))
                dve.tensor_tensor(sc[:, 1, :], sc[:, 5, :], sc[:, 6, :], ALU.add).then_inc(sc_dve.sem, sc_dve.mark("num"))
                w8("num")
                dve.tensor_tensor(sc[:, 3, :], sc[:, 1, :], sc[:, 8, :], ALU.mult).then_inc(sc_dve.sem, sc_dve.mark("q"))
                w8("q")
                dve.tensor_tensor(sc[:, 4, :], sc[:, 3, :], sc[:, 2, :], ALU.mult).then_inc(sc_dve.sem, sc_dve.mark("r"))
                w8("r")
                sp_at, scaled_at = (9, 6) if n == 0 else (5, 9)
                dve.scalar_tensor_tensor(out=sc[:, sp_at, :], in0=sc[:, 0, :], scalar=0.0, in1=sc[:, 4, :],
                                         op0=ALU.max, op1=ALU.add).then_inc(sc_dve.sem, sc_dve.mark("sp"))
                w8("sp")
                dve.tensor_scalar(sc[:, scaled_at, :], sc[:, sp_at, :], row_scale[:, n:n + 1], None, ALU.mult)\
                   .then_inc(sc_dve.sem, sc_dve.mark("scaled"))
                w8("scaled")
                dve.tensor_tensor_scan(cs[:], keep[:], sc[:, scaled_at, :], 0.0, ALU.mult, ALU.add)\
                   .then_inc(sc_dve.sem, sc_dve.mark("sums"))

            def scalars_by_token(n):
                dve.wait_ge(sc_pe.sem, sc_pe.value("turned", n))
                dve.tensor_copy(tok[:].rearrange("p a b c -> p (a b c)"), ps[:, 5, 0:384])\
                   .then_inc(sc_dve.sem, sc_dve.mark("tok"))
                dve.wait_ge(sc_dve.sem, sc_dve.value("tok", n))
                dve.wait_ge(sc_pe.sem, sc_pe.value("last", n))
                dve.tensor_tensor(decay_end[:].rearrange("p a b -> p (a b)"), ps[:, 6, 0:192],
                                  tok[:, 0, :, :].rearrange("p a b -> p (a b)"), ALU.subtract)\
                   .then_inc(sc_dve.sem, sc_dve.mark("end"))

            def conv4(ph, w_name, turn0, buf):
                with dve.Fori(0, PLAN[ph].quads // 2) as i:
                    turn = i + turn0
                    for g in range(2):
                        for c in range(2):
                            b, t = 2 * g + c, 4 * i + 2 * g + c
                            dve.wait_ge(conv_act.sem, conv_act.value(f"t{b}", turn))
                            dve.scalar_tensor_tensor(out=buf[:, b, 1:S], in0=ps[:, b, 0:S - 1], scalar=column(w_name, t + 2 * TAPS[ph]),
                                                     in1=buf[:, b, 1:S], op0=ALU.mult, op1=ALU.add)\
                               .then_inc(conv_dve.sem, conv_dve.mark(f"a{b}"))
                        for c in range(2):
                            b, t = 2 * g + c, 4 * i + 2 * g + c
                            dve.wait_ge(conv_dve.sem, conv_dve.value(f"a{b}", turn))
                            dve.scalar_tensor_tensor(out=buf[:, b, 2:S], in0=ps[:, b, 0:S - 2], scalar=column(w_name, t + TAPS[ph]),
                                                     in1=buf[:, b, 2:S], op0=ALU.mult, op1=ALU.add)\
                               .then_inc(conv_dve.sem, conv_dve.mark(f"b{b}"))
                        for c in range(2):
                            b, t = 2 * g + c, 4 * i + 2 * g + c
                            dve.wait_ge(conv_dve.sem, conv_dve.value(f"b{b}", turn))
                            dve.scalar_tensor_tensor(out=buf[:, b, 3:S], in0=ps[:, b, 0:S - 3], scalar=column(w_name, t),
                                                     in1=buf[:, b, 3:S], op0=ALU.mult, op1=ALU.add)\
                               .then_inc(lin_free[g], 1)

            def added(ph, bias=None):
                with dve.Fori(0, PLAN[ph].quads // 2) as i:
                    for g in range(2):
                        dve.wait_ge(pe_used, 8 * i + (4 * (PLAN[ph].first + g) + 8))
                        for c in range(2):
                            t = bass.ds(4 * i + 2 * g + c, 1)
                            src = ps[:, 2 * g + c:2 * g + c + 1, :]
                            if bias:
                                dve.scalar_tensor_tensor(out=h[:, t, :], in0=src, scalar=column(bias, 4 * i + 2 * g + c),
                                                         in1=h[:, t, :], op0=ALU.add, op1=ALU.add).then_inc(lin_free[g], 1)
                            else:
                                dve.tensor_tensor(h[:, t, :], src, h[:, t, :], ALU.add).then_inc(lin_free[g], 1)

            dve.wait_ge(consts_ready, 1)
            for b in range(3):
                n = min(4, 9 - 4 * b)
                dve.wait_ge(x_pe.sem, x_pe.value(f"par{b}"))
                dve.tensor_copy(par[:, 4 * b:4 * b + n, :].rearrange("p a b -> p (a b)"), ps[:, 5 + b, 0:P * n])\
                   .then_inc(prep_dve.sem, prep_dve.mark(f"par{b}"))
            for k in k8:
                dve.wait_ge(x_pe.sem, x_pe.value(f"x{k}"))
                dve.tensor_copy(h[:, k, :], bank(k % 4)).then_inc(x_ready, 1)
            dve.wait_ge(small_landed, 16 * 9)
            dve.tensor_copy(wsh[:], ws[:]).then_inc(prep_dve.sem, prep_dve.mark("wsh"))
            dve.wait_ge(prep_dve.sem, prep_dve.value("wsh"))
            dve.tensor_tensor(wsl[:], ws[:], wsh[:].bitcast(F32), ALU.subtract).then_inc(prep_dve.sem, prep_dve.mark("wsl"))
            dve.tensor_scalar(sgn_bias[:], raw_bias[:], sgn[:], None, ALU.mult).then_inc(prep_dve.sem, prep_dve.mark("sgn_bias"))
            dve.wait_ge(prep_act.sem, prep_act.value("a_exp"))
            dve.tensor_scalar(row_scale[:], row_scale[:], -1.0, None, ALU.mult).then_inc(prep_dve.sem, prep_dve.mark("a_neg"))
            dve.wait_ge(prep_dve.sem, prep_dve.value("a_neg"))
            norm(0)
            normed(0, 0, "norm_mix", ul)
            scalars(0)
            conv4("xbc", "ssd_conv_w", 0, cv)
            scalars_by_token(0)

            def heads16(t):
                return t.unsqueeze(2).to_broadcast([P, SSD_HEADS, HD])

            def by_head(t):
                return t.rearrange("p (h d) -> p h d", d=HD)

            def own(name):
                dve.wait_ge(ssd_dve.sem, ssd_dve.value(name))

            def mark(name):
                return ssd_dve.sem, ssd_dve.mark(name)

            for g in range(SSD_GROUPS):
                dve.wait_ge(ssd_pe.sem, ssd_pe.value(f"cb{g}"))
                dve.tensor_tensor(cb[:, g, :].rearrange("p (c l) -> p c l", c=NT), ps[:, 4 + g, :].rearrange("p (c l) -> p c l", c=NT),
                                  upto[:].unsqueeze(1).to_broadcast([P, NT, P]), ALU.mult).then_inc(*mark(f"cb{g}"))
            dve.wait_ge(sc_act.sem, sc_act.value("chunk", 0))
            for c in ch:
                dve.wait_ge(ssd_pe.sem, ssd_pe.value(f"x{c}"))
                dve.tensor_tensor(by_head(xd[:, c, :]), by_head(ps[:, 4:6, :].rearrange("p a b -> p (a b)")),
                                  heads16(tok[:, 1, c, 32:48]), ALU.mult).then_inc(*mark(f"xd{c}"))
                if c == 3:
                    break
                dve.wait_ge(ssd_pe.sem, ssd_pe.value(f"b{c}"))
                if c:
                    dve.wait_ge(ssd_pe.sem, ssd_pe.value(f"state{c - 1}_1"))
                dve.tensor_copy(bt[:], ps[:, 6, 0:2 * P]).then_inc(*mark(f"b{c}"))
                own(f"xd{c}")
                dve.tensor_tensor(by_head(xdd[:]), by_head(xd[:, c, :]), heads16(decay_end[:, c, 32:48]), ALU.mult)\
                   .then_inc(*mark(f"xdd{c}"))
                if c:
                    dve.tensor_tensor(by_head(stq[:]), by_head(st[:, c - 1, :]), heads16(chunk_decay[:, c, 32:48]), ALU.mult)\
                       .then_inc(*mark(f"dec{c}"))
                    own(f"dec{c}")
                dve.wait_ge(ssd_pe.sem, ssd_pe.value(f"state{c}_1"))
                src = ps[:, 6:8, :].rearrange("p a b -> p (a b)")
                if c:
                    dve.tensor_tensor(st[:, c, :], src, stq[:], ALU.add).then_inc(*mark(f"st{c}"))
                else:
                    dve.tensor_copy(st[:, 0, :], src).then_inc(*mark("st0"))
            own("xd3")
            for grp in range(SSD_GROUPS):
                with dve.Fori(0, 4) as i:
                    turn = i + 4 * grp
                    for e in range(2):
                        dve.tensor_scalar(oh[:, e, :], cs[:], ident[0:48, bass.ds(2 * i + (32 + 8 * grp + e), 1)], None, ALU.mult)\
                           .then_inc(sh_dve.sem, sh_dve.mark(f"oh{e}"))
                    for e in range(2):
                        dve.wait_ge(sh_pe.sem, sh_pe.value(f"row{e}", turn))
                        for c in ch:
                            last = dve.tensor_scalar(dd[:, e, c * P:(c + 1) * P], ps[:, 4 + e, c * P:(c + 1) * P],
                                                     tok[:, 0, c, bass.ds(2 * i + (32 + 8 * grp + e), 1)], 0.0,
                                                     ALU.subtract, ALU.min)
                        last.then_inc(sh_dve.sem, sh_dve.mark(f"d{e}"))
                    for e in range(2):
                        dve.wait_ge(sh_act.sem, sh_act.value(f"e{e}", turn))
                        dve.wait_ge(sh_pe.sem, sh_pe.value(f"y{e}", turn - 1))
                        dve.tensor_tensor(mt[:, e, :], dd[:, e, :], cb[:, grp, :], ALU.mult)\
                           .then_inc(sh_dve.sem, sh_dve.mark(f"m{e}"))
                        dve.wait_ge(sh_act.sem, sh_act.value(f"r{e}", turn))
                        dve.tensor_tensor(ce[:, e, :], xc[:, 10 + grp, :], ec[:, e, :], ALU.mult)\
                           .then_inc(sh_dve.sem, sh_dve.mark(f"c{e}"))
            for k in k8:
                dve.wait_ge(sy_pe.sem, sy_pe.value(f"t{k}"))
                dve.scalar_tensor_tensor(out=yf[:, k % 2, :], in0=xc[:, k, :], scalar=d_skip[:, k:k + 1], in1=bank(4 + k % 2),
                                         op0=ALU.mult, op1=ALU.add).then_inc(sy_dve.sem, sy_dve.mark(f"w{k}"))
                dve.wait_ge(sy_dve.sem, sy_dve.value(f"w{k}"))
                if k == 0:
                    for p in range(2):
                        dve.wait_ge(lin_free[p], std_value("z", p, 1))
                dve.tensor_tensor(zs[:, k, :], yf[:, k % 2, :], zs[:, k, :], ALU.mult).then_inc(sy_dve.sem, sy_dve.mark(f"g{k}"))
            for g in range(2):
                dve.wait_ge(sy_pe.sem, sy_pe.value(f"sum{4 * g + 3}"))
                dve.tensor_scalar(yms[:, g, :], bank(6 + g), 1.0 / 512, EPS, ALU.mult, ALU.add).then_inc(sy_dve.sem, sy_dve.mark(f"ms{g}"))
                dve.wait_ge(sy_dve.sem, sy_dve.value(f"ms{g}"))
                dve.reciprocal(yrs[:, g, :], yms[:, g, :]).then_inc(sy_dve.sem, sy_dve.mark(f"rc{g}"))

            def y_normed(k):
                dve.wait_ge(sy_act.sem, sy_act.value(f"rs{k // 4}"))
                if k >= 2:
                    dve.wait_ge(sy_act.sem, sy_act.value(f"h{k - 2}"))
                    dve.wait_ge(sy_dve.sem, sy_dve.value(f"l{k - 2}"))
                dve.scalar_tensor_tensor(out=yf[:, k % 2, :], in0=zs[:, k, :], scalar=column("ssd_norm", k), in1=yms[:, k // 4, :],
                                         op0=ALU.mult, op1=ALU.mult).then_inc(sy_dve.sem, sy_dve.mark(f"f{k}"))

            y_normed(0)
            for k in k8:
                if k < 7:
                    y_normed(k + 1)
                dve.wait_ge(sy_act.sem, sy_act.value(f"h{k}"))
                dve.tensor_tensor(ysl[:, k, :], yf[:, k % 2, :], ysh[:, k, :].bitcast(F32), ALU.subtract)\
                   .then_inc(sy_dve.sem, sy_dve.mark(f"l{k}"))

            def pmark(name):
                return po_dve.sem, po_dve.mark(name)

            def pown(name):
                dve.wait_ge(po_dve.sem, po_dve.value(name))

            dve.memset(pv[:, :, 0:PADV], 0.0).then_inc(*pmark("pad"))
            for g in range(4):
                dve.wait_ge(lin_free[g // 2], std_value("pool", g // 2, 0, 1))
                src, W = pv[:, g, :], PADV + S
                pown(f"e{g - 1}" if g else "pad")
                for n in range(g + 1):
                    dst, lag = win[:, n % 2, :], 1 << n
                    lo = 2 * lag - 1
                    if n:
                        pown(f"s{g}_{n - 1}")
                    dve.tensor_tensor(dst[:, lo:W], src[:, lo:W], src[:, lo - lag:W - lag], ALU.add).then_inc(*pmark(f"s{g}_{n}"))
                    src = dst
                pown(f"s{g}_{g}")
                w = WINDOWS[g]
                dve.scalar_tensor_tensor(out=dp[:, g, :], in0=src[:, PADV:W], scalar=1.0 / w, in1=pv[:, g, PADV:W],
                                         op0=ALU.mult, op1=ALU.subtract).then_inc(*pmark(f"d{g}"))
                pown(f"d{g}")
                dve.tensor_tensor(src[:, PADV:PADV + w - 1], src[:, PADV:PADV + w - 1], inv_count[:, 0:w - 1], ALU.mult)\
                   .then_inc(*pmark(f"q{g}"))
                pown(f"q{g}")
                dve.tensor_tensor(dp[:, g, 0:w - 1], src[:, PADV:PADV + w - 1], pv[:, g, PADV:PADV + w - 1], ALU.subtract)\
                   .then_inc(*pmark(f"e{g}"))
            for g in range(4):
                dve.wait_ge(po_act.sem, g + 1)
                dve.scalar_tensor_tensor(out=ypl[:, g, :], in0=bank(4 + g), scalar=column("pool_scale", g),
                                         in1=yph[:, g, :].bitcast(F32), op0=ALU.mult, op1=ALU.subtract).then_inc(*pmark(f"l{g}"))
            pown("l3")
            with dve.Fori(0, 4) as i:
                for ev in AT_DVE:
                    e = int(ev[0])
                    if ev[1:] == "oh":
                        last = dve.tensor_scalar(ohc[:], cs[:], ident[0:48, bass.ds(2 * i + e, 1)], -1.0, ALU.mult, ALU.mult)
                    elif ev[1:] == "nb":
                        dve.wait_ge(at_pe.sem, at_pe.value(f"{e}bc", i))
                        last = dve.tensor_copy(nb[:, e, :], bank(0))
                    else:
                        kind, n = ev[1], int(ev[2])
                        u = 4 * e + n
                        L = P * (n + 1)
                        if kind == "s":
                            dve.wait_ge(at_pe.sem, at_pe.value(f"{e}s{n}", i))
                            dve.wait_ge(at_act.sem, step_back(at_act, "p", u, 2, i))
                            dve.wait_ge(at_dve.sem, at_dve.value(f"{e}nb", i))
                            last = dve.tensor_tensor(sm[:, u % 2, 0:L], ps[:, 2 + u % 4, 0:L], nb[:, e, 0:L], ALU.add)
                        elif kind == "x":
                            dve.wait_ge(at_dve.sem, at_dve.value(f"{e}s{n}", i))
                            last = dve.tensor_reduce(stat[:, u:u + 1], sm[:, u % 2, 0:L], AX_X, ALU.max)
                        elif kind == "m":
                            dve.wait_ge(at_dve.sem, at_dve.value(f"{e}x{n}", i))
                            last = dve.tensor_scalar(stat[:, 8 + u:9 + u], stat[:, u:u + 1], -1.0, None, ALU.mult)
                        elif kind == "r":
                            dve.wait_ge(at_act.sem, at_act.value(f"{e}p{n}", i))
                            last = dve.reciprocal(stat[:, 24 + u:25 + u], stat[:, 16 + u:17 + u])
                        else:
                            dve.wait_ge(at_dve.sem, at_dve.value(f"{e}r{n}", i))
                            dve.wait_ge(at_pe.sem, at_pe.value(f"{e}o{n}", i))
                            last = dve.tensor_scalar(oa[:, n, bass.ds(128 * i + 64 * e, HD)], ps[:, (7, 1)[u % 2], 64 * u:64 * u + 64],
                                                     stat[:, 24 + u:25 + u], None, ALU.mult)
                    last.then_inc(at_dve.sem, at_dve.mark(ev))
            for k in range(4):
                dve.wait_ge(ay_act.sem, ay_act.value(f"h{k}"))
                dve.tensor_tensor(yal[:, k, :], bank(4 + k), yah[:, k, :].bitcast(F32), ALU.subtract)\
                   .then_inc(ay_dve.sem, ay_dve.mark(f"l{k}"))
            for ph in ("proj_pool", "proj_attn"):
                with dve.Fori(0, 2) as i:
                    for p in range(2):
                        dve.wait_ge(pe_used, 4 * i + (4 * PLAN[ph].first + 2 * p + 6))
                        if p == 0 and i is not None:
                            gate = "gate0" if ph == "proj_pool" else "gate1"
                            for pp in range(2):
                                dve.wait_ge(lin_free[pp], std_value(gate, pp, 1))
                        for c in range(2):
                            t = bass.ds(4 * i + 2 * p + c, 1)
                            b = 2 * p + c
                            if ph == "proj_pool":
                                dve.tensor_tensor(mg[:, t, :], ps[:, b:b + 1, :], gt[:, t, :], ALU.mult).then_inc(lin_free[p], 1)
                                continue
                            if b >= 2:
                                dve.wait_ge(mg_dve.sem, mg_dve.value(f"m{b - 2}", i))
                            else:
                                dve.wait_ge(mg_dve.sem, mg_dve.value(f"m{b + 2}", i - 1))
                            dve.tensor_tensor(tmp[:, c:c + 1, :], ps[:, b:b + 1, :], gt[:, t, :], ALU.mult).then_inc(lin_free[p], 1)
                            dve.wait_ge(lin_free[p], 2 * i + (2 * PLAN[ph].fills[p] + 3 + c))
                            dve.tensor_tensor(mg[:, t, :], tmp[:, c:c + 1, :], mg[:, t, :], ALU.add)\
                               .then_inc(mg_dve.sem, mg_dve.mark(f"m{b}"))
            with dve.Fori(0, 2) as i:
                for g in range(2):
                    dve.wait_ge(pe_used, 8 * i + (4 * (PLAN["proj_ssd"].first + g) + 8))
                    if g == 0:
                        for pp in range(2):
                            dve.wait_ge(lin_free[pp], std_value("gate2", pp, 1))
                    for c in range(2):
                        t = bass.ds(4 * i + 2 * g + c, 1)
                        b = 2 * g + c
                        dve.wait_ge(mg_dve.sem, mg_dve.value(f"m{b - 2}", i + 2) if b >= 2 else mg_dve.value(f"m{b + 2}", i + 1))
                        dve.tensor_tensor(tmp[:, c:c + 1, :], ps[:, b:b + 1, :], gt[:, t, :], ALU.mult).then_inc(lin_free[g], 1)
                        dve.wait_ge(lin_free[g], std_value("proj_ssd", g, i, c))
                        dve.tensor_tensor(mg[:, t, :], tmp[:, c:c + 1, :], mg[:, t, :], ALU.add)\
                           .then_inc(mg_dve.sem, mg_dve.mark(f"m{b}"))
                    for c in range(2):
                        t = bass.ds(4 * i + 2 * g + c, 1)
                        dve.wait_ge(mg_act.sem, 4 * i + (2 * g + c + 1))
                        dve.wait_ge(mg_dve.sem, mg_dve.value(f"m{2 * g + c}", i + 2))
                        dve.tensor_tensor(ul[:, t, :], mg[:, t, :], uh[:, t, :].bitcast(F32), ALU.subtract).then_inc(mg_low.sem, 1)
            added("w_out")

            def ffn(f):
                up, w = f"up{f}", f"f{f}w"
                with dve.Fori(0, FT // 2) as i:
                    turn = i + (FT // 2) * f
                    own = lambda name, back=0: dve.wait_ge(ffn_dve.sem, ffn_dve.value(name, turn - back if back else turn))
                    for g in range(2):
                        for c in range(2):
                            b, t = 2 * g + c, 2 * i + (FT * g + c)
                            dve.wait_ge(ffn_act.sem, ffn_act.value(f"t{b}", turn))
                            dve.scalar_tensor_tensor(out=fc[:, b, 1:S], in0=ps[:, b, 0:S - 1], scalar=column(w, t + 2 * FT),
                                                     in1=fc[:, b, 1:S], op0=ALU.mult, op1=ALU.add)\
                               .then_inc(ffn_dve.sem, ffn_dve.mark(f"a{b}"))
                        for c in range(2):
                            b, t = 2 * g + c, 2 * i + (FT * g + c)
                            own(f"a{b}")
                            dve.scalar_tensor_tensor(out=fc[:, b, 2:S], in0=ps[:, b, 0:S - 2], scalar=column(w, t),
                                                     in1=fc[:, b, 2:S], op0=ALU.mult, op1=ALU.add).then_inc(lin_free[g], 1)
                    for c in range(2):
                        dve.wait_ge(ffn_act.sem, ffn_act.value(f"s{c}", turn))
                        dve.wait_ge(ffn_act.sem, ffn_act.value(f"fh{c}", turn - 1))
                        own(f"fl{c}", 1)
                        dve.wait_ge(lin_free[1], std_value(up, 1, i, c))
                        dve.tensor_tensor(ff[:, c, :], fg[:, c, :], fc[:, 2 + c, :], ALU.mult)\
                           .then_inc(ffn_dve.sem, ffn_dve.mark(f"hf{c}"))
                    for c in range(2):
                        t = bass.ds(2 * i + c, 1)
                        dve.wait_ge(ffn_act.sem, ffn_act.value(f"fh{c}", turn))
                        own(f"hf{c}")
                        dve.tensor_tensor(fl[:, t, :], ff[:, c:c + 1, :], fh[:, t, :].bitcast(F32), ALU.subtract)\
                           .then_inc(ffn_dve.sem, ffn_dve.mark(f"fl{c}"))
                ph = PLAN[f"down{f}"]
                for t in k8:
                    if t % 4 == 0:
                        dve.wait_ge(pe_used, 4 * (ph.first + ph.quads) + 2 + t // 2)
                    dve.tensor_tensor(h[:, t, :], bank((t + 4) % 8), h[:, t, :], ALU.add)\
                       .then_inc(h_low if t < 4 else lin_free[t // 2 - 2], 1)

            norm(1)
            normed(1, 1, "norm_ffn", ul)
            ffn(0)
            dve.memset(ws[:], 0.0).then_inc(prep_dve2.sem, prep_dve2.mark("zero"))
            norm(2)
            for k in k8:
                dve.wait_ge(norm_pe.sem, norm_pe.value("row", 2))
                h_wait(dve, 2, k)
                dve.scalar_tensor_tensor(out=h[:, k, :], in0=h[:, k, :], scalar=column("norm_final", k), in1=bank(7),
                                         op0=ALU.mult, op1=ALU.mult).then_inc(renormed, 1)

            dve.wait_ge(small_landed, 16 * 11)
            dve.tensor_copy(wsh[:], ws[:]).then_inc(prep_dve2.sem, prep_dve2.mark("wsh"))
            dve.wait_ge(prep_dve2.sem, prep_dve2.value("wsh"))
            dve.tensor_tensor(wsl[:], ws[:], wsh[:].bitcast(F32), ALU.subtract).then_inc(prep_dve2.sem, prep_dve2.mark("wsl"))
            norm(3)
            normed(3, 2, "a_norm", ul)
            scalars(1)
            conv4("a_qkv", "a_conv_w", 3, acv)
            scalars_by_token(1)

            def gmark(name):
                return gn_dve.sem, gn_dve.mark(name)

            def after(events, name, turn=0):
                dve.wait_ge(events.sem, events.value(name, turn))

            dve.memset(pick[:], 0.0).then_inc(*gmark("zeros"))
            after(gn_dve, "zeros")
            dve.memset(pick[:, 15:16], 1.0).then_inc(*gmark("pick"))
            dve.wait_ge(pe_used, 4 * PLAN["a_out"].first + 4)
            dve.tensor_copy(cs2[:], cs[:]).then_inc(*gmark("cs"))
            after(gn_pe, "n15")
            dve.tensor_scalar(qk_sums[:], ps[0:16, 4, :], EPS, None, ALU.add).then_inc(*gmark("ns"))
            after(gn_pe, "nt")
            dve.reciprocal(rn[:].rearrange("p a b -> p (a b)"), ps[:, 4, 0:64]).then_inc(*gmark("nr"))
            after(gn_act, "rt")
            dve.tensor_scalar(rn2[:, :, 0:8], rn2[:, :, 0:8], float(P) ** -0.5, None, ALU.mult).then_inc(*gmark("qs"))
            dve.tensor_tensor(bege[:], beta[:], egc[:], ALU.mult).then_inc(*gmark("bege"))
            after(gn_dve, "bege")

            def by_chunk(t):
                return t.rearrange("p (c d) -> p c d", c=NT)

            with dve.Fori(0, DN_HEADS // 2) as i:
                for step in GD:
                    for e in range(2):
                        B = [ps[:, 4 * e + b, :] for b in range(4)]
                        head = bass.ds(2 * i + e, 1)

                        def scaled(dst, src, factor):
                            return dve.tensor_tensor(by_chunk(dst), by_chunk(src), factor.to_broadcast([P, NT, P]), ALU.mult)

                        def own(name):
                            after(g_dve, f"{e}{name}", i)

                        if step == "goh":
                            last = dve.tensor_scalar(goh[:, e, :], cs2[:], ident[0:48, bass.ds(2 * i + (32 + e), 1)], None, ALU.mult)
                        elif step == "kn":
                            after(g_pe, f"{e}rk", i)
                            last = scaled(kn[e][:], B[0], rn2[:, :, bass.ds(2 * i + (8 + e), 1)])
                        elif step == "qn":
                            after(g_pe, f"{e}rq", i)
                            last = scaled(qn[e][:], B[2], rn2[:, :, head])
                        elif step == "kb":
                            own("kn")
                            last = scaled(kb[e][:], kn[e][:], beta[:, :, head])
                        elif step == "d":
                            after(g_act, f"{e}eg", i)
                            for c in ch:
                                last = dve.tensor_scalar(em[e][:, c * P:(c + 1) * P], B[3][:, c * P:(c + 1) * P],
                                                         tok[:, 0, c, bass.ds(2 * i + (32 + e), 1)], 0.0, ALU.subtract, ALU.min)
                        elif step == "kbe":
                            own("kn")
                            last = scaled(kbe[e][:], kn[e][:], bege[:, :, head])
                        elif step == "kd":
                            last = scaled(kd[e][:], kn[e][:], decay_end[:, :, bass.ds(2 * i + (32 + e), 1)])
                        elif step == "mask":
                            own("lt")
                            last = dve.tensor_tensor(by_chunk(em[e][:]), by_chunk(em[e][:]),
                                                     upto[:].unsqueeze(1).to_broadcast([P, NT, P]), ALU.mult)
                        elif step == "qd":
                            after(g_act, f"{e}qt", i)
                            last = dve.tensor_tensor(eg[e][:], qt[e][:], eg[e][:], ALU.mult)
                        elif step in ("lt", "an"):
                            if step == "lt":
                                after(g_pe, f"{e}prod", i)
                                after(g_act, f"{e}em", i)
                            else:
                                after(g_pe, f"{e}prq", i)
                                own("mask")
                            dst, b = (lt, 0) if step == "lt" else (an, 1)
                            last = dve.tensor_tensor(dst[e][:], B[b], em[e][:], ALU.mult)
                        elif step == "i0":
                            own("lt")
                            last = dve.tensor_tensor(by_chunk(tt[e][:]), by_chunk(lt[e][:]),
                                                     level[:, 0, :].unsqueeze(1).to_broadcast([P, NT, P]), ALU.mult)
                        elif step == "tt0":
                            own("i0")
                            last = dve.tensor_tensor(by_chunk(tt[e][:]), by_chunk(tt[e][:]),
                                                     ident[:].unsqueeze(1).to_broadcast([P, NT, P]), ALU.add)
                        elif step[:3] == "ltk":
                            k = int(step[3])
                            if k > 1:
                                after(g_pe, f"{e}x{k - 1}", i)
                            else:
                                own("lt")
                            last = dve.tensor_tensor(by_chunk(ltk[e][:]), by_chunk(lt[e][:]),
                                                     level[:, k, :].unsqueeze(1).to_broadcast([P, NT, P]), ALU.mult)
                        elif step[:2] == "xi":
                            after(g_pe, f"{e}x{step[2]}", i)
                            own("an")
                            last = dve.tensor_tensor(by_chunk(xi[e][:]), by_chunk(B[3]),
                                                     ident[:].unsqueeze(1).to_broadcast([P, NT, P]), ALU.add)
                        elif step[:2] == "tt":
                            after(g_pe, f"{e}tt{step[2]}", i)
                            last = dve.tensor_copy(halves(tt[e][:], int(step[2]), 1), halves(B[0], int(step[2]), 1))
                        elif step == "ot":
                            after(g_pe, f"{e}o3", i)
                            last = dve.tensor_copy(ot[:, :, bass.ds(256 * i + P * e, P)], by_chunk(B[1]))
                        else:
                            c = int(step[1])
                            after(g_pe, f"{e}s{c}", i)
                            src = B[2][:, c * P:(c + 1) * P]
                            if c == 0:
                                last = dve.tensor_copy(sg[e][:], src)
                            else:
                                last = dve.scalar_tensor_tensor(out=sg[e][:], in0=sg[e][:],
                                                                scalar=chunk_decay[:, c, bass.ds(2 * i + (32 + e), 1)],
                                                                in1=src, op0=ALU.mult, op1=ALU.add)
                        last.then_inc(g_dve.sem, g_dve.mark(f"{e}{step}"))
            for n in ch:
                after(gn_act, f"q{n}")
                dve.tensor_reduce(oss[:, n, :], osq[:, n % 2, :].rearrange("p (h d) -> p h d", d=P), AX_X, ALU.add)\
                   .then_inc(*gmark(f"red{n}"))
            after(gn_dve, "red3")
            dve.tensor_scalar(oss2[:], oss[:], 1.0 / P, EPS, ALU.mult, ALU.add).then_inc(*gmark("om"))
            after(gn_dve, "om")
            dve.reciprocal(oss[:], oss2[:]).then_inc(*gmark("orc"))
            after(gn_act, "or")
            for n in ch:
                v_ = ot[:, n, :].rearrange("p (h d) -> p h d", d=P)
                dve.tensor_tensor(v_, v_, oss2[:, n, :].unsqueeze(2).to_broadcast([P, 8, P]), ALU.mult).then_inc(*gmark(f"sc{n}"))

            def gated(k):
                after(gn_pe, f"t{k}")
                if k >= 2:
                    after(gn_dve, f"l{k - 2}")
                dve.scalar_tensor_tensor(out=ayf[:, k % 2, :], in0=bank(k), scalar=column("onorm", 0), in1=ga[:, k, :],
                                         op0=ALU.mult, op1=ALU.mult).then_inc(*gmark(f"f{k}"))

            gated(0)
            for k in k8:
                if k < 7:
                    gated(k + 1)
                after(gn_act, f"h{k}")
                dve.tensor_tensor(ayl[:, k, :], ayf[:, k % 2, :], ayh[:, k, :].bitcast(F32), ALU.subtract).then_inc(*gmark(f"l{k}"))
            added("a_out")
            norm(4)
            normed(4, 3, "f_norm0", ul)
            ffn(1)

            norm(5)
            normed(5, 4, "kv_norm", ul)
            dve.wait_ge(u_dve.sem, u_dve.value("ul7", 4))
            normed(5, 5, "b_norm", ubl)
            dve.memset(sm2[:, :, 0, 0:P], MASKED).then_inc(kv_dve.sem, kv_dve.mark("far"))
            dve.wait_ge(pe_used, 4 * PLAN["kv_k"].first + 8)
            for c in range(2):
                dve.tensor_scalar(kraw[:, c, :], bank(c), column("kv_b", c), None, ALU.add).then_inc(lin_free[0], 1)
            dve.wait_ge(pe_used, 4 * PLAN["kv_v"].first + 8)
            dve.wait_ge(vbias_landed, 16)
            dve.tensor_tensor(vv[:], ps[:, 2:4, :].rearrange("p a (b c) -> p (a b) c", b=2),
                              vbias[:].unsqueeze(1).to_broadcast([P, NT, 256]), ALU.add).then_inc(lin_free[1], 2)
            dve.wait_ge(lin_free[0], std_value("kv_k", 0, 0))
            for j in range(KV_HEADS):
                for half_ in range(2):
                    dve.tensor_copy(kk[HD * half_:HD * half_ + HD, j, :], kraw[HD * (j % 2):HD * (j % 2) + HD, j // 2, :])\
                       .then_inc(kv_dve.sem, kv_dve.mark(f"k{2 * j + half_}"))
            with dve.Fori(0, 2) as i:
                for g in range(2):
                    dve.wait_ge(pe_used, 8 * i + (4 * (PLAN["q2"].first + g) + 8))
                    for c in range(2):
                        dve.tensor_scalar(q2[:, bass.ds(4 * i + 2 * g + c, 1), :], ps[:, 2 * g + c:2 * g + c + 1, :],
                                          column("b_q", 4 * i + 2 * g + c), HD ** -0.5, ALU.add, ALU.mult).then_inc(lin_free[g], 1)
            dve.wait_ge(sinks_landed, 16)
            dve.wait_ge(later_ready, 1)
            dve.wait_ge(kv_dve.sem, kv_dve.value("far"))
            def back(events, name, u, lag, turn):
                return events.value(f"{name}{u - lag}", turn) if u >= lag else events.value(f"{name}{u - lag + NH}", turn - 1)

            with dve.Fori(0, SWA_HEADS // NH) as i:
                for step in BD:
                    u, kind = int(step[-1]), step[:-1]
                    own = lambda name: after(b_dve, f"{name}{u}", i)
                    head = bass.ds(NH * i + u, 1)
                    s_ = 8 * (u % 4)
                    peak = st2[:, 48 + 4 * (u % 2):52 + 4 * (u % 2)]
                    if kind == "ab":
                        dve.wait_ge(b_dve.sem, back(b_dve, "sb", u, 2, i))
                        last = dve.scalar_tensor_tensor(out=ab[:, u % 2, :], in0=dist[:], scalar=minus_slope[:, head],
                                                        in1=far[:], op0=ALU.mult, op1=ALU.add)
                    elif kind == "sa":
                        after(b_pe, f"s{u}", i)
                        own("ab")
                        dve.wait_ge(b_act.sem, back(b_act, "p", u, 2, i))
                        last = dve.tensor_tensor(sm2[:, u % 2, 0, P:], ps[:, 2 * (u % 2), P:2 * P], ab[:, u % 2, P:], ALU.add)
                    elif kind == "sb":
                        last = dve.tensor_tensor(sm2[:, u % 2, 1:, :], ps[:, 2 * (u % 2):2 * (u % 2) + 2, :]
                                                 .rearrange("p a (b c) -> p (a b) c", b=2)[:, 1:, :],
                                                 ab[:, u % 2, :].unsqueeze(1).to_broadcast([P, 3, 256]), ALU.add)
                    elif kind == "mx":
                        own("sb")
                        last = dve.tensor_reduce(peak, sm2[:, u % 2, :, :], AX_X, ALU.max)
                    elif kind == "ng":
                        own("mx")
                        last = dve.tensor_scalar(st2[:, s_:s_ + 4], peak, sinks[:, head], -1.0, ALU.max, ALU.mult)
                    elif kind == "den":
                        after(b_act, f"p{u}", i)
                        last = dve.tensor_tensor(st2[:, 56:60], st2[:, s_ + 4:s_ + 8], st2[:, 32 + 4 * (u % 4):36 + 4 * (u % 4)], ALU.add)
                    elif kind == "rec":
                        own("den")
                        last = dve.reciprocal(st2[:, 60:64], st2[:, 56:60])
                    else:
                        after(b_pe, f"o{u}", i)
                        own("rec")
                        last = dve.tensor_tensor(o_tok[:, :, bass.ds(NH * HD * i + HD * u, HD)],
                                                 ps[:, 6 + u % 2, 0:256].rearrange("p (n d) -> p n d", n=NT),
                                                 st2[:, 60:64].unsqueeze(2).to_broadcast([P, NT, HD]), ALU.mult)
                    last.then_inc(b_dve.sem, b_dve.mark(step))
            for k in k8:
                after(bo_act, f"h{k}")
                dve.tensor_tensor(ul[:, k, :], bank(4 + k % 4), uh[:, k, :].bitcast(F32), ALU.subtract)\
                   .then_inc(bo_dve.sem, bo_dve.mark(f"l{k}"))
            added("o2", "b_o")
            norm(6)
            normed(6, 6, "f_norm1", ul)
            ffn(2)
            norm(7)
            for k in k8:
                dve.wait_ge(norm_pe.sem, norm_pe.value("row", 7))
                h_wait(dve, 7, k)
                dve.scalar_tensor_tensor(out=out_t[:, k, :], in0=h[:, k, :], scalar=column("final_norm", k), in1=bank(7),
                                         op0=ALU.mult, op1=ALU.mult).then_inc(out_made, 1)

            for n in ch:
                dve.wait_ge(fin_pe.sem, fin_pe.value(f"t{n}"))
                dve.tensor_copy(x_in[:, n, :], ps[:, 4 + 2 * (n % 2):6 + 2 * (n % 2), :].rearrange("p a b -> p (a b)"))\
                   .then_inc(fin_dve.sem, fin_dve.mark(f"c{n}"))


_INS = ["x", "norm_mix", "w_in", "pool_mix", "pool_scale", "f_bias", "ssd_conv_w", "ssd_conv_b",
        "ssd_dt_bias", "ssd_a_log", "ssd_d", "ssd_norm", "p_pool", "p_attn", "p_ssd", "w_out",
        "norm_ffn", "ffn_up", "ffn_conv_w", "ffn_conv_b", "ffn_down", "norm_final",
        "a_norm_2", "a_w_in_2", "a_conv_w_2", "a_A_log_2", "a_dt_bias_2", "a_onorm_2", "a_w_out_2",
        "kv_norm_2", "kv_w_2", "kv_b_2", "b_norm_2", "b_w_q_2", "b_b_q_2", "b_sinks_2",
        "b_w_o_2", "b_b_o_2", "f_norm_2", "f_w_up_2", "f_conv_w_2", "f_conv_b_2", "f_w_down_2",
        "final_norm_2"]
_OUTS = [((1, S, D), "float32")]


def kernel(**inputs):
    import numpy as _np
    import concourse.bacc as _bacc
    from concourse import mybir as _mybir
    from concourse.bass_utils import run_bass_kernel_spmd as _run

    nc = _bacc.Bacc("TRN2", target_bir_lowering=False, num_devices=1)
    arrays, args = {}, []
    for name in _INS:
        a = _np.ascontiguousarray(inputs[name])
        arrays[f"in_{name}_dram"] = a
        args.append(nc.dram_tensor(f"in_{name}_dram", a.shape, _mybir.dt.from_np(a.dtype), kind="ExternalInput").ap())
    for i, (shape, dtype) in enumerate(_OUTS):
        dt = _mybir.dt.from_np(_np.dtype(dtype))
        args.append(nc.dram_tensor(f"out_{i}_dram", shape, dt, kind="ExternalOutput").ap())
    layered_mixers(nc, *args)
    r = _run(nc, [arrays], core_ids=[0])
    got = tuple(r.results[0][f"out_{i}_dram"] for i in range(len(_OUTS)))
    return got[0]
```
